# Optimizing a Trainium2 kernel written in Bass

```python
import jax
import jax.numpy as jnp
from jax import lax
import numpy as np

D_MODEL = 1024
BATCH = 1
SEQ = 512
DEPTH = 1
DEC_BATCH = 8
DEC_SEQ = 1
PAST_LEN = 1024
PAGE_SIZE = 128

MIX_WIDTH = D_MODEL
H_M = 4
MIX_M = MIX_WIDTH // 2
DH_M = MIX_M // H_M
H_A = 4
MIX_A = MIX_WIDTH - MIX_M
DH_A = MIX_A // H_A
H_IDX = 4
D_IDX = 64
TOPK_MAX = 256
N_MEM = 256
H_C = 4
DH_C = D_MODEL // H_C
D_FF = ((8 * D_MODEL // 3 + 127) // 128) * 128
CONV_W = 3
CHUNK = 128
Q_BLOCK = 128
ROPE_THETA = 10000.0
EPS = 1e-6
N_IN = 4 * MIX_M + 2 * H_M + 3 * MIX_A + H_IDX * D_IDX + D_IDX + H_IDX

kernel_name = 'hymba_mlstm_dsa_memxattn_convffn_step'

def rms_norm(x, g):
    xf = x.astype(jnp.float32)
    y = xf * lax.rsqrt(jnp.mean(xf * xf, axis=-1, keepdims=True) + EPS)
    return (y * g.astype(jnp.float32)).astype(x.dtype)

def rope(x, pos):
    half = x.shape[-1] // 2
    inv = ROPE_THETA ** (-jnp.arange(half, dtype=jnp.float32) / half)
    ang = pos.astype(jnp.float32)[:, None] * inv[None, :]
    cos = jnp.cos(ang)[:, None, :]
    sin = jnp.sin(ang)[:, None, :]
    xf = x.astype(jnp.float32)
    x1, x2 = xf[..., :half], xf[..., half:]
    return jnp.concatenate([x1 * cos - x2 * sin, x2 * cos + x1 * sin], axis=-1).astype(x.dtype)

def split_in(z):
    sizes = [MIX_M, MIX_M, MIX_M, MIX_M, H_M, H_M, MIX_A, MIX_A, MIX_A, H_IDX * D_IDX, D_IDX, H_IDX]
    offs = [int(o) for o in np.cumsum(sizes)[:-1]]
    return jnp.split(z, offs, axis=-1)

def mixer_inputs(h, pos, lp):
    B, T, _ = h.shape
    f32 = jnp.float32
    z = h @ lp['w_in']
    mq, mk, mv, mo, mi, mf, aq, ak, av, iq, ik, iw = split_in(z)
    gates = jnp.concatenate([mi, mf], axis=-1).astype(f32) + lp['b_if'].astype(f32)
    return dict(
        m_q=mq.reshape(B, T, H_M, DH_M).astype(f32),
        m_k=mk.reshape(B, T, H_M, DH_M).astype(f32) * (DH_M ** -0.5),
        m_v=mv.reshape(B, T, H_M, DH_M).astype(f32),
        m_o=mo,
        log_i=gates[..., :H_M],
        log_f=jax.nn.log_sigmoid(gates[..., H_M:]),
        a_q=rope(rms_norm(aq.reshape(B, T, H_A, DH_A), lp['q_norm']), pos),
        a_k=rope(rms_norm(ak.reshape(B, T, H_A, DH_A), lp['k_norm']), pos),
        a_v=av.reshape(B, T, H_A, DH_A),
        i_q=rope(iq.reshape(B, T, H_IDX, D_IDX), pos),
        i_k=rope(ik[:, :, None, :], pos)[:, :, 0, :],
        i_w=iw,
    )

def mlstm_chunk(carry, inp):
    C, n, m = carry
    q, k, v, li, lf = inp
    L = q.shape[2]
    b = jnp.cumsum(lf, axis=-1)
    causal = jnp.tril(jnp.ones((L, L), dtype=bool))
    logd = jnp.where(causal, b[..., :, None] - b[..., None, :] + li[..., None, :], -jnp.inf)
    inter = b + m[..., None]
    m_t = jnp.maximum(inter, jnp.max(logd, axis=-1))
    s = jnp.einsum('bhtd,bhsd->bhts', q, k) * jnp.exp(logd - m_t[..., None])
    g_inter = jnp.exp(inter - m_t)
    num = g_inter[..., None] * jnp.einsum('bhed,bhtd->bhte', C, q) + jnp.einsum('bhts,bhse->bhte', s, v)
    den = g_inter * jnp.einsum('bhd,bhtd->bht', n, q) + jnp.sum(s, axis=-1)
    h = num / jnp.maximum(jnp.abs(den), jnp.exp(-m_t))[..., None]
    m_new = m_t[..., -1]
    g_prev = jnp.exp(b[..., -1] + m - m_new)
    w_s = jnp.exp(b[..., -1:] - b + li - m_new[..., None])
    C_new = g_prev[..., None, None] * C + jnp.einsum('bhs,bhse,bhsd->bhed', w_s, v, k)
    n_new = g_prev[..., None] * n + jnp.einsum('bhs,bhsd->bhd', w_s, k)
    return (C_new, n_new, m_new), h

def mlstm_prompt(q, k, v, li, lf):
    B, S, H, D = q.shape
    L = min(CHUNK, S)
    nc = S // L
    to_c = lambda t: t.reshape(B, nc, L, H, D).transpose(1, 0, 3, 2, 4)
    to_g = lambda g: g.reshape(B, nc, L, H).transpose(1, 0, 3, 2)
    f32 = jnp.float32
    carry0 = (jnp.zeros((B, H, D, D), f32), jnp.zeros((B, H, D), f32), jnp.zeros((B, H), f32))
    carry, hs = lax.scan(mlstm_chunk, carry0, (to_c(q), to_c(k), to_c(v), to_g(li), to_g(lf)))
    return hs.transpose(1, 0, 3, 2, 4).reshape(B, S, H, D), carry

def mlstm_sample(q, k, v, li, lf, C, n, m):
    f32 = jnp.float32
    carry = (C.astype(f32), n.astype(f32), m.astype(f32))
    tr = lambda t: t.transpose(0, 2, 1, 3)
    carry, h = mlstm_chunk(carry, (tr(q), tr(k), tr(v), li.transpose(0, 2, 1), lf.transpose(0, 2, 1)))
    return tr(h), carry

def mlstm_out(h, o, lp):
    B, T = h.shape[:2]
    hn = rms_norm(h, lp['mlstm_norm'].reshape(H_M, DH_M)).reshape(B, T, MIX_M)
    return (jax.nn.sigmoid(o.astype(jnp.float32)) * hn).astype(o.dtype)

def indexer_topk(iq, iw, ik, q_pos, topk):
    s = jnp.einsum('bqhd,bld->bqhl', iq.astype(jnp.float32), ik.astype(jnp.float32))
    score = jnp.einsum('bqh,bqhl->bql', iw.astype(jnp.float32), jax.nn.relu(s))
    key_pos = jnp.arange(ik.shape[1])
    score = jnp.where(key_pos[None, None, :] <= q_pos[None, :, None], score, -jnp.inf)
    _, sel = lax.top_k(score, topk)
    return sel

def sparse_attend(q, k_sel, v_sel, sel, q_pos):
    s = jnp.einsum('bqhd,bqkhd->bqhk', q, k_sel).astype(jnp.float32) * (DH_A ** -0.5)
    valid = sel <= q_pos[None, :, None]
    s = jnp.where(valid[:, :, None, :], s, -jnp.inf)
    p = jax.nn.softmax(s, axis=-1).astype(v_sel.dtype)
    return jnp.einsum('bqhk,bqkhd->bqhd', p, v_sel)

def gather_rows(t, idx):
    return jax.vmap(lambda tb, ib: tb[ib])(t, idx)

def dsa_prompt(q, k, v, iq, iw, ik):
    B, S, H, D = q.shape
    topk = min(TOPK_MAX, S // 4)
    nb = S // Q_BLOCK

    def block(i):
        start = i * Q_BLOCK
        qb = lax.dynamic_slice_in_dim(q, start, Q_BLOCK, axis=1)
        iqb = lax.dynamic_slice_in_dim(iq, start, Q_BLOCK, axis=1)
        iwb = lax.dynamic_slice_in_dim(iw, start, Q_BLOCK, axis=1)
        q_pos = start + jnp.arange(Q_BLOCK)
        sel = indexer_topk(iqb, iwb, ik, q_pos, topk)
        return sparse_attend(qb, gather_rows(k, sel), gather_rows(v, sel), sel, q_pos)

    out = lax.map(block, jnp.arange(nb))
    return out.transpose(1, 0, 2, 3, 4).reshape(B, S, H, D)

def dsa_sample(q, k_new, v_new, iq, iw, ik_new, pool_k, pool_v, pool_ik, page_table):
    Bd, T = q.shape[:2]
    past = page_table.shape[1] * PAGE_SIZE
    topk = min(TOPK_MAX, (past + T) // 4)
    ik_past = pool_ik[page_table].reshape(Bd, past, D_IDX)
    ik_all = jnp.concatenate([ik_past, ik_new.astype(ik_past.dtype)], axis=1)
    q_pos = past + jnp.arange(T)
    sel = indexer_topk(iq, iw, ik_all, q_pos, topk)
    in_past = sel < past
    sp = jnp.minimum(sel, past - 1)
    phys_page = jax.vmap(lambda pt, s: pt[s])(page_table, sp // PAGE_SIZE)
    row = phys_page * PAGE_SIZE + sp % PAGE_SIZE
    k_flat = pool_k.reshape(-1, H_A, DH_A)
    v_flat = pool_v.reshape(-1, H_A, DH_A)
    jn = jnp.clip(sel - past, 0, T - 1)
    mask = in_past[..., None, None]
    k_sel = jnp.where(mask, k_flat[row], gather_rows(k_new, jn).astype(k_flat.dtype))
    v_sel = jnp.where(mask, v_flat[row], gather_rows(v_new, jn).astype(v_flat.dtype))
    return sparse_attend(q.astype(k_sel.dtype), k_sel, v_sel, sel, q_pos)

def memory_kv(mem, lp):
    B, M, _ = mem.shape
    hm = rms_norm(mem, lp['norm_mem'])
    k = rms_norm((hm @ lp['w_ck']).reshape(B, M, H_C, DH_C), lp['ck_norm'])
    v = (hm @ lp['w_cv']).reshape(B, M, H_C, DH_C)
    return k, v

def finish_layer(x, y_m, y_a, mem_k, mem_v, conv_hist, lp):
    B, T, _ = x.shape
    x = x + jnp.concatenate([y_m, y_a.astype(y_m.dtype)], axis=-1) @ lp['w_out']
    h = rms_norm(x, lp['norm_cross'])
    q = rms_norm((h @ lp['w_cq']).reshape(B, T, H_C, DH_C), lp['cq_norm'])
    s = jnp.einsum('bthd,bmhd->bhtm', q, mem_k.astype(q.dtype)).astype(jnp.float32) * (DH_C ** -0.5)
    p = jax.nn.softmax(s, axis=-1).astype(x.dtype)
    o = jnp.einsum('bhtm,bmhd->bthd', p, mem_v.astype(x.dtype)).reshape(B, T, D_MODEL)
    x = x + o @ lp['w_co']
    h = rms_norm(x, lp['norm_ffn'])
    u = h @ lp['w_up']
    u_ext = jnp.concatenate([conv_hist.astype(u.dtype), u], axis=1)
    c = lp['conv_b'] + u_ext[:, 0:T] * lp['conv_w'][0]
    for j in range(1, CONV_W):
        c = c + u_ext[:, j:j + T] * lp['conv_w'][j]
    a, g = jnp.split(c, 2, axis=-1)
    x = x + (jax.nn.gelu(g) * a) @ lp['w_down']
    return x, u_ext[:, -(CONV_W - 1):]

def setup_inputs(seed: int = 0) -> dict:
    key = jax.random.key(seed)
    keys = iter(jax.random.split(key, 48))
    f32 = jnp.float32
    n_pages = PAST_LEN // PAGE_SIZE
    n_pool = (DEC_BATCH * n_pages * 5) // 4

    def normal(shape, scale=1.0):
        return jax.random.normal(next(keys), shape, f32) * scale

    def gain(shape):
        return 1.0 + normal(shape, 0.02)

    x_prompt = normal((BATCH, SEQ, D_MODEL))
    x_sample = normal((DEC_BATCH, DEC_SEQ, D_MODEL))
    mem_prompt = normal((BATCH, N_MEM, D_MODEL))
    cache_k = normal((DEPTH, n_pool, PAGE_SIZE, H_A, DH_A))
    cache_v = normal((DEPTH, n_pool, PAGE_SIZE, H_A, DH_A))
    cache_idx_k = normal((DEPTH, n_pool, PAGE_SIZE, D_IDX))
    cache_mem_k = normal((DEPTH, DEC_BATCH, N_MEM, H_C, DH_C))
    cache_mem_v = normal((DEPTH, DEC_BATCH, N_MEM, H_C, DH_C))
    state_mlstm_c = normal((DEPTH, DEC_BATCH, H_M, DH_M, DH_M), DH_M ** -0.5)
    state_mlstm_n = normal((DEPTH, DEC_BATCH, H_M, DH_M), DH_M ** -0.5)
    state_mlstm_m = normal((DEPTH, DEC_BATCH, H_M))
    state_conv = normal((DEPTH, DEC_BATCH, CONV_W - 1, 2 * D_FF))
    perm = jax.random.permutation(next(keys), n_pool)[: DEC_BATCH * n_pages]
    page_table = perm.reshape(DEC_BATCH, n_pages).astype(jnp.int32)
    b_if = jnp.concatenate([normal((DEPTH, H_M), 0.1),
                            jnp.linspace(3.0, 6.0, H_M, dtype=f32)[None, :] + normal((DEPTH, H_M), 0.1)], axis=-1)
    return {
        'x_prompt': x_prompt, 'x_sample': x_sample, 'mem_prompt': mem_prompt,
        'cache_k': cache_k, 'cache_v': cache_v, 'cache_idx_k': cache_idx_k,
        'cache_mem_k': cache_mem_k, 'cache_mem_v': cache_mem_v,
        'state_mlstm_c': state_mlstm_c, 'state_mlstm_n': state_mlstm_n, 'state_mlstm_m': state_mlstm_m,
        'state_conv': state_conv, 'page_table': page_table,
        'norm_mix': gain((DEPTH, D_MODEL)),
        'w_in': normal((DEPTH, D_MODEL, N_IN), D_MODEL ** -0.5),
        'b_if': b_if,
        'mlstm_norm': gain((DEPTH, MIX_M)),
        'q_norm': gain((DEPTH, DH_A)),
        'k_norm': gain((DEPTH, DH_A)),
        'w_out': normal((DEPTH, MIX_WIDTH, D_MODEL), MIX_WIDTH ** -0.5),
        'norm_cross': gain((DEPTH, D_MODEL)),
        'norm_mem': gain((DEPTH, D_MODEL)),
        'w_cq': normal((DEPTH, D_MODEL, D_MODEL), D_MODEL ** -0.5),
        'w_ck': normal((DEPTH, D_MODEL, D_MODEL), D_MODEL ** -0.5),
        'w_cv': normal((DEPTH, D_MODEL, D_MODEL), D_MODEL ** -0.5),
        'w_co': normal((DEPTH, D_MODEL, D_MODEL), D_MODEL ** -0.5),
        'cq_norm': gain((DEPTH, DH_C)),
        'ck_norm': gain((DEPTH, DH_C)),
        'norm_ffn': gain((DEPTH, D_MODEL)),
        'w_up': normal((DEPTH, D_MODEL, 2 * D_FF), D_MODEL ** -0.5),
        'conv_w': normal((DEPTH, CONV_W, 2 * D_FF), 0.5),
        'conv_b': normal((DEPTH, 2 * D_FF), 0.02),
        'w_down': normal((DEPTH, D_FF, D_MODEL), D_FF ** -0.5),
    }

def reference(x_prompt, x_sample, mem_prompt, cache_k, cache_v, cache_idx_k, cache_mem_k, cache_mem_v,
              state_mlstm_c, state_mlstm_n, state_mlstm_m, state_conv, page_table,
              norm_mix, w_in, b_if, mlstm_norm, q_norm, k_norm, w_out, norm_cross, norm_mem,
              w_cq, w_ck, w_cv, w_co, cq_norm, ck_norm, norm_ffn, w_up, conv_w, conv_b, w_down):
    B, S, _ = x_prompt.shape
    Bd, T, _ = x_sample.shape
    past = page_table.shape[1] * PAGE_SIZE
    pos_p = jnp.arange(S)
    pos_s = past + jnp.arange(T)
    names = ('p_k', 'p_v', 'p_ik', 'p_c', 'p_n', 'p_m', 'p_mk', 'p_mv', 'p_conv',
             's_k', 's_v', 's_ik', 's_c', 's_n', 's_m', 's_conv')
    new = {nm: [] for nm in names}
    xp, xs = x_prompt, x_sample
    for l in range(DEPTH):
        lp = {'norm_mix': norm_mix[l], 'w_in': w_in[l], 'b_if': b_if[l], 'mlstm_norm': mlstm_norm[l],
              'q_norm': q_norm[l], 'k_norm': k_norm[l], 'w_out': w_out[l], 'norm_cross': norm_cross[l],
              'norm_mem': norm_mem[l], 'w_cq': w_cq[l], 'w_ck': w_ck[l], 'w_cv': w_cv[l], 'w_co': w_co[l],
              'cq_norm': cq_norm[l], 'ck_norm': ck_norm[l], 'norm_ffn': norm_ffn[l], 'w_up': w_up[l],
              'conv_w': conv_w[l], 'conv_b': conv_b[l], 'w_down': w_down[l]}
        mi = mixer_inputs(rms_norm(xp, lp['norm_mix']), pos_p, lp)
        h_m, (c_p, n_p, m_p) = mlstm_prompt(mi['m_q'], mi['m_k'], mi['m_v'], mi['log_i'], mi['log_f'])
        y_m = mlstm_out(h_m, mi['m_o'], lp)
        y_a = dsa_prompt(mi['a_q'], mi['a_k'], mi['a_v'], mi['i_q'], mi['i_w'], mi['i_k']).reshape(B, S, MIX_A)
        mk_p, mv_p = memory_kv(mem_prompt, lp)
        xp, conv_p = finish_layer(xp, y_m, y_a, mk_p, mv_p,
                                  jnp.zeros((B, CONV_W - 1, 2 * D_FF), xp.dtype), lp)
        new['p_k'].append(mi['a_k'])
        new['p_v'].append(mi['a_v'])
        new['p_ik'].append(mi['i_k'])
        new['p_c'].append(c_p)
        new['p_n'].append(n_p)
        new['p_m'].append(m_p)
        new['p_mk'].append(mk_p)
        new['p_mv'].append(mv_p)
        new['p_conv'].append(conv_p)
        ms = mixer_inputs(rms_norm(xs, lp['norm_mix']), pos_s, lp)
        h_s, (c_s, n_s, m_s) = mlstm_sample(ms['m_q'], ms['m_k'], ms['m_v'], ms['log_i'], ms['log_f'],
                                            state_mlstm_c[l], state_mlstm_n[l], state_mlstm_m[l])
        y_ms = mlstm_out(h_s, ms['m_o'], lp)
        y_as = dsa_sample(ms['a_q'], ms['a_k'], ms['a_v'], ms['i_q'], ms['i_w'], ms['i_k'],
                          cache_k[l], cache_v[l], cache_idx_k[l], page_table).reshape(Bd, T, MIX_A)
        xs, conv_s = finish_layer(xs, y_ms, y_as, cache_mem_k[l], cache_mem_v[l], state_conv[l], lp)
        new['s_k'].append(ms['a_k'])
        new['s_v'].append(ms['a_v'])
        new['s_ik'].append(ms['i_k'])
        new['s_c'].append(c_s)
        new['s_n'].append(n_s)
        new['s_m'].append(m_s)
        new['s_conv'].append(conv_s)
    st = {nm: jnp.stack(v) for nm, v in new.items()}
    return (xp, xs, st['p_k'], st['p_v'], st['p_ik'], st['p_c'], st['p_n'], st['p_m'], st['p_mk'], st['p_mv'],
            st['p_conv'], st['s_k'], st['s_v'], st['s_ik'], st['s_c'], st['s_n'], st['s_m'], st['s_conv'])


_drawn_inputs = setup_inputs


def setup_inputs(seed=0):
    import zlib

    import numpy as np

    out = dict(_drawn_inputs(seed))
    spreads = {}
    factors = {'mlstm_norm': 7.738,
     'q_norm': 8.0,
     'k_norm': 2.825,
     'norm_cross': 8.0,
     'norm_mem': 2.826,
     'cq_norm': 8.0,
     'ck_norm': 2.763,
     'norm_ffn': 8.152,
     'conv_b': 4.247}
    for name, (base, spread) in spreads.items():
        noise = np.random.default_rng([zlib.crc32(name.encode()), seed]).standard_normal(out[name].shape)
        drawn = base * np.exp(spread * noise) if base else spread * noise
        out[name] = jnp.asarray(drawn.astype(out[name].dtype))
    for name, factor in factors.items():
        out[name] = (out[name] * factor).astype(out[name].dtype)
    return out
```

```python
import numpy as np
from contextlib import ExitStack

import concourse.bass as bass
from concourse import mybir

F32 = mybir.dt.float32
F32R = mybir.dt.float32r
I32 = mybir.dt.int32
U32 = mybir.dt.uint32
ALU = mybir.AluOpType
ACT = mybir.ActivationFunctionType
AX = mybir.AxisListType.X

P = 128
D = 1024
KT = D // P
SEQ = 512
NTT = SEQ // P
B = 8
T = SEQ + B
HALF = T // 2
H = 4
DH = 128
MIX = H * DH
D_IDX = 64
N_MISC = H * D_IDX + D_IDX + H + 2 * H
DFF = 2816
NFT = DFF // P
PAGE = 128
NPG = 8
PAST = NPG * PAGE
TOPK_P = 128
TOPK_S = 256
NMEM = 256
EPS = 1e-6
NEG = -1e30
TAKEN = -3e38
SCALE = DH ** -0.5
SCALE_C = 256 ** -0.5
C_MQ, C_MK, C_MV, C_MO, C_G = 0, MIX, 2 * MIX, 3 * MIX, 4 * MIX
C_AQ = C_G + 2 * H
C_AK, C_AV = C_AQ + MIX, C_AQ + 2 * MIX
C_IQ = C_AQ + 3 * MIX
IN_TILES = ([("iq0", C_IQ), ("iq1", C_IQ + P), ("ikw", C_IQ + 2 * P)]
            + [(f"{g}{h}", c + h * DH) for g, c in (("aq", C_AQ), ("ak", C_AK), ("av", C_AV), ("mq", C_MQ),
                                                     ("mk", C_MK), ("mv", C_MV), ("mo", C_MO)) for h in range(H)])
TI = {name: n for n, (name, _) in enumerate(IN_TILES)}


def rope_tables():
    pos = np.concatenate([np.arange(SEQ), np.full(B, PAST)]).astype(np.float32)
    out = []
    for half in (DH // 2, D_IDX // 2):
        inv = (np.float32(10000.0) ** (-np.arange(half, dtype=np.float32) / np.float32(half))).astype(np.float32)
        ang = pos[:, None] * inv[None, :]
        out.append(np.stack([np.cos(ang), np.sin(ang)], axis=1).astype(np.float32))
    return out


def build(nc, A, O, last_stage=99):
    with ExitStack() as ctx:
        sems = {}

        def sem(name):
            sems[name] = ctx.enter_context(nc.semaphore(name))
            return sems[name]

        cursor = [(nc.sbuf_base + 63) // 64 * 64]

        def sb(name, shape, dt=F32):
            n = int(np.prod(shape[1:])) * 4
            t = nc.alloc_sbuf_tensor_at(name, shape, dt, offset=cursor[0])
            cursor[0] += (n + 31) // 32 * 32
            return t

        raw = sb("raw", [P, 2, KT, P])
        whi = sb("whi", [P, 2, KT, P], F32R)
        wlo = sb("wlo", [P, 2, KT, P], F32R)
        ahi_at = cursor[0]
        ahi = sb("ahi", [P, KT, T], F32R)
        alo = sb("alo", [P, KT, T], F32R)
        ident = sb("ident", [P, P])
        ones = sb("ones", [P, P])
        tri = sb("tri", [P, P])
        negm = sb("negm", [P, P])
        posm = sb("posm", [P, P])
        rowsel = sb("rowsel", [B, B, P])
        own = sb("own", [B, H, B])
        rope_m = sb("rope_m", [P, NTT, 2, DH // 2])
        rope_ms = sb("rope_ms", [B, 2, DH // 2])
        rope_i = sb("rope_i", [P, NTT, 2, D_IDX // 2])
        rope_is = sb("rope_is", [B, 2, D_IDX // 2])
        vecs = sb("vecs", [82, P])
        gains = sb("gains", [P, 82])
        cwrows = sb("cwrows", [2 * NFT, 3, P])
        cw = sb("cw", [P, 3, 2 * NFT])
        qg = sb("qg", [P, DH])
        kg = sb("kg", [P, DH])
        ckg = sb("ckg", [P, 2 * DH])
        bif = sb("bif", [P, 2 * H])
        epsc = sb("epsc", [P, 1])
        gt = sb("gt", [P, NTT + 1, 2 * H])
        ptw = sb("ptw", [B * NPG, 1], I32)
        pidx = sb("pidx", [B * NPG, 4], U32)
        ptr = sb("ptr", [B, NPG], I32)
        G_MIX, G_CROSS, G_MEM, G_FFN, G_CQ, G_ML, G_CB = 0, 8, 16, 24, 32, 34, 38
        R0 = cursor[0]

        def reg(name, shape, at, dt=F32):
            return nc.alloc_sbuf_tensor_at(name, shape, dt, offset=R0 + 4 * at)

        z_m = reg("z_m", [P, 4 * H, T], 0)
        mk_tok = reg("mk_tok", [P, NTT, MIX], 8320)
        mv_tok = reg("mv_tok", [P, NTT, MIX], 10368)
        z_a = reg("z_a", [P, 3 * H, T], 12416)
        av_tok = reg("av_tok", [P, NTT, MIX], 18656)
        tk = reg("tk", [P, 4, SEQ], 20704)
        selb = reg("selb", [P, 9, P], 22752)
        aw = reg("aw", [P, 4, SEQ], 23904)
        rt = reg("rt", [P, 2, NTT, DH], 25952)
        rw = reg("rw", [P, 3, NTT, DH], 26976)
        s_tok = reg("s_tok", [B, 3, MIX], 28512)
        skv = reg("skv", [P, 2, 2, MIX], 30048)
        iw_tok = reg("iw_tok", [P, NTT, H], 32096)
        sw = reg("sw", [B, MIX], 32112)
        srow = reg("srow", [B, PAST + 8], 32624)
        sidx = reg("sidx", [B, TOPK_S], 33656, U32)
        rowf = reg("rowf", [B, TOPK_S], 33912)
        maskf = reg("maskf", [B, TOPK_S], 34168)
        sv = reg("sv", [B, MIX], 33912)
        rowT = reg("rowT", [P, 2, B], 34424, U32)
        maskT = reg("maskT", [P, 2, B], 34440)
        iqS = reg("iqS", [D_IDX, H, B], 34456)
        iwb = reg("iwb", [P, B, H], 34488)
        tiny = reg("tiny", [P, 200], 34520)
        s_scr = reg("s_scr", [P, 4, 2, B, H], 7400)
        s_sum = reg("s_sum", [P, 4, 2, B], 7656)
        sg = reg("sg", [B * NPG, 2048], 30048)
        ikc = reg("ikc", [D_IDX, B * NPG, 32], 23904)
        x_in = reg("x_in", [P, NTT, D], 4160)
        xs_in = reg("xs_in", [B, D], 8320)
        xT0 = reg("xT0", [P, KT, T], 0)
        sq = reg("sq", [P, 2, T], 12416)
        rstd = reg("rstd", [P, T], 13456)
        hs = reg("hs", [P, 2, T], 13976)
        z_i = reg("z_i", [P, 3, T], 4160)
        m_tok = reg("m_tok", [P, NTT, N_MISC], 5720)
        ms_tok = reg("ms_tok", [B, N_MISC], 7048)
        m_rot = reg("m_rot", [P, NTT, 3 * P], 8320)
        ms_rot = reg("ms_rot", [B, 3 * P], 9856)
        m_tmp = reg("m_tmp", [P, 2, 5 * D_IDX], 10240)
        iqT = reg("iqT", [P, 3, SEQ], 10880)

        PS = ctx.enter_context(nc.psum_tensor("PS", [P, 8, 512], F32))
        PJ = [PS[:, 0:2, :], PS[:, 2:4, :]]
        TA, TB, XA, XB = (PS[:, b, :] for b in (4, 5, 6, 7))

        consts_in, gates_in, x_in_s = sem("consts_in"), sem("gates_in"), sem("x_in_s")
        consts_made, vec_ready = sem("consts_made"), sem("vec_ready")
        raw_full = [sem("raw_full0"), sem("raw_full1")]
        hi_full = [sem("hi_full0"), sem("hi_full1")]
        split_full = [sem("split_full0"), sem("split_full1")]
        w_used = [sem("w_used0"), sem("w_used1")]
        out_free = [sem("out_free0"), sem("out_free1")]
        xT_turned, xT_ready, sq_ready, sq_used = sem("xT_turned"), sem("xT_ready"), sem("sq_ready"), sem("sq_used")
        rstd_ready, hs_ready, nhi_ready, nlo_ready = (
            sem("rstd_ready"), sem("hs_ready"), sem("nhi_ready"), sem("nlo_ready"))
        v_step, a_step = sem("v_step"), sem("a_step")

        bank_full = [sem(f"bank{b}_full") for b in range(4)]
        bank_read = [sem(f"bank{b}_read") for b in range(4)]
        BANKS = [TA, TB, XA, XB]
        filled, taken = [0] * 4, [0] * 4

        def pe_bank(pe, b):
            if filled[b]:
                pe.wait_ge(bank_read[b], filled[b])
            filled[b] += 1
            return BANKS[b]

        def rd_bank(eng, b):
            taken[b] += 1
            eng.wait_ge(bank_full[b], taken[b])
            return BANKS[b]

        count = {}

        def signal(eng, ins, s):
            count[s.name] = count.get(s.name, 0) + 1
            ins.then_inc(s, 1)
            eng.wait_ge(s, count[s.name])

        def S(ins, s=None):
            signal(nc.scalar, ins, a_step if s is None else s)

        def V(ins, s=None):
            signal(nc.vector, ins, v_step if s is None else s)

        def uses(n):
            return n % 2, n // 2

        N_IN = len(IN_TILES)
        BASE0 = (N_IN + 1) // 2


        def pe_product(s, out, m, kt, hi, lo, first=True, last=True, k0=0):
            for k in range(kt):
                for j, (w, x) in enumerate(((whi, hi), (whi, lo), (wlo, hi))):
                    for half in range(2):
                        ins = nc.tensor.matmul(out[0:m, half, 0:HALF], w[:, s, k, 0:m],
                                               x[:, k0 + k, half * HALF:(half + 1) * HALF],
                                               start=(first and k == 0 and j == 0),
                                               stop=(last and k == kt - 1 and j == 2))
            return ins

        def pe_sumsq(pe, stage, k, squares, width):
            pe.wait_ge(sq_ready, KT * stage + k + 1)
            w = width // 2
            for half in range(2):
                bank = pe_bank(pe, half) if k == 0 else BANKS[half]
                ins = nc.tensor.matmul(bank[:, 0:w], ones[:], squares[:, k % 2, half * w:(half + 1) * w],
                                       start=(k == 0), stop=(k == KT - 1))
            ins.then_inc(sq_used, 1)

        def act_rstd(act, stage, out, width, n):
            act.wait_ge(sq_used, KT * (stage + 1))
            w = width // 2
            for half in range(2):
                S(nc.scalar.activation(out[:, half * w:(half + 1) * w], BANKS[half][:, 0:w], ACT.Ln, bias=epsc[:],
                                       scale=1.0 / n), bank_read[half])
            S(nc.scalar.activation(out[:, 0:width], out[:, 0:width], ACT.Exp, scale=-0.5), rstd_ready)

        def vec_norm(dve, stage, src, r, g0, h, width, lo=None):
            hi, lo = (ahi, alo) if lo is None else lo
            dve.wait_ge(rstd_ready, stage + 1)
            for k in range(KT + 1):
                if k < KT:
                    if KT * stage + k >= 2:
                        dve.wait_ge(nlo_ready, KT * stage + k - 1)
                    nc.vector.scalar_tensor_tensor(h[:, k % 2, 0:width], src[:, k, 0:width], gains[:, g0 + k:g0 + k + 1],
                                                   r[:, 0:width], ALU.mult, ALU.mult).then_inc(hs_ready, 1)
                if k:
                    dve.wait_ge(nhi_ready, KT * stage + k)
                    nc.vector.tensor_tensor(lo[:, k - 1, 0:width], h[:, (k - 1) % 2, 0:width],
                                            hi[:, k - 1, 0:width].bitcast(F32), ALU.subtract).then_inc(nlo_ready, 1)

        AFTER = {3: ["misc"], 5: ["idx_back"], 6: ["idx_score:1"], 7: ["idx_score:2"], 8: ["idx_score:3"],
                 9: ["gather:0"], 13: ["gather:1"], 14: ["turn:aq0"], 15: ["turn:aq1", "back:aq0", "turn:av0"],
                 16: ["turn:aq2", "back:aq1", "turn:av1"], 17: ["gather:2", "turn:aq3", "back:aq2", "turn:av2"],
                 18: ["turn:av3", "back:aq3", "back_s:aq", "turn:ak0"], 19: ["turn:ak1", "back:ak0", "turn:mq0", "turn:mq1"],
                 20: ["turn:ak2", "back:ak1", "turn:mq2", "turn:mq3"], 21: ["gather:3", "turn:ak3", "back:ak2"],
                 22: ["sidx", "back:ak3", "back_s:ak"], 23: ["turn:mk0"], 24: ["turn:mk1"], 25: ["turn:mk2"],
                 26: ["turn:mk3"], 27: ["turn:mv0"], 28: ["turn:mv1"], 29: ["turn:mv2"], 30: ["turn:mv3"]}
        ROT = 5 * D_IDX

        def halves(x, h):
            return x.rearrange("p (h a d) -> p h a d", h=h, a=2)

        def rope(x, t1, t2, out, cos, sin):
            shape = list(x.shape)
            for a in range(2):
                V(nc.vector.tensor_tensor(t1[:, :, a], x[:, :, a], cos, ALU.mult))
                V(nc.vector.tensor_tensor(t2[:, :, a], x[:, :, 1 - a], sin, ALU.mult))
            V(nc.vector.tensor_tensor(out[:, :, 0], t1[:, :, 0], t2[:, :, 0], ALU.subtract))
            return nc.vector.tensor_tensor(out[:, :, 1], t1[:, :, 1], t2[:, :, 1], ALU.add)

        def tile_ready(eng, name):
            s, u = uses(TI[name])
            eng.wait_ge(out_free[s], u + 1)

        (misc_tok, gate_abs, gate_ln, iqT_ready, m_rot_ready, iwm_ready, rl_used, rl_ready, sg_full, ikc_full, s_scr_ready,
         s_sum_ready, srow_ready, rows_found, rt_ready, rs_ready, head_copied, head_sq, head_ss, head_rstd,
         back_ready, sv_stored, stores, pidx_ready) = (sem(x) for x in (
             "misc_tok gate_abs gate_ln iqT_ready m_rot_ready iwm_ready rl_used rl_ready sg_full ikc_full s_scr_ready "
             "s_sum_ready srow_ready rows_found rt_ready rs_ready head_copied head_sq head_ss head_rstd "
             "back_ready sv_stored stores pidx_ready").split())
        rt_stored = [sem("rt_stored0"), sem("rt_stored1")]
        turn_ready = {g: sem(f"turn_{g}") for g in ("aq", "ak", "av", "mq", "mk", "mv")}

        def pe_misc(pe):
            tile_ready(pe, "iq1")
            tile_ready(pe, "ikw")
            r = D_IDX + 3 * H
            for tt in range(NTT + 1):
                w = P if tt < NTT else B
                bank = pe_bank(pe, tt % 2)
                for f, rows in ((0, P), (1, P), (2, r)):
                    m = nc.tensor.transpose(bank[0:w, f * P:f * P + rows], z_i[0:rows, f, tt * P:tt * P + w],
                                            ident[0:rows, 0:rows])
                m.then_inc(bank_full[tt % 2], 1)

        def pe_idx_back(pe):
            pe.wait_ge(m_rot_ready, NTT + 1)
            for f in range(3):
                bank = pe_bank(pe, f % 2)
                for tt in range(NTT):
                    m = nc.tensor.transpose(bank[:, tt * P:(tt + 1) * P], m_rot[:, tt, f * P:(f + 1) * P], ident[:])
                m.then_inc(bank_full[f % 2], 1)
            bank = pe_bank(pe, 1)
            for h in range(H):
                m = nc.tensor.transpose(bank[0:D_IDX, h * B:(h + 1) * B], ms_rot[:, h * D_IDX:(h + 1) * D_IDX],
                                        ident[0:B, 0:B])
            m.then_inc(bank_full[1], 1)
            pe.wait_ge(iwm_ready, 1)
            m = nc.tensor.matmul(pe_bank(pe, 0)[:, 0:B * H], ones[0:B, :], tiny[0:B, 64:96], start=True, stop=True)
            m.then_inc(bank_full[0], 1)

        def pe_idx_score(pe, qt):
            pe.wait_ge(iqT_ready, 3)
            n = (qt + 1) * P
            for h in range(H):
                r = D_IDX * (h % 2)
                nc.tensor.matmul(pe_bank(pe, h % 2)[:, 0:n], iqT[r:r + D_IDX, h // 2, qt * P:(qt + 1) * P],
                                 iqT[r:r + D_IDX, 2, 0:n], start=True, stop=True).then_inc(bank_full[h % 2], 1)

        def pe_gather(pe, c):
            pe.wait_ge(sg_full, 16 * (c + 1))
            for g in range(4):
                bank = pe_bank(pe, g % 2)
                for r in range(8):
                    m = nc.tensor.transpose(bank[0:D_IDX, r * D_IDX:(r + 1) * D_IDX],
                                            sg[:, (g * 8 + r) * D_IDX:(g * 8 + r + 1) * D_IDX], ident[0:B * NPG, 0:B * NPG])
                m.then_inc(bank_full[g % 2], 1)
            pe.wait_ge(ikc_full, 4 * (c + 1))
            bank = pe_bank(pe, 0)
            for b in range(B):
                for pg in range(2):
                    j = (pg * B + b) * H
                    p0 = b * NPG + 4 * pg
                    m = nc.tensor.matmul(bank[:, j:j + H], ikc[:, p0:p0 + 4, :].rearrange("d a r -> d (a r)"),
                                         iqS[:, :, b], start=True, stop=True)
            m.then_inc(bank_full[0], 1)

        def pe_sidx(pe):
            pe.wait_ge(s_sum_ready, 1)
            for pg in range(2):
                bank = pe_bank(pe, pg)
                for c in range(4):
                    m = nc.tensor.transpose(bank[0:B, c * P:(c + 1) * P], s_sum[:, c, pg, :], ident[:])
                m.then_inc(bank_full[pg], 1)

        def pe_turn(pe, name):
            tile_ready(pe, name)
            n = TI[name]
            z = z_a[:, n - 3] if n < 15 else z_m[:, n - 15]
            if name[:2] != "mq":
                bank = pe_bank(pe, 0)
                for tt in range(NTT):
                    m = nc.tensor.transpose(bank[:, tt * P:(tt + 1) * P], z[:, tt * P:(tt + 1) * P], ident[:])
                m.then_inc(bank_full[0], 1)
            if name[:2] != "mv":
                nc.tensor.transpose(pe_bank(pe, 1)[0:B, 0:P], z[:, SEQ:T], ident[:]).then_inc(bank_full[1], 1)

        def pe_back(pe, g, h):
            j = H * g + h
            pe.wait_ge(rt_ready, j + 1)
            bank = pe_bank(pe, 0)
            for tt in range(NTT):
                m = nc.tensor.transpose(bank[:, tt * P:(tt + 1) * P], rt[:, j % 2, tt, :], ident[:])
            m.then_inc(bank_full[0], 1)

        def pe_back_s(pe, g):
            pe.wait_ge(rs_ready, g + 1)
            bank = pe_bank(pe, 1)
            src = sw if g == 0 else s_tok[:, 0, :]
            for h in range(H):
                m = nc.tensor.transpose(bank[:, h * B:(h + 1) * B], src[:, h * DH:(h + 1) * DH], ident[0:B, 0:B])
            m.then_inc(bank_full[1], 1)

        def act_misc(act):
            for tt in range(NTT + 1):
                bank = rd_bank(act, tt % 2)
                dst, w = (m_tok[:, tt, :], P) if tt < NTT else (ms_tok[:], B)
                S(nc.scalar.copy(dst, bank[0:w, 0:N_MISC]), bank_read[tt % 2])
            act.sem_inc(misc_tok, 1)

        def act_gates(act):
            act.wait_ge(gate_abs, 1)
            S(nc.scalar.activation(tiny[:, 0:20], tiny[:, 0:20], ACT.Exp))
            S(nc.scalar.activation(tiny[:, 0:20], tiny[:, 0:20], ACT.Ln, bias=ones[:, 0:1]), gate_ln)

        def act_idx_back(act):
            for f in range(3):
                bank = rd_bank(act, f % 2)
                S(nc.scalar.copy(iqT[:, f, :], bank[:]), bank_read[f % 2])
                act.sem_inc(iqT_ready, 1)
            S(nc.scalar.copy(iqS[:].rearrange("d h b -> d (h b)"), rd_bank(act, 1)[0:D_IDX, 0:H * B]), bank_read[1])
            S(nc.scalar.copy(iwb[:].rearrange("p b h -> p (b h)"), rd_bank(act, 0)[:, 0:H * B]), bank_read[0])
            act.dma_start(O["p_idx_k"][0, 0].rearrange("(t p) d -> p t d", p=P),
                          m_rot[:, :, H * D_IDX:ROT]).then_inc(stores, 16)
            act.dma_start(O["s_idx_k"][0, :, 0, :], ms_rot[:, H * D_IDX:ROT]).then_inc(stores, 16)

        def act_idx_score(act, qt):
            n = (qt + 1) * P
            for h in range(H):
                j = 4 * (qt - 1) + h
                bank = rd_bank(act, h % 2)
                if j >= 2:
                    act.wait_ge(rl_used, j - 1)
                S(nc.scalar.activation(tk[:, 2 + h % 2, 0:n], bank[:, 0:n], ACT.Relu), bank_read[h % 2])
                act.sem_inc(rl_ready, 1)

        def act_gather(act, c):
            for g in range(4):
                bank = rd_bank(act, g % 2)
                S(nc.scalar.copy(ikc[:, :, g * 8:(g + 1) * 8].rearrange("d q r -> d r q"),
                                 bank[0:D_IDX, :].rearrange("d (r q) -> d r q", r=8)), bank_read[g % 2])
                act.sem_inc(ikc_full, 1)
            S(nc.scalar.activation(s_scr[:, c].rearrange("p g b h -> p (g b h)"), rd_bank(act, 0)[:, 0:2 * B * H],
                                   ACT.Relu), bank_read[0])
            act.sem_inc(s_scr_ready, 1)

        def act_sidx(act):
            for pg in range(2):
                bank = rd_bank(act, pg)
                for c in range(4):
                    S(nc.scalar.copy(srow[:, pg * 512:(pg + 1) * 512].rearrange("b (g c r) -> b g c r", g=4, c=4)[:, :, c],
                                     bank[0:B, c * P:(c + 1) * P].rearrange("b (g r) -> b g r", g=4)),
                      bank_read[pg] if c == 3 else None)
            act.sem_inc(srow_ready, 1)

        def act_rms_small(act, x, n, sem_in, k, sem_out):
            act.wait_ge(sem_in, k)
            S(nc.scalar.activation(x, x, ACT.Ln, bias=epsc[0:x.shape[0]], scale=1.0 / n))
            S(nc.scalar.activation(x, x, ACT.Exp, scale=-0.5), sem_out)

        def act_turn(act, name):
            g, h = name[:2], int(name[2])
            if g in ("aq", "ak"):
                j = h + (H if g == "ak" else 0)
                if j:
                    act.wait_ge(rt_ready, j)
            dst = {"aq": rw[:, 0], "ak": rw[:, 0], "av": av_tok[:, :, h * DH:(h + 1) * DH],
                   "mk": mk_tok[:, :, h * DH:(h + 1) * DH], "mv": mv_tok[:, :, h * DH:(h + 1) * DH]}.get(g)
            if dst is not None:
                S(nc.scalar.copy(dst, rd_bank(act, 0)[:].rearrange("p (t d) -> p t d", t=NTT)), bank_read[0])
            sdst = {"aq": sw[:, h * DH:(h + 1) * DH], "ak": s_tok[:, 0, h * DH:(h + 1) * DH], "av": sv[:, h * DH:(h + 1) * DH],
                    "mq": s_tok[:, 1, h * DH:(h + 1) * DH], "mk": s_tok[:, 2, h * DH:(h + 1) * DH]}.get(g)
            if sdst is not None:
                S(nc.scalar.copy(sdst, rd_bank(act, 1)[0:B, 0:DH]), bank_read[1])
            act.sem_inc(turn_ready[g], 1)
            if g == "av" and h == H - 1:
                act.dma_start(O["p_v"][0, 0].rearrange("(t p) h d -> p t (h d)", p=P), av_tok[:]).then_inc(stores, 16)
                act.dma_start(O["s_v"][0, :, 0].rearrange("b h d -> b (h d)"), sv[:]).then_inc(sv_stored, 16)

        def act_norm_head(act, j):
            act.wait_ge(head_copied, j + 1)
            S(nc.scalar.activation(rw[:, 1], rw[:, 0], ACT.Square), head_sq)
            k = jn(j // H, j % H) + 1
            act_rms_small(act, tiny[:, 20:24], DH, head_ss, k, head_rstd)

        def act_back(act, g, h):
            j = H * g + h
            bank = rd_bank(act, 0)
            S(nc.scalar.copy(z_a[:, j, 0:SEQ], bank[:]), bank_read[0])
            act.sem_inc(back_ready, 1)
            if g == 1:
                act.dma_start(O["p_k"][0, 0].rearrange("(t p) h d -> p t h d", p=P)[:, :, h, :],
                              rt[:, j % 2]).then_inc(rt_stored[j % 2], 16)

        def act_back_s(act, g):
            S(nc.scalar.copy(z_a[:, H * g:H * (g + 1), SEQ:T],
                             rd_bank(act, 1)[:, 0:H * B].rearrange("p (h b) -> p h b", h=H)), bank_read[1])
            if g == 1:
                act.dma_start(O["s_k"][0, :, 0].rearrange("b h d -> b (h d)"), s_tok[:, 0, :]).then_inc(stores, 16)

        def vec_misc(dve):
            v = nc.vector
            dve.wait_ge(misc_tok, 1)
            dve.wait_ge(consts_in, 16 * 18)
            for tt in range(NTT + 1):
                prompt = tt < NTT
                x, rot, w = (m_tok[:, tt], m_rot[:, tt], P) if prompt else (ms_tok[:], ms_rot[:], B)
                tab = rope_i[:, tt] if prompt else rope_is[:]
                cos, sin = (tab[:, a].unsqueeze(1).to_broadcast([w, 5, D_IDX // 2]) for a in range(2))
                V(rope(halves(x[:, 0:ROT], 5), halves(m_tmp[0:w, 0], 5), halves(m_tmp[0:w, 1], 5),
                       halves(rot[:, 0:ROT], 5), cos, sin))
                V(v.tensor_copy(rot[:, ROT:ROT + D_IDX], rot[:, H * D_IDX:ROT]), m_rot_ready)
                if prompt:
                    V(v.tensor_copy(iw_tok[:, tt], x[:, ROT:ROT + H]))
                V(v.tensor_tensor(gt[0:w, tt], x[:, ROT + H:N_MISC], bif[0:w], ALU.add))
            f = gt[:, :, H:2 * H]
            ab = tiny[:, 0:20].rearrange("p (t h) -> p t h", h=H)
            V(v.scalar_tensor_tensor(ab, f, -1.0, f, ALU.mult, ALU.min), gate_abs)
            V(v.tensor_tensor(tiny[0:B, 64:96].rearrange("r (b h) -> r b h", b=B), own[:].rearrange("r h b -> r b h"),
                              ms_tok[:, ROT:ROT + H].unsqueeze(1).to_broadcast([B, B, H]), ALU.mult), iwm_ready)

        def vec_gates(dve):
            f = gt[:, :, H:2 * H]
            dve.wait_ge(gate_ln, 1)
            V(nc.vector.scalar_tensor_tensor(f, f, 0.0, tiny[:, 0:20].rearrange("p (t h) -> p t h", h=H), ALU.min,
                                             ALU.subtract))

        def vec_new_score(dve):
            v = nc.vector
            t = rw[0:B, 2].rearrange("b t d -> b (t d)")[:, 0:256]
            V(v.tensor_tensor(t.rearrange("b (h d) -> b h d", h=H), ms_rot[:, 0:256].rearrange("b (h d) -> b h d", h=H),
                              ms_rot[:, 256:320].unsqueeze(1).to_broadcast([B, H, D_IDX]), ALU.mult))
            V(v.tensor_reduce(tiny[0:B, 96:100], t.rearrange("b (h d) -> b h d", h=H), AX, ALU.add))
            V(v.scalar_tensor_tensor(tiny[0:B, 100:104], tiny[0:B, 96:100], 0.0, ms_tok[:, ROT:ROT + H], ALU.max, ALU.mult))
            V(v.tensor_reduce(srow[:, PAST:PAST + 1], tiny[0:B, 100:104], AX, ALU.add))

        def take_rounds(row, m8, rounds, idx=None):
            v = nc.vector
            for r in range(rounds):
                V(v.max(m8, row))
                if idx is not None:
                    V(v.max_index(idx[:, r * 8:(r + 1) * 8], m8, row))
                V(v.match_replace(row, m8, row, TAKEN))

        def vec_idx_score(dve, qt):
            v = nc.vector
            n = (qt + 1) * P
            acc = tk[:, qt % 2, 0:n]
            for h in range(H):
                dve.wait_ge(rl_ready, 4 * (qt - 1) + h + 1)
                w = iw_tok[:, qt, h:h + 1]
                if h == 0:
                    V(v.tensor_scalar(acc, tk[:, 2 + h % 2, 0:n], w, None, ALU.mult), rl_used)
                else:
                    V(v.scalar_tensor_tensor(acc, tk[:, 2 + h % 2, 0:n], w, acc, ALU.mult, ALU.add), rl_used)
            V(v.tensor_tensor(acc[:, qt * P:n], acc[:, qt * P:n], negm[:], ALU.add))
            take_rounds(acc, tiny[:, 24:32], TOPK_P // 8)
            o = (0, 2, 5)[qt - 1]
            V(v.tensor_scalar(selb[:, o:o + qt + 1, :].rearrange("p a b -> p (a b)"), acc, 0.1 * TAKEN, NEG,
                              ALU.is_gt, ALU.mult))

        def vec_gather(dve, c):
            if c < 3:
                return
            v = nc.vector
            dve.wait_ge(s_scr_ready, 4)
            x = s_scr[:].rearrange("p c g b h -> p (c g) (b h)")
            V(v.tensor_tensor(x, x, iwb[:].rearrange("p b h -> p (b h)").unsqueeze(1).to_broadcast([P, 8, B * H]), ALU.mult))
            V(v.tensor_reduce(s_sum[:].rearrange("p c g b -> p (c g b)"),
                              s_scr[:].rearrange("p c g b h -> p (c g b) h"), AX, ALU.add), s_sum_ready)

        def vec_sidx(dve):
            v = nc.vector
            dve.wait_ge(srow_ready, 1)
            row = srow[:, 0:PAST + 1]
            take_rounds(row, tiny[0:B, 32:40], TOPK_S // 8, sidx)
            V(v.tensor_scalar(tiny[0:B, 40:41], srow[:, PAST:PAST + 1], 0.1 * TAKEN, NEG, ALU.is_gt, ALU.mult))
            dve.wait_ge(sv_stored, 16)
            V(v.tensor_copy(rowf[:], sidx[:]))
            V(v.tensor_scalar(maskf[:], rowf[:], float(PAST), NEG, ALU.is_ge, ALU.mult))
            V(v.tensor_scalar(rowf[:], rowf[:], float(PAST - 1), None, ALU.min))
            d = tiny[0:B, 48:56]
            V(v.tensor_copy(d, ptr[:]))
            V(v.tensor_scalar(d, d, float(PAGE), None, ALU.mult))
            e = tiny[0:B, 56:64]
            V(v.tensor_tensor(e[:, 1:8], d[:, 1:8], d[:, 0:7], ALU.subtract))
            V(v.tensor_scalar(e[:, 1:8], e[:, 1:8], -float(PAGE), None, ALU.add))
            V(v.tensor_scalar(srow[:, 0:256], rowf[:], d[:, 0:1], None, ALU.add))
            for p in range(1, NPG):
                V(v.tensor_scalar(srow[:, 256:512], rowf[:], float(PAGE * p), e[:, p:p + 1], ALU.is_ge, ALU.mult))
                V(v.tensor_tensor(srow[:, 0:256], srow[:, 0:256], srow[:, 256:512], ALU.add))
            V(v.tensor_copy(rowf[:], srow[:, 0:256]), rows_found)

        def vec_norm_rope(dve, x, t1, t2, out, gain, tab, rstd_col, ready_s, j, w):
            v = nc.vector
            V(v.tensor_reduce(rstd_col, t1, AX, ALU.add), head_ss)
            dve.wait_ge(head_rstd, j + 1)
            V(v.tensor_tensor(x, x, rstd_col.unsqueeze(2).to_broadcast([w, 4, DH]), ALU.mult))
            V(v.tensor_tensor(x, x, gain[0:w].unsqueeze(1).to_broadcast([w, 4, DH]), ALU.mult))
            spl = lambda y: y.rearrange("p t (a d) -> p t a d", a=2)
            V(rope(spl(x), spl(t1), spl(t2), spl(out), tab[0], tab[1]), ready_s)

        def vec_head(dve, g, h):
            j = H * g + h
            dve.wait_ge(turn_ready[("aq", "ak")[g]], h + 1)
            dve.sem_inc(head_copied, 1)
            dve.wait_ge(head_sq, j + 1)
            if j >= 2:
                dve.wait_ge(back_ready, j - 1)
                if j >= 6:
                    dve.wait_ge(rt_stored[j % 2], 16 * ((j - 4) // 2))
            tab = [rope_m[:, :, a] for a in range(2)]
            vec_norm_rope(dve, rw[:, 0], rw[:, 1], rw[:, 2], rt[:, j % 2], (qg, kg)[g], tab, tiny[:, 20:24], rt_ready,
                          jn(g, h), P)

        def vec_head_s(dve, g):
            x = (sw[:] if g == 0 else s_tok[:, 0, :]).rearrange("b (h d) -> b h d", h=H)
            V(nc.vector.tensor_tensor(rw[0:B, 1], x, x, ALU.mult))
            tab = [rope_ms[:, a].unsqueeze(1).to_broadcast([B, 4, DH // 2]) for a in range(2)]
            vec_norm_rope(dve, x, rw[0:B, 1], rw[0:B, 2], x, (qg, kg)[g], tab, tiny[0:B, 20:24], rs_ready, jn(g, H), B)

        def jn(g, h):
            return (H + 1) * g + h

        def pe_hooks(pe, n):
            for step in AFTER.get(n, ()):
                what, _, arg = step.partition(":")
                if what == "misc":
                    pe_misc(pe)
                elif what == "idx_back":
                    pe_idx_back(pe)
                elif what == "idx_score":
                    pe_idx_score(pe, int(arg))
                elif what == "gather":
                    pe_gather(pe, int(arg))
                elif what == "sidx":
                    pe_sidx(pe)
                elif what == "turn":
                    pe_turn(pe, arg)
                elif what == "back":
                    pe_back(pe, ("aq", "ak").index(arg[:2]), int(arg[2]))
                elif what == "back_s":
                    pe_back_s(pe, ("aq", "ak").index(arg))

        def act_hooks(act, n):
            for step in AFTER.get(n, ()):
                what, _, arg = step.partition(":")
                if what == "misc":
                    act_misc(act)
                    act_gates(act)
                elif what == "idx_back":
                    act_idx_back(act)
                elif what == "idx_score":
                    act_idx_score(act, int(arg))
                elif what == "gather":
                    act_gather(act, int(arg))
                elif what == "sidx":
                    act_sidx(act)
                elif what == "turn":
                    act_turn(act, arg)
                    if arg[:2] in ("aq", "ak"):
                        act_norm_head(act, H * ("aq", "ak").index(arg[:2]) + int(arg[2]))
                elif what == "back":
                    act_back(act, ("aq", "ak").index(arg[:2]), int(arg[2]))
                elif what == "back_s":
                    g = ("aq", "ak").index(arg)
                    act_rms_small(act, tiny[0:B, 20:24], DH, head_ss, jn(g, H) + 1, head_rstd)
                    act_back_s(act, g)

        def vec_hooks(dve, n):
            for step in AFTER.get(n, ()):
                what, _, arg = step.partition(":")
                if what == "misc":
                    vec_misc(dve)
                    vec_gates(dve)
                    vec_new_score(dve)
                elif what == "idx_score":
                    vec_idx_score(dve, int(arg))
                elif what == "gather":
                    vec_gather(dve, int(arg))
                elif what == "sidx":
                    vec_sidx(dve)
                elif what == "turn" and arg[:2] in ("aq", "ak"):
                    vec_head(dve, ("aq", "ak").index(arg[:2]), int(arg[2]))
                elif what == "back_s":
                    vec_head_s(dve, ("aq", "ak").index(arg))

        def pool_hooks(pool, n):
            c = {6: 0, 12: 1, 16: 2, 20: 3}.get(n)
            if c is not None:
                if c == 0:
                    pool.wait_ge(pidx_ready, 1)
                else:
                    pool.wait_ge(ikc_full, 4 * c)
                nc.gpsimd.indirect_dma_start(sg[:], None, A["cache_idx_k"][0].rearrange("n (c r) d -> (n c) (r d)", c=4),
                                             bass.IndirectOffsetOnAxis(ap=pidx[:, c:c + 1], axis=0)).then_inc(sg_full, 16)

        (att_max, att_exp, att_p, p_turned, pv_done, kT_ready, rowT_ready, sk_masked, sp_max, sp_exp, sp_ready, spT_ready, v_used,
         ya_ready, ab_ready, arow_ready, mrow_ready, mb_ready, em_ready, md_ready, dd_ready, wd_ready, nd_done,
         wv_ready, h_ready, hsq_ready, hrs_ready, sig_exp, ym_ready, n_ready, qm_ready, cs_in, sc_in,
         y_hi, y_lo, sst_ready, sx_a, sx_b, shs_ready) = (sem(x) for x in (
             "att_max att_exp att_p p_turned pv_done kT_ready rowT_ready sk_masked sp_max sp_exp sp_ready spT_ready v_used "
             "ya_ready ab_ready arow_ready mrow_ready mb_ready em_ready md_ready dd_ready wd_ready nd_done "
             "wv_ready h_ready hsq_ready hrs_ready sig_exp ym_ready n_ready qm_ready cs_in sc_in "
             "y_hi y_lo sst_ready sx_a sx_b shs_ready").split())
        skv_full = [sem("skv_full0"), sem("skv_full1")]
        SEL = [None, (0, 2), (2, 5), (5, 9)]
        N_ATT = H * NTT

        def acol(j, c):
            return tiny[:, 8 + 4 * (j % 2) + c:9 + 4 * (j % 2) + c]

        def pe_att(pe, i):
            if i < N_ATT:
                h, qt = divmod(i, NTT)
                if i == 0:
                    pe.wait_ge(back_ready, 2 * H)
                nc.tensor.matmul(pe_bank(pe, 2 + i % 2)[:, 0:(qt + 1) * P], z_a[:, h, qt * P:(qt + 1) * P],
                                 z_a[:, H + h, 0:(qt + 1) * P], start=True, stop=True).then_inc(bank_full[2 + i % 2], 1)
            if 0 <= i - 1 < N_ATT:
                j = i - 1
                pe.wait_ge(att_p, j + 1)
                bank = pe_bank(pe, 0)
                for kt in range(j % NTT + 1):
                    m = nc.tensor.transpose(bank[:, kt * P:(kt + 1) * P], aw[:, j % 2, kt * P:(kt + 1) * P], ident[:])
                m.then_inc(bank_full[0], 1)
            if i >= 2:
                j = i - 2
                h, qt = divmod(j, NTT)
                pe.wait_ge(p_turned, j + 1)
                bank = pe_bank(pe, 1) if qt == 0 else BANKS[1]
                for kt in range(qt + 1):
                    m = nc.tensor.matmul(bank[:, qt * P:(qt + 1) * P], av_tok[:, kt, h * DH:(h + 1) * DH],
                                         aw[:, 2 + j % 2, kt * P:(kt + 1) * P], start=(kt == 0), stop=(kt == qt))
                m.then_inc(pv_done, 1)

        def act_att(act, i):
            if i < N_ATT:
                n = (i % NTT + 1) * P
                act.wait_ge(att_max, i + 1)
                S(nc.scalar.activation(aw[:, i % 2, 0:n], aw[:, i % 2, 0:n], ACT.Exp, bias=acol(i, 1), scale=SCALE,
                                       accum_out=acol(i, 2)), att_exp)
            if 0 <= i - 1 < N_ATT:
                j = i - 1
                n = (j % NTT + 1) * P
                bank = rd_bank(act, 0)
                if j >= 2:
                    act.wait_ge(pv_done, j - 1)
                S(nc.scalar.copy(aw[:, 2 + j % 2, 0:n], bank[:, 0:n]), bank_read[0])
                act.sem_inc(p_turned, 1)
            if i >= 2 and (i - 2) % NTT == NTT - 1:
                h = (i - 2) // NTT
                act.wait_ge(pv_done, i - 1)
                S(nc.scalar.copy(z_a[:, 2 * H + h, 0:SEQ], BANKS[1][:]), bank_read[1])

        def vec_att(dve, i):
            v = nc.vector
            if i < N_ATT:
                qt = i % NTT
                n = (qt + 1) * P
                bank = rd_bank(dve, 2 + i % 2)
                if i >= 2:
                    dve.wait_ge(p_turned, i - 1)
                bias = negm[:] if qt == 0 else selb[:, SEL[qt][0]:SEL[qt][1], :].rearrange("p a b -> p (a b)")
                V(v.tensor_tensor_reduce(aw[:, i % 2, 0:n], bank[:, 0:n], bias, 1.0, TAKEN, ALU.add, ALU.max, acol(i, 0)),
                  bank_read[2 + i % 2])
                V(v.tensor_scalar(acol(i, 1), acol(i, 0), -SCALE, None, ALU.mult), att_max)
            if 0 <= i - 1 < N_ATT:
                j = i - 1
                n = (j % NTT + 1) * P
                dve.wait_ge(att_exp, j + 1)
                V(v.reciprocal(acol(j, 3), acol(j, 2)))
                V(v.tensor_scalar(aw[:, j % 2, 0:n], aw[:, j % 2, 0:n], acol(j, 3), None, ALU.mult), att_p)

        HB = H * B
        S64 = tiny[:, 104:168]
        spT = tiny[:, 104:200]
        qkn = iwb[:].rearrange("p b h -> p (b h)")
        sp = aw[0:HB, 0, 0:2 * P + 1]

        def pe_satt_rows(pe):
            pe.wait_ge(rows_found, 1)
            bank = pe_bank(pe, 2)
            for t in range(2):
                nc.tensor.transpose(bank[:, t * B:(t + 1) * B], rowf[:, t * P:(t + 1) * P], ident[0:B, 0:B])
            for t in range(2):
                m = nc.tensor.transpose(bank[:, (2 + t) * B:(3 + t) * B], maskf[:, t * P:(t + 1) * P], ident[0:B, 0:B])
            m.then_inc(bank_full[2], 1)

        def vec_satt_rows(dve):
            bank = rd_bank(dve, 2)
            V(nc.vector.tensor_copy(rowT[:].rearrange("p t b -> p (t b)"), bank[:, 0:2 * B]), rowT_ready)
            V(nc.vector.tensor_copy(maskT[:].rearrange("p t b -> p (t b)"), bank[:, 2 * B:4 * B]), bank_read[2])
            V(nc.vector.tensor_tensor(qkn.rearrange("p (h b) -> p h b", h=H), z_a[:, 0:H, SEQ:T], z_a[:, H:2 * H, SEQ:T],
                                      ALU.mult))

        def pool_satt(pool):
            pool.wait_ge(rowT_ready, 1)
            for i, (cache, sem_used) in enumerate(((A["cache_k"], kT_ready), (A["cache_v"], v_used))):
                table = cache[0].rearrange("n r h d -> (n r) (h d)")
                for b in range(B):
                    if i == 0 and b >= 2:
                        pool.wait_ge(kT_ready, 2 * (b - 1))
                    if i == 1:
                        if b < 2:
                            pool.wait_ge(kT_ready, 2 * (B - 1 + b))
                        else:
                            pool.wait_ge(v_used, b - 1)
                    for t in range(2):
                        nc.gpsimd.indirect_dma_start(skv[:, b % 2, t, :], None, table, bass.IndirectOffsetOnAxis(
                            ap=rowT[:, t, b:b + 1], axis=0)).then_inc(skv_full[b % 2], 16)

        def pe_satt_k(pe, b):
            if b < B:
                pe.wait_ge(skv_full[b % 2], 32 * (b // 2 + 1))
                for t in range(2):
                    bank = pe_bank(pe, t)
                    for h in range(H):
                        m = nc.tensor.transpose(bank[:, h * P:(h + 1) * P], skv[:, b % 2, t, h * DH:(h + 1) * DH], ident[:])
                    m.then_inc(bank_full[t], 1)
            if b >= 1:
                c = b - 1
                pe.wait_ge(kT_ready, 2 * (c + 1))
                bank = pe_bank(pe, 2) if c == 0 else BANKS[2]
                for t in range(2):
                    for h in range(H):
                        j = (t * H + h) * B + c
                        m = nc.tensor.matmul(bank[:, j:j + 1], tk[:, 2 * (c % 2) + t, h * P:(h + 1) * P],
                                             z_a[:, h, SEQ + c:SEQ + c + 1], start=True, stop=True)
                m.then_inc(sx_a if c < B - 1 else bank_full[2], 1)

        def act_satt_k(act, b):
            if b < B:
                for t in range(2):
                    bank = rd_bank(act, t)
                    if t == 0 and b >= 2:
                        act.wait_ge(sx_a, b - 1)
                    S(nc.scalar.copy(tk[:, 2 * (b % 2) + t, :], bank[:]), bank_read[t])
                    act.sem_inc(kT_ready, 1)

        def pe_satt_soft(pe):
            pe.wait_ge(sk_masked, 1)
            bank = pe_bank(pe, 2)
            for t in range(2):
                nc.tensor.transpose(bank[0:HB, t * P:(t + 1) * P], S64[:, t * HB:(t + 1) * HB], ident[:])
            nc.tensor.matmul(bank[0:HB, 2 * P:2 * P + 1], qkn, ones[:, 0:1], start=True, stop=False)
            nc.tensor.matmul(bank[0:HB, 2 * P:2 * P + 1], own[:].rearrange("r h b -> r (h b)"), tiny[0:B, 40:41],
                             start=False, stop=True).then_inc(bank_full[2], 1)
            pe.wait_ge(sp_ready, 1)
            bank = pe_bank(pe, 3)
            for t in range(2):
                nc.tensor.transpose(bank[:, t * HB:(t + 1) * HB], sp[:, t * P:(t + 1) * P], ident[0:HB, 0:HB])
            nc.tensor.matmul(bank[:, 2 * HB:3 * HB], aw[0:HB, 1, 0:P], ident[0:HB, 0:HB], start=True,
                             stop=True).then_inc(bank_full[3], 1)

        def act_satt_soft(act):
            act.wait_ge(sp_max, 1)
            S(nc.scalar.activation(sp, sp, ACT.Exp, bias=tiny[0:HB, 9:10], scale=SCALE, accum_out=tiny[0:HB, 10:11]), sp_exp)

        def vec_satt_soft(dve):
            v = nc.vector
            V(v.tensor_tensor(S64.rearrange("p (t h b) -> p t h b", t=2, h=H),
                              rd_bank(dve, 2)[:, 0:2 * HB].rearrange("p (t h b) -> p t h b", t=2, h=H),
                              maskT[:].unsqueeze(2).to_broadcast([P, 2, H, B]), ALU.add), bank_read[2])
            dve.sem_inc(sk_masked, 1)
            V(v.tensor_copy(sp, rd_bank(dve, 2)[0:HB, 0:2 * P + 1]), bank_read[2])
            V(v.tensor_reduce(tiny[0:HB, 8:9], sp, AX, ALU.max))
            V(v.tensor_scalar(tiny[0:HB, 9:10], tiny[0:HB, 8:9], -SCALE, None, ALU.mult), sp_max)
            dve.wait_ge(sp_exp, 1)
            V(v.reciprocal(tiny[0:HB, 11:12], tiny[0:HB, 10:11]))
            V(v.tensor_scalar(sp, sp, tiny[0:HB, 11:12], None, ALU.mult))
            V(v.tensor_copy(aw[0:HB, 1, 0:P], sp[:, 2 * P:2 * P + 1].to_broadcast([HB, P])), sp_ready)
            V(v.tensor_copy(spT, rd_bank(dve, 3)[:, 0:3 * HB]), bank_read[3])
            dve.sem_inc(spT_ready, 1)

        def pe_satt_v(pe, b):
            if b == 0:
                pe.wait_ge(spT_ready, 1)
            bank = pe_bank(pe, 2) if b == 0 else BANKS[2]
            pe.wait_ge(skv_full[b % 2], 32 * (B // 2 + b // 2 + 1))
            for h in range(H):
                for t in range(2):
                    j = h * B + b
                    m = nc.tensor.matmul(bank[:, j:j + 1], skv[:, b % 2, t, h * DH:(h + 1) * DH],
                                         spT[:, t * HB + j:t * HB + j + 1], start=(t == 0), stop=(t == 1))
            m.then_inc(v_used, 1)

        def vec_satt_v(dve):
            ys = z_a[:, 2 * H:3 * H, SEQ:T]
            V(nc.vector.tensor_tensor(ys, ys, spT[:, 2 * HB:3 * HB].rearrange("p (h b) -> p h b", h=H), ALU.mult))
            dve.wait_ge(v_used, B)
            V(nc.vector.tensor_tensor(ys, ys, BANKS[2][:, 0:HB].rearrange("p (h b) -> p h b", h=H), ALU.add), bank_read[2])

        ab = reg("ab", [P, 2, NTT, H], 25952)
        wcol = reg("wcol", [P, 2, NTT], 25984)
        nml = reg("nml", [P, 1], 25992)
        sg_s = reg("sg_s", [P, H, B], 26000)
        Qb = reg("Qb", [P, 4, H, B], 26032)
        cq = reg("cq", [P, H, B], 26160)
        sx = reg("sx", [P, 4, HB], 26192)
        s8 = reg("s8", [B, 16, H], 26320)
        qm = reg("qm", [B, 4, H, B], 26384)
        rows = reg("rows", [H, 3, SEQ], 26976)
        mb, em, md = (reg(x, [P, SEQ], 12416 + 512 * i) for i, x in enumerate(("mb", "em", "md")))
        dd = reg("dd", [P, 2, SEQ], 13952)
        wv = reg("wv", [P, NTT, DH], 14976)
        dn = reg("dn", [P, SEQ], 15488)
        hb = reg("hb", [P, SEQ], 16000)
        hsq = reg("hsq", [P, SEQ], 30048)
        hrs = reg("hrs", [P, SEQ], 30560)
        sg_e = reg("sg_e", [P, T], 31072)
        cst = reg("cst", [P, 2, DH], 23904)
        nst = reg("nst", [1, H, DH], 24160)

        def pe_ml_prep(pe):
            bank = pe_bank(pe, 2)
            for c in range(NTT):
                for e in range(c + 1):
                    m = nc.tensor.matmul(bank[:, c * H:(c + 1) * H], ones[:] if e < c else tri[:], gt[:, e, H:2 * H],
                                         start=(e == 0), stop=(e == c))
            m.then_inc(bank_full[2], 1)
            pe.wait_ge(ab_ready, 1)
            for i in range(2):
                bank = pe_bank(pe, i)
                for c in range(NTT):
                    m = nc.tensor.transpose(bank[0:H, c * P:(c + 1) * P], ab[:, i, c, :], ident[:])
                m.then_inc(bank_full[i], 1)

        def act_ml_prep(act):
            for i in range(2):
                S(nc.scalar.copy(rows[:, i], rd_bank(act, i)[0:H, :]), bank_read[i])
            act.sem_inc(arow_ready, 1)

        def vec_ml_prep(dve):
            v = nc.vector
            for i in range(2):
                dve.wait_ge(rt_stored[i], 32)
            V(v.tensor_copy(ab[:, 1].rearrange("p c h -> p (c h)"), rd_bank(dve, 2)[:, 0:NTT * H]), bank_read[2])
            V(v.tensor_tensor(ab[:, 0], gt[:, 0:NTT, 0:H], ab[:, 1], ALU.subtract), ab_ready)
            dve.wait_ge(arow_ready, 1)
            V(v.tensor_tensor_scan(rows[:, 2], rows[:, 0], rows[:, 0], 0.0, ALU.max, ALU.max))
            V(v.tensor_tensor(rows[:, 1], rows[:, 1], rows[:, 2], ALU.add), mrow_ready)

        def pe_ml(pe, h):
            pe.wait_ge(mrow_ready, 1)
            for i, r in enumerate((2, 1)):
                nc.tensor.matmul(pe_bank(pe, i)[:], rowsel[0:H, h, :], rows[:, r], start=True,
                                 stop=True).then_inc(bank_full[i], 1)
            nd = PJ[h % 2]
            for st in range(NTT + 1):
                if st < NTT:
                    n = SEQ - st * P
                    nc.tensor.matmul(pe_bank(pe, 2 + st % 2)[:, 0:n], z_m[:, H + h, st * P:(st + 1) * P],
                                     z_m[:, h, st * P:SEQ], start=True, stop=True).then_inc(bank_full[2 + st % 2], 1)
                if st >= 1:
                    s = st - 1
                    n = SEQ - s * P
                    if s == 0 and h >= 2:
                        pe.wait_ge(h_ready, h - 1)
                    pe.wait_ge(wd_ready, NTT * h + s + 1)
                    nc.tensor.matmul(nd[:, 0, s * P:SEQ], mv_tok[:, s, h * DH:(h + 1) * DH], dd[:, s % 2, 0:n],
                                     start=(s == 0), stop=(s == NTT - 1))
                    nc.tensor.matmul(nd[:, 1, s * P:SEQ], ones[:], dd[:, s % 2, 0:n],
                                     start=(s == 0), stop=(s == NTT - 1)).then_inc(nd_done, 1)
            pe.wait_ge(wv_ready, h + 1)
            bank = pe_bank(pe, 0)
            for c in range(NTT):
                m = nc.tensor.matmul(bank[:, 0:DH], wv[:, c, :], mk_tok[:, c, h * DH:(h + 1) * DH],
                                     start=(c == 0), stop=(c == NTT - 1))
            m.then_inc(bank_full[0], 1)
            bank = pe_bank(pe, 1)
            for c in range(NTT):
                m = nc.tensor.matmul(bank[0:1, 0:DH], wcol[:, 1, c:c + 1], mk_tok[:, c, h * DH:(h + 1) * DH],
                                     start=(c == 0), stop=(c == NTT - 1))
            m.then_inc(bank_full[1], 1)
            pe.wait_ge(hsq_ready, h + 1)
            nc.tensor.matmul(pe_bank(pe, 0)[:], ones[:], hsq[:], start=True, stop=True).then_inc(bank_full[0], 1)

        def act_ml(act, h):
            a = nc.scalar
            S(a.copy(mb[:], rd_bank(act, 0)[:]), bank_read[0])
            act.sem_inc(mb_ready, 1)
            S(a.activation(em[:], rd_bank(act, 1)[:], ACT.Exp, scale=-1.0), bank_read[1])
            act.sem_inc(em_ready, 1)
            act.wait_ge(md_ready, h + 1)
            S(a.activation(wcol[:, 0, :], ab[:, 0, :, h], ACT.Exp, bias=nml[:]))
            for st in range(NTT):
                j = NTT * h + st
                if j >= 2:
                    act.wait_ge(nd_done, j - 1)
                bias = ab[:, 0, st, h:h + 1]
                S(a.activation(dd[:, st % 2, 0:P], md[:, st * P:(st + 1) * P], ACT.Exp, bias=bias, scale=-1.0))
                if st < NTT - 1:
                    S(a.activation(dd[:, st % 2, P:SEQ - st * P], mb[:, (st + 1) * P:SEQ], ACT.Exp, bias=bias, scale=-1.0))
                act.sem_inc(dd_ready, 1)
            if h >= 1:
                act.wait_ge(ym_ready, h)
            S(a.activation(sg_e[:], z_m[:, 3 * H + h, :], ACT.Exp, scale=-1.0), sig_exp)
            if h >= 2:
                act.wait_ge(c_stored[h % 2], 16 * (h // 2))
            S(a.copy(cst[:, h % 2], rd_bank(act, 0)[:, 0:DH]), bank_read[0])
            act.dma_start(O["p_c"][0, 0, h], cst[:, h % 2]).then_inc(c_stored[h % 2], 16)
            S(a.copy(nst[:, h], rd_bank(act, 1)[0:1, 0:DH]), bank_read[1])
            act.wait_ge(h_ready, h + 1)
            S(a.activation(hsq[:], hb[:], ACT.Square), hsq_ready)
            S(a.activation(hrs[:], rd_bank(act, 0)[:], ACT.Ln, bias=epsc[:], scale=1.0 / DH), bank_read[0])
            S(a.activation(hrs[:], hrs[:], ACT.Exp, scale=-0.5), hrs_ready)

        def vec_ml(dve, h):
            v = nc.vector
            dve.wait_ge(mb_ready, h + 1)
            V(v.tensor_tensor(md[:].rearrange("p (c t) -> p c t", c=NTT), mb[:].rearrange("p (c t) -> p c t", c=NTT),
                              posm[:].unsqueeze(1).to_broadcast([P, NTT, P]), ALU.add))
            V(v.tensor_scalar(nml[:], mb[:, SEQ - 1:SEQ], -1.0, None, ALU.mult), md_ready)
            for st in range(NTT):
                n = SEQ - st * P
                dve.wait_ge(dd_ready, NTT * h + st + 1)
                V(v.scalar_tensor_tensor(dd[:, st % 2, 0:n], rd_bank(dve, 2 + st % 2)[:, 0:n], SCALE, dd[:, st % 2, 0:n],
                                         ALU.mult, ALU.mult), bank_read[2 + st % 2])
                dve.sem_inc(wd_ready, 1)
                if st == 1:
                    V(v.tensor_scalar(wcol[:, 1], wcol[:, 0], SCALE, None, ALU.mult))
                    V(v.tensor_tensor(wv[:], mv_tok[:, :, h * DH:(h + 1) * DH],
                                      wcol[:, 1].unsqueeze(2).to_broadcast([P, NTT, DH]), ALU.mult), wv_ready)
            dve.wait_ge(sig_exp, h + 1)
            V(v.tensor_scalar(sg_e[:], sg_e[:], 1.0, None, ALU.add))
            V(v.reciprocal(sg_e[:], sg_e[:]))
            V(v.tensor_copy(sg_s[:, h], sg_e[:, SEQ:T]))
            dve.wait_ge(em_ready, h + 1)
            dve.wait_ge(nd_done, NTT * (h + 1))
            V(v.tensor_tensor(dn[:], PJ[h % 2][:, 1, :], em[:], ALU.max))
            V(v.scalar_tensor_tensor(dn[:], PJ[h % 2][:, 1, :], -1.0, dn[:], ALU.mult, ALU.max))
            V(v.reciprocal(dn[:], dn[:]))
            V(v.tensor_tensor(hb[:], PJ[h % 2][:, 0, :], dn[:], ALU.mult), h_ready)
            dve.wait_ge(hrs_ready, h + 1)
            y = z_m[:, 3 * H + h, 0:SEQ]
            V(v.scalar_tensor_tensor(y, hb[:], gains[:, G_ML + h:G_ML + h + 1], hrs[:], ALU.mult, ALU.mult))
            V(v.tensor_tensor(y, y, sg_e[:, 0:SEQ], ALU.mult), ym_ready)

        cb = reg("cb", [P, 2, H, DH], 20704)
        ct = reg("ct", [P, 2, H, DH], 21728)
        sn = reg("sn", [B, 2, H, DH], 22752)
        sm = reg("sm", [B, H], 23776)

        def sync_mls(sp):
            for b in range(B):
                if b >= 2:
                    sp.wait_ge(sc_stored[b % 2], 16 * (b // 2))
                else:
                    sp.wait_ge(kT_ready, 2 * B)
                    sp.wait_ge(spT_ready, 1)
                sp.dma_start(cb[:, b % 2], A["state_mlstm_c"][0, b].rearrange("h e d -> e h d")).then_inc(cs_slot[b % 2], 16)

        c_stored, sc_stored = ([sem(f"{n}{i}") for i in range(2)] for n in ("c_stored", "sc_stored"))
        cs_slot = [sem("cs_slot0"), sem("cs_slot1")]

        def act_mls_load(act):
            act.wait_ge(spT_ready, 1)
            act.dma_start(sn[:, 0], A["state_mlstm_n"][0]).then_inc(cs_in, 16)
            act.dma_start(sm[:], A["state_mlstm_m"][0]).then_inc(cs_in, 16)

        def pe_mls(pe):
            pe.wait_ge(qm_ready, 1)
            nc.tensor.matmul(pe_bank(pe, 2)[:, 0:4 * HB], ones[0:B, :], qm[:].rearrange("r q h b -> r (q h b)"),
                             start=True, stop=True).then_inc(bank_full[2], 1)
            for b in range(B):
                for i in range(2):
                    nc.tensor.matmul(pe_bank(pe, 2 + i)[:], rowsel[:, b, :], s_tok[:, 1 + i, :], start=True,
                                     stop=True).then_inc(bank_full[2 + i], 1)
            pe.wait_ge(sst_ready, 1)
            nc.tensor.matmul(pe_bank(pe, 0)[:, 0:HB], ones[:], sx[:, 1], start=True, stop=True).then_inc(bank_full[0], 1)

        def vec_mls(dve):
            v = nc.vector
            dve.wait_ge(cs_in, 32)
            li, lf = gt[0:B, NTT, 0:H], gt[0:B, NTT, H:2 * H]
            bc = lambda x: x.unsqueeze(2).to_broadcast([B, H, DH])
            heads = lambda x: x.rearrange("b (h d) -> b h d", h=H)
            q, k = heads(s_tok[:, 1]), heads(s_tok[:, 2])
            V(v.tensor_tensor(s8[:, 0], lf, sm[:], ALU.add))
            V(v.tensor_tensor(s8[:, 1], s8[:, 0], li, ALU.max), n_ready)
            V(v.tensor_tensor(s8[:, 4], s8[:, 0], s8[:, 1], ALU.subtract))
            V(v.tensor_tensor(s8[:, 5], li, s8[:, 1], ALU.subtract))
            V(v.tensor_scalar(s8[:, 6], s8[:, 1], -1.0, None, ALU.mult), sx_b)
            V(v.tensor_tensor(sn[:, 1], q, k, ALU.mult))
            V(v.tensor_reduce(s8[:, 7], sn[:, 1], AX, ALU.add))
            V(v.tensor_tensor(sn[:, 1], q, sn[:, 0], ALU.mult))
            V(v.tensor_reduce(s8[:, 8], sn[:, 1], AX, ALU.add))
            dve.wait_ge(shs_ready, 1)
            V(v.tensor_scalar(s8[:, 5], s8[:, 5], SCALE, None, ALU.mult))
            V(v.tensor_tensor(s8[:, 9], s8[:, 7], s8[:, 5], ALU.mult))
            V(v.tensor_tensor(s8[:, 10], s8[:, 8], s8[:, 4], ALU.mult))
            V(v.tensor_tensor(s8[:, 10], s8[:, 10], s8[:, 9], ALU.add))
            V(v.scalar_tensor_tensor(s8[:, 10], s8[:, 10], -1.0, s8[:, 10], ALU.mult, ALU.max))
            V(v.tensor_tensor(s8[:, 10], s8[:, 10], s8[:, 6], ALU.max))
            V(v.reciprocal(s8[:, 10], s8[:, 10]))
            V(v.tensor_tensor(s8[:, 11], s8[:, 9], s8[:, 10], ALU.mult))
            V(v.tensor_tensor(s8[:, 12], s8[:, 4], s8[:, 10], ALU.mult))
            for i, c in enumerate((4, 5, 11, 12)):
                V(v.tensor_tensor(qm[:, i], own[:], s8[:, c].unsqueeze(2).to_broadcast([B, H, B]), ALU.mult),
                  qm_ready if i == 3 else None)
            V(v.tensor_tensor(sn[:, 0], sn[:, 0], bc(s8[:, 4]), ALU.mult))
            V(v.tensor_tensor(sn[:, 1], k, bc(s8[:, 5]), ALU.mult))
            V(v.tensor_tensor(sn[:, 0], sn[:, 0], sn[:, 1], ALU.add), n_ready)
            V(v.tensor_copy(Qb[:].rearrange("p q h b -> p (q h b)"), rd_bank(dve, 2)[:, 0:4 * HB]), bank_read[2])
            vT = z_m[:, 2 * H:3 * H, SEQ:T]
            vw = sx[:, 3].rearrange("p (h b) -> p h b", h=H)
            V(v.tensor_tensor(vw, vT, Qb[:, 1], ALU.mult))
            cbc = lambda x: x.unsqueeze(2).to_broadcast([P, H, DH])
            for b in range(B):
                c = cb[:, b % 2]
                dve.wait_ge(cs_slot[b % 2], 16 * (b // 2 + 1))
                V(v.tensor_tensor(ct[:, 0], c, rd_bank(dve, 2)[:].rearrange("p (h d) -> p h d", h=H), ALU.mult), bank_read[2])
                V(v.tensor_reduce(cq[:, :, b], ct[:, 0], AX, ALU.add))
                V(v.tensor_tensor(c, c, cbc(Qb[:, 0, :, b]), ALU.mult))
                V(v.tensor_tensor(ct[:, 1], rd_bank(dve, 3)[:].rearrange("p (h d) -> p h d", h=H), cbc(vw[:, :, b]),
                                  ALU.mult), bank_read[3])
                V(v.tensor_tensor(c, c, ct[:, 1], ALU.add), sc_in)
            sh = sx[:, 0].rearrange("p (h b) -> p h b", h=H)
            V(v.tensor_tensor(cq[:], cq[:], Qb[:, 3], ALU.mult))
            V(v.tensor_tensor(sh, vT, Qb[:, 2], ALU.mult))
            V(v.tensor_tensor(sh, sh, cq[:], ALU.add))
            V(v.tensor_tensor(sx[:, 1], sx[:, 0], sx[:, 0], ALU.mult), sst_ready)
            dve.wait_ge(shs_ready, 2)
            V(v.tensor_tensor(sx[:, 0], sx[:, 0], sx[:, 2], ALU.mult))
            V(v.tensor_tensor(sh, sh, gains[:, G_ML:G_ML + H].unsqueeze(2).to_broadcast([P, H, B]), ALU.mult))
            V(v.tensor_tensor(z_m[:, 3 * H:4 * H, SEQ:T], sh, sg_s[:], ALU.mult))

        def act_mls_store(act):
            act.dma_start(O["p_n"][0, 0].rearrange("(o h) d -> o h d", o=1), nst[:]).then_inc(stores, 16)
            act.dma_start(O["p_m"][0, 0].rearrange("(h o) -> h o", o=1), rows[:, 1, SEQ - 1:SEQ]).then_inc(stores, 16)
            act.wait_ge(n_ready, 2)
            act.dma_start(O["s_m"][0], s8[:, 1]).then_inc(stores, 16)
            act.dma_start(O["s_n"][0], sn[:, 0]).then_inc(stores, 16)
            for b in range(B):
                act.wait_ge(sc_in, b + 1)
                act.dma_start(O["s_c"][0, b].rearrange("h e d -> e h d"), cb[:, b % 2]).then_inc(sc_stored[b % 2], 16)

        def y_tile(k):
            return z_m[:, 3 * H + k, :] if k < H else z_a[:, 2 * H + k - H, :]

        def act_split_y(act):
            act.wait_ge(ya_ready, 1)
            act.wait_ge(w_used[0], BASE0)
            for k in range(KT):
                S(nc.scalar.copy(ahi[:, k], y_tile(k)), y_hi)

        def vec_split_y(dve):
            for k in range(KT):
                dve.wait_ge(y_hi, k + 1)
                V(nc.vector.tensor_tensor(alo[:, k], y_tile(k), ahi[:, k].bitcast(F32), ALU.subtract), y_lo)

        def pe_mixers(pe):
            for i in range(N_ATT + 2):
                pe_att(pe, i)
            pe_satt_rows(pe)
            for b in range(B + 1):
                pe_satt_k(pe, b)
            pe_satt_soft(pe)
            for b in range(B):
                pe_satt_v(pe, b)
            pe_ml_prep(pe)
            for h in range(H):
                pe_ml(pe, h)
            pe_mls(pe)

        def act_mixers(act):
            for i in range(N_ATT + 2):
                act_att(act, i)
            for b in range(B + 1):
                act_satt_k(act, b)
            act_satt_soft(act)
            act_mls_load(act)
            act_ml_prep(act)
            for h in range(H):
                act_ml(act, h)
            act_mls_first(act)
            act_mls_store(act)
            act_mls_last(act)
            act_split_y(act)

        def act_mls_first(act):
            act.wait_ge(sx_b, 1)
            S(nc.scalar.activation(s8[:, 4:7].rearrange("b q h -> b (q h)"), s8[:, 4:7].rearrange("b q h -> b (q h)"),
                                   ACT.Exp), shs_ready)

        def act_mls_last(act):
            S(nc.scalar.activation(sx[:, 2], rd_bank(act, 0)[:, 0:HB], ACT.Ln, bias=epsc[:], scale=1.0 / DH), bank_read[0])
            S(nc.scalar.activation(sx[:, 2], sx[:, 2], ACT.Exp, scale=-0.5), shs_ready)

        def vec_mixers(dve):
            for i in range(N_ATT + 2):
                vec_att(dve, i)
            vec_satt_rows(dve)
            vec_satt_soft(dve)
            vec_satt_v(dve)
            vec_ml_prep(dve)
            for h in range(H):
                vec_ml(dve, h)
            vec_mls(dve)
            dve.sem_inc(ya_ready, 1)
            vec_split_y(dve)


        FREE = 15600
        gHi = reg("gHi", [P, NFT, T], 0, F32R)
        gLo = reg("gLo", [P, NFT, T], FREE, F32R)
        xT = reg("xT", [P, KT, T], 11440)
        qT = reg("qT", [P, KT, T], 0)
        oT = reg("oT", [P, KT, T], 4160)
        px = reg("px", [P, 2, NMEM], 9344)
        pT = reg("pT", [P, 2, SEQ], 9856)
        mem_in = reg("mem_in", [P, 2, D], FREE)
        memT = reg("memT", [P, KT, NMEM], FREE + 2048)
        hmhi = reg("hmhi", [P, KT, NMEM], FREE + 4096, F32R)
        hmlo = reg("hmlo", [P, KT, NMEM], FREE + 6144, F32R)
        ckv = reg("ckv", [P, 2, 2, D], FREE)
        prod = reg("prod", [P, 2, D], FREE + 4096)
        qs_tok = reg("qs_tok", [B, D], FREE + 6144)
        xS = reg("xS", [P, 2, H, B], FREE + 7168)
        xp = reg("xp", [HB, NMEM], FREE + 7232)
        qs = reg("qs", [P, KT, B], FREE + 7488)
        mk_t = reg("mk_t", [P, 2, D], 23792)
        mv_t = reg("mv_t", [P, 2, D], 25840)
        mkT = reg("mkT", [P, KT, NMEM], 27888)
        hs2 = reg("hs2", [P, 2, T], 29936)
        rstd2 = reg("rstd2", [P, T], 30976)
        sq2 = reg("sq2", [P, 2, T], 31496)
        rq = reg("rq", [P, 5, H], 32536)
        xc = reg("xc", [P, 16], 32560)
        hist_rows = reg("hist_rows", [2 * B, 2 * DFF], FREE)
        ub = reg("ub", [P, 2, 2 + T], 27040)
        cc = reg("cc", [P, 2, T], 28088)
        gl = reg("gl", [P, T], 29128)
        hist = reg("hist", [P, 2 * NFT, B, 2], 32704)
        ulast = reg("ulast", [P, 2 * NFT, 2 + B], 33408)
        y_tok = reg("y_tok", [P, NTT, D], 27040)
        ys_tok = reg("ys_tok", [B, D], 31136)
        conv_rows = nc.alloc_sbuf_tensor_at("conv_rows", [2 + B, 2 * DFF], F32, offset=ahi_at)

        (mix_stored, xm_in, memT_ready, ck_ss, ck_rstd, mk_ready, kn_ready, qsq_used, rq_ready,
         xa_max, xa_exp, xa_p, xa_turned, xa_done, xa_read, qs_ready, qst_ready, qsn_ready, xs_max, xs_exp, xs_p, xsT_ready,
         xs_scored, xs_used, o_ready, hist_in, u_free, c_ready, gelu_done, act_ready, g_hi, g_lo,
         up_step, y_ready, out_stores, mem_stored, h_zero) = (sem(x) for x in (
             "mix_stored xm_in memT_ready ck_ss ck_rstd mk_ready kn_ready qsq_used rq_ready "
             "xa_max xa_exp xa_p xa_turned xa_done xa_read qs_ready qst_ready qsn_ready xs_max xs_exp xs_p xsT_ready "
             "xs_scored xs_used o_ready hist_in u_free c_ready gelu_done act_ready g_hi g_lo "
             "up_step y_ready out_stores mem_stored h_zero").split())
        ckv_full = [sem("ckv_full0"), sem("ckv_full1")]

        PAIRS = [("out", 4), ("ck", 4), ("cv", 4), ("cq", 4), ("co", 4), ("up", NFT), ("down", 12)]
        BASE, at = {}, (BASE0, N_IN - BASE0)
        for stage, n in PAIRS:
            BASE[stage] = at
            at = (at[0] + n, at[1] + n)
        N_PAIRS = sum(n for _, n in PAIRS)

        def sp_stream(sp, stage, start=0):
            w = A["w_" + stage][0].rearrange("(k p) c -> p k c", p=P)
            base = BASE[stage]
            with sp.Fori(start, dict(PAIRS)[stage]) as i:
                for s in range(2):
                    sp.wait_ge(split_full[s], i + base[s])
                    col = i * P + s * DFF if stage == "up" else i * (2 * P) + s * P
                    sp.dma_start(raw[:, s], w[:, :, bass.ds(col, P)]).then_inc(raw_full[s], 16)

        def act_split(act, s, u):
            act.wait_ge(raw_full[s], (u + 1) * 16)
            act.wait_ge(w_used[s], u)
            nc.scalar.copy(whi[:, s], raw[:, s]).then_inc(hi_full[s], 1)

        def act_proj(act, stage, evac=None):
            base = BASE[stage]
            with act.Fori(0, dict(PAIRS)[stage]) as i:
                for s in range(2):
                    if evac is not None:
                        act.wait_ge(w_used[s], i + (base[s] + 1))
                        evac(i, s)
                    act_split(act, s, i + (base[s] + 1))

        def pool_split(pool, i):
            for s in range(2):
                pool.wait_ge(hi_full[s], i + (BASE["out"][s] + 1))
                nc.gpsimd.tensor_tensor(wlo[:, s], raw[:, s], whi[:, s].bitcast(F32), ALU.subtract).then_inc(split_full[s], 1)

        def pe_proj(pe, stage, after=None):
            base = BASE[stage]
            with pe.Fori(0, dict(PAIRS)[stage]) as i:
                for s in range(2):
                    pe.wait_ge(split_full[s], i + (base[s] + 1))
                    pe.wait_ge(out_free[s], i + base[s])
                    if stage in ("ck", "cv"):
                        for mt in range(2):
                            for k in range(KT):
                                for j, (x, w) in enumerate(((hmhi, whi), (hmlo, whi), (hmhi, wlo))):
                                    m = nc.tensor.matmul(PJ[s][:, mt, 0:P], x[:, k, mt * P:(mt + 1) * P], w[:, s, k, :],
                                                         start=(k == 0 and j == 0), stop=(k == KT - 1 and j == 2))
                        m.then_inc(w_used[s], 1)
                    else:
                        pe_product(s, PJ[s], P, KT, ahi, alo).then_inc(w_used[s], 1)
                if after is not None:
                    after(i)

        def vec_residual(dve, stage):
            base = BASE[stage]
            with dve.Fori(0, dict(PAIRS)[stage]) as i:
                for s in range(2):
                    dve.wait_ge(w_used[s], i + (base[s] + 1))
                    x = xT[:, bass.ds(i * 2 + s, 1), :].rearrange("p o (a b) -> p (o a) b", a=2)
                    nc.vector.tensor_tensor(x, x, PJ[s][:, :, 0:HALF], ALU.add).then_inc(out_free[s], 1)

        def stage_done(eng, stage, sems_):
            for s in range(2):
                eng.wait_ge(sems_[s], BASE[stage][s] + dict(PAIRS)[stage])

        def act_norm(act, stage, src, width, hi):
            for k in range(KT):
                act.wait_ge(sq_used, KT * stage + k - 1 if k >= 2 else KT * stage)
                nc.scalar.activation(sq2[:, k % 2, 0:width], src[:, k, 0:width], ACT.Square).then_inc(sq_ready, 1)
            act_rstd(act, stage, rstd2, width, D)
            for k in range(KT):
                act.wait_ge(hs_ready, KT * stage + k + 1)
                nc.scalar.copy(hi[:, k, 0:width], hs2[:, k % 2, 0:width]).then_inc(nhi_ready, 1)

        def pe_turn_in(pe):
            pe.wait_ge(xm_in, 16 * 6)
            for k in range(KT):
                bank = pe_bank(pe, 2 + k % 2)
                for mt in range(2):
                    m = nc.tensor.transpose(bank[:, mt * P:(mt + 1) * P], mem_in[:, mt, k * P:(k + 1) * P], ident[:])
                m.then_inc(bank_full[2 + k % 2], 1)
            for k in range(KT):
                bank = pe_bank(pe, 2 + k % 2)
                for tt in range(NTT):
                    m = nc.tensor.transpose(bank[:, tt * P:(tt + 1) * P], x_in[:, tt, k * P:(k + 1) * P], ident[:])
                m.then_inc(bank_full[2 + k % 2], 1)
            bank = pe_bank(pe, 2)
            for k in range(KT):
                m = nc.tensor.transpose(bank[:, k * B:(k + 1) * B], xs_in[:, k * P:(k + 1) * P], ident[0:B, 0:B])
            m.then_inc(bank_full[2], 1)
            for k in range(KT):
                pe_sumsq(pe, 1, k, sq2, NMEM)

        def vec_turn_in(dve):
            v = nc.vector
            dve.wait_ge(mix_stored, 1)
            for k in range(KT):
                V(v.tensor_copy(memT[:, k], rd_bank(dve, 2 + k % 2)[:, 0:NMEM]), bank_read[2 + k % 2])
                dve.sem_inc(memT_ready, 1)
            for k in range(KT):
                V(v.tensor_copy(xT[:, k, 0:SEQ], rd_bank(dve, 2 + k % 2)), bank_read[2 + k % 2])
            V(v.tensor_copy(xT[:, :, SEQ:T], rd_bank(dve, 2)[:, 0:KT * B].rearrange("p (k b) -> p k b", k=KT)), bank_read[2])

        def vec_mem_keys(dve):
            v = nc.vector
            stage_done(dve, "ck", out_free)
            k4 = mk_t[:].rearrange("p t (h d) -> p (t h) d", h=H)
            q4 = mem_in[:].rearrange("p t (h d) -> p (t h) d", h=H)
            V(v.tensor_tensor(q4, k4, k4, ALU.mult))
            V(v.tensor_reduce(xc[:, 0:8], q4, AX, ALU.add), ck_ss)
            dve.wait_ge(ck_rstd, 1)
            V(v.tensor_tensor(k4, k4, xc[:, 0:8].unsqueeze(2).to_broadcast([P, 8, 2 * DH]), ALU.mult))
            V(v.tensor_tensor(k4, k4, ckg[:].unsqueeze(1).to_broadcast([P, 8, 2 * DH]), ALU.mult), mk_ready)
            for f in range(KT):
                V(v.tensor_scalar(mkT[:, f], rd_bank(dve, 2 + f % 2)[:, 0:NMEM], gains[:, G_CQ + f % 2:G_CQ + f % 2 + 1], None,
                                  ALU.mult), bank_read[2 + f % 2])
                dve.sem_inc(kn_ready, 1)

        def act_mem_keys(act):
            act.wait_ge(ck_ss, 1)
            S(nc.scalar.activation(xc[:, 0:8], xc[:, 0:8], ACT.Ln, bias=epsc[:], scale=1.0 / (2 * DH)))
            S(nc.scalar.activation(xc[:, 0:8], xc[:, 0:8], ACT.Exp, scale=-0.5), ck_rstd)

        def pe_mem_keys(pe):
            pe.wait_ge(mk_ready, 1)
            for f in range(KT):
                bank = pe_bank(pe, 2 + f % 2)
                for mt in range(2):
                    m = nc.tensor.transpose(bank[:, mt * P:(mt + 1) * P], mk_t[:, mt, f * P:(f + 1) * P], ident[:])
                m.then_inc(bank_full[2 + f % 2], 1)

        def act_query(act):
            def evac(i, s):
                nc.scalar.copy(qT[:, bass.ds(i * 2 + s, 1), :].rearrange("p o (a b) -> p (o a) b", a=2), PJ[s][:, :, 0:HALF])
                act.wait_ge(qsq_used, i)
                nc.scalar.activation(sq2[:, s].rearrange("p (a b) -> p a b", a=2), PJ[s][:, :, 0:HALF],
                                     ACT.Square).then_inc(out_free[s], 1)
            act_proj(act, "cq", evac)
            bank = rd_bank(act, 0)
            r = rq[:].rearrange("p t h -> p (t h)")
            for w, a, b in ((P, 0, NTT * H), (B, NTT * H, (NTT + 1) * H)):
                S(nc.scalar.activation(r[0:w, a:b], bank[0:w, a:b], ACT.Ln, bias=epsc[0:w], scale=1.0 / (2 * DH)),
                  bank_read[0] if w == B else None)
                S(nc.scalar.activation(r[0:w, a:b], r[0:w, a:b], ACT.Exp, scale=-0.5))
            act.sem_inc(rq_ready, 1)

        def pe_query(pe):
            bank = pe_bank(pe, 0)

            def sums(i):
                for s in range(2):
                    pe.wait_ge(out_free[s], i + (BASE["cq"][s] + 1))
                for tt in range(NTT + 1):
                    w = P if tt < NTT else B
                    for dh in range(2):
                        m = nc.tensor.matmul(bank[0:w, bass.ds(i + tt * H, 1)], sq2[:, dh, tt * P:tt * P + w], ones[:, 0:1],
                                             start=(dh == 0), stop=(dh == 1))
                m.then_inc(qsq_used, 1)
            pe_proj(pe, "cq", sums)
            pe.wait_ge(qsq_used, H)
            pe.sem_inc(bank_full[0], 1)

        def vec_query(dve):
            dve.wait_ge(rq_ready, 1)
            V(nc.vector.tensor_scalar(rq[:, 0:NTT], rq[:, 0:NTT], SCALE_C, None, ALU.mult))
            V(nc.vector.tensor_scalar(rq[0:B, NTT], rq[0:B, NTT], SCALE_C, None, ALU.mult))

        def xcol(j, c):
            return xc[:, 4 * (j % 2) + c:4 * (j % 2) + c + 1]

        def pe_cross(pe, i):
            if i < N_ATT:
                h, qt = divmod(i, NTT)
                if i == 0:
                    pe.wait_ge(kn_ready, KT)
                bank = pe_bank(pe, 2 + i % 2)
                for dh in range(2):
                    m = nc.tensor.matmul(bank[:, 0:NMEM], qT[:, 2 * h + dh, qt * P:(qt + 1) * P], mkT[:, 2 * h + dh, :],
                                         start=(dh == 0), stop=(dh == 1))
                m.then_inc(bank_full[2 + i % 2], 1)
            if 0 <= i - 1 < N_ATT:
                j = i - 1
                pe.wait_ge(xa_p, j + 1)
                bank = pe_bank(pe, 0)
                for mt in range(2):
                    m = nc.tensor.transpose(bank[:, mt * P:(mt + 1) * P], px[:, j % 2, mt * P:(mt + 1) * P], ident[:])
                m.then_inc(bank_full[0], 1)
            if i >= 2 and (i - 2) % NTT == NTT - 1:
                h = (i - 2) // NTT
                pe.wait_ge(xa_turned, i - 1)
                if h >= 2:
                    pe.wait_ge(xa_read, h - 1)
                for dh in range(2):
                    for mt in range(2):
                        c = (2 * h + dh) * P
                        m = nc.tensor.matmul(PJ[h % 2][:, dh, :], mv_t[:, mt, c:c + P], pT[:, mt, :], start=(mt == 0),
                                             stop=(mt == 1))
                m.then_inc(xa_done, 1)

        def act_cross(act, i):
            if i < N_ATT:
                act.wait_ge(xa_max, i + 1)
                S(nc.scalar.activation(px[:, i % 2], px[:, i % 2], ACT.Exp, bias=xcol(i, 1), accum_out=xcol(i, 2)), xa_exp)
            if i >= 2 and (i - 2) % NTT == NTT - 1:
                h = (i - 2) // NTT
                act.wait_ge(xa_done, h + 1)
                S(nc.scalar.copy(oT[:, 2 * h:2 * h + 2, 0:SEQ], PJ[h % 2]), xa_read)
            if 0 <= i - 1 < N_ATT:
                j = i - 1
                qt = j % NTT
                bank = rd_bank(act, 0)
                S(nc.scalar.copy(pT[:, :, qt * P:(qt + 1) * P], bank[:, 0:NMEM].rearrange("p (t q) -> p t q", t=2)), bank_read[0])
                act.sem_inc(xa_turned, 1)

        def vec_cross(dve, i):
            v = nc.vector
            if i < N_ATT:
                h, qt = divmod(i, NTT)
                bank = rd_bank(dve, 2 + i % 2)
                if i >= 2:
                    dve.wait_ge(xa_turned, i - 1)
                V(v.tensor_scalar(px[:, i % 2], bank[:, 0:NMEM], rq[:, qt, h:h + 1], None, ALU.mult), bank_read[2 + i % 2])
                V(v.tensor_reduce(xcol(i, 0), px[:, i % 2], AX, ALU.max))
                V(v.tensor_scalar(xcol(i, 1), xcol(i, 0), -1.0, None, ALU.mult), xa_max)
            if 0 <= i - 1 < N_ATT:
                j = i - 1
                dve.wait_ge(xa_exp, j + 1)
                V(v.reciprocal(xcol(j, 3), xcol(j, 2)))
                V(v.tensor_scalar(px[:, j % 2], px[:, j % 2], xcol(j, 3), None, ALU.mult), xa_p)

        def sp_cache(sp):
            for i, name in enumerate(("cache_mem_k", "cache_mem_v")):
                for b in range(B):
                    if i == 0 and b < 2:
                        stage_done(sp, "cv", w_used)
                        sp.wait_ge(mk_ready, 1)
                    else:
                        sp.wait_ge((xs_scored, xs_used)[0 if i == 0 or b < 2 else 1],
                                   b - 1 if i == 0 or b >= 2 else B - 1 + b)
                    sp.dma_start(ckv[:, b % 2], A[name][0, b].rearrange("(t p) h d -> p t (h d)", p=P)).then_inc(
                        ckv_full[b % 2], 16)

        def vec_sample_q(dve):
            v = nc.vector
            V(v.tensor_tensor(qs[:].rearrange("p (h a) b -> p h a b", a=2), qT[:, :, SEQ:T].rearrange("p (h a) b -> p h a b", a=2),
                              gains[:, G_CQ:G_CQ + 2].unsqueeze(1).unsqueeze(3).to_broadcast([P, H, 2, B]), ALU.mult), qs_ready)
            dve.wait_ge(qst_ready, 1)
            q = qs_tok[:].rearrange("b (h d) -> b h d", h=H)
            V(v.tensor_tensor(q, q, rq[0:B, NTT].unsqueeze(2).to_broadcast([B, H, 2 * DH]), ALU.mult), qsn_ready)

        def pe_sample_q(pe):
            pe.wait_ge(qs_ready, 1)
            for i in range(2):
                bank = pe_bank(pe, i)
                for k in range(4):
                    m = nc.tensor.transpose(bank[0:B, k * P:(k + 1) * P], qs[:, 4 * i + k, :], ident[:])
                m.then_inc(bank_full[i], 1)
            pe.wait_ge(qsn_ready, 1)

        def act_sample_q(act):
            for i in range(2):
                S(nc.scalar.copy(qs_tok[:, i * SEQ:(i + 1) * SEQ], rd_bank(act, i)[0:B, :]), bank_read[i])
            act.sem_inc(qst_ready, 1)

        def pe_sample_k(pe, b):
            for i in range(2):
                nc.tensor.matmul(pe_bank(pe, 2 + i)[:], rowsel[:, b, :], qs_tok[:, i * SEQ:(i + 1) * SEQ], start=True,
                                 stop=True).then_inc(bank_full[2 + i], 1)

        def vec_sample_k(dve, b):
            v = nc.vector
            dve.wait_ge(ckv_full[b % 2], 16 * (b // 2 + 1))
            for i in range(2):
                V(v.tensor_tensor(prod[:, :, i * SEQ:(i + 1) * SEQ], ckv[:, b % 2, :, i * SEQ:(i + 1) * SEQ],
                                  rd_bank(dve, 2 + i).unsqueeze(1).to_broadcast([P, 2, SEQ]), ALU.mult), bank_read[2 + i])
            dve.sem_inc(xs_scored, 1)
            V(v.tensor_reduce(xS[:, :, :, b], prod[:].rearrange("p t (h d) -> p t h d", h=H), AX, ALU.add),
              qs_ready if b == B - 1 else None)

        def pe_sample_soft(pe):
            pe.wait_ge(qs_ready, 2)
            bank = pe_bank(pe, 2)
            for t in range(2):
                m = nc.tensor.transpose(bank[0:HB, t * P:(t + 1) * P], xS[:, t].rearrange("p h b -> p (h b)"), ident[:])
            m.then_inc(bank_full[2], 1)
            pe.wait_ge(xs_p, 1)
            bank = pe_bank(pe, 3)
            for t in range(2):
                m = nc.tensor.transpose(bank[:, t * HB:(t + 1) * HB], xp[:, t * P:(t + 1) * P], ident[0:HB, 0:HB])
            m.then_inc(bank_full[3], 1)

        def vec_sample_soft(dve):
            v = nc.vector
            V(v.tensor_copy(xp[:], rd_bank(dve, 2)[0:HB, 0:NMEM]), bank_read[2])
            V(v.tensor_reduce(xc[0:HB, 8:9], xp[:], AX, ALU.max))
            V(v.tensor_scalar(xc[0:HB, 9:10], xc[0:HB, 8:9], -1.0, None, ALU.mult), xs_max)
            dve.wait_ge(xs_exp, 1)
            V(v.reciprocal(xc[0:HB, 11:12], xc[0:HB, 10:11]))
            V(v.tensor_scalar(xp[:], xp[:], xc[0:HB, 11:12], None, ALU.mult), xs_p)
            V(v.tensor_copy(xS[:].rearrange("p t h b -> p (t h b)"), rd_bank(dve, 3)[:, 0:2 * HB]), bank_read[3])
            dve.sem_inc(xsT_ready, 1)

        def act_sample_soft(act):
            act.wait_ge(xs_max, 1)
            S(nc.scalar.activation(xp[:], xp[:], ACT.Exp, bias=xc[0:HB, 9:10], accum_out=xc[0:HB, 10:11]), xs_exp)

        def pe_sample_v(pe, b):
            if b == 0:
                pe.wait_ge(xsT_ready, 1)
            bank = pe_bank(pe, 2) if b == 0 else BANKS[2]
            pe.wait_ge(ckv_full[b % 2], 16 * (B // 2 + b // 2 + 1))
            for f in range(KT):
                for t in range(2):
                    j = f * B + b
                    m = nc.tensor.matmul(bank[:, j:j + 1], ckv[:, b % 2, t, f * P:(f + 1) * P], xS[:, t, f // 2, b:b + 1],
                                         start=(t == 0), stop=(t == 1))
            m.then_inc(xs_used, 1)

        def vec_sample_v(dve):
            dve.wait_ge(xs_used, B)
            V(nc.vector.tensor_copy(oT[:, :, SEQ:T], BANKS[2][:, 0:KT * B].rearrange("p (k b) -> p k b", k=KT)), bank_read[2])
            dve.sem_inc(o_ready, 1)

        def act_split_o(act):
            act.wait_ge(o_ready, 1)
            for k in range(KT):
                S(nc.scalar.copy(ahi[:, k], oT[:, k]), y_hi)

        def vec_split_o(dve):
            for k in range(KT):
                dve.wait_ge(y_hi, KT + k + 1)
                V(nc.vector.tensor_tensor(alo[:, k], oT[:, k], ahi[:, k].bitcast(F32), ALU.subtract), y_lo)

        def pe_hist(pe):
            pe.wait_ge(hist_in, 16)
            for i in range(2):
                bank = pe_bank(pe, 2 + i)
                for f in range(NFT):
                    m = nc.tensor.transpose(bank[:, f * 2 * B:(f + 1) * 2 * B],
                                            hist_rows[:, (i * NFT + f) * P:(i * NFT + f + 1) * P], ident[0:2 * B, 0:2 * B])
                m.then_inc(bank_full[2 + i], 1)

        def vec_hist(dve):
            for i in range(2):
                V(nc.vector.tensor_copy(hist[:, i * NFT:(i + 1) * NFT].rearrange("p f b j -> p (f b j)"),
                                        rd_bank(dve, 2 + i)[:, 0:NFT * 2 * B]), bank_read[2 + i])
            stage_done(dve, "co", w_used)
            V(nc.vector.memset(ub[:, :, 0:2], 0.0), h_zero)

        UP_STEPS = 16

        def act_up(act):
            base = BASE["up"]
            nc.scalar.preload_act_table_set("gelu_apprx_tanh_and_others")
            with act.Fori(0, NFT) as i:
                for s in range(2):
                    act.wait_ge(w_used[s], i + (base[s] + 1))
                    act.wait_ge(u_free, i * 2 + s)
                    nc.scalar.copy(ub[:, s, 2:2 + T].rearrange("p (a b) -> p a b", a=2), PJ[s][:, :, 0:HALF]).then_inc(out_free[s], 1)
                    act_split(act, s, i + (base[s] + 1))
                act.wait_ge(c_ready, i * 2 + 2)
                nc.scalar.activation(gl[:], cc[:, 1], ACT.Gelu_apprx_tanh).then_inc(gelu_done, 1)
                act.wait_ge(act_ready, i + 1)
                nc.scalar.copy(gHi[:, bass.ds(i, 1), :], gl[:].unsqueeze(1)).then_inc(g_hi, 1)

        def vec_up(dve):
            v = nc.vector
            base = BASE["up"]
            with dve.Fori(0, NFT) as i:
                n = [0]

                def step(ins, s=None):
                    n[0] += 1
                    ins.then_inc(up_step, 1)
                    dve.wait_ge(up_step, i * UP_STEPS + n[0])
                    if s is not None:
                        dve.sem_inc(s, 1)

                for s in range(2):
                    f = i + s * NFT
                    c = cc[:, s]
                    col = lambda j: cw[:, j, bass.ds(f, 1)]
                    dve.wait_ge(out_free[s], i + (base[s] + 1))
                    step(v.tensor_scalar(c, ub[:, s, 2:2 + T], col(2), gains[:, bass.ds(G_CB + f, 1)], ALU.mult, ALU.add))
                    step(v.scalar_tensor_tensor(c[:, 0:SEQ], ub[:, s, 1:1 + SEQ], col(1), c[:, 0:SEQ], ALU.mult, ALU.add))
                    step(v.scalar_tensor_tensor(c[:, 0:SEQ], ub[:, s, 0:SEQ], col(0), c[:, 0:SEQ], ALU.mult, ALU.add))
                    for j in (1, 0):
                        h = hist[:, bass.ds(f, 1), :, j].rearrange("p o b -> p (o b)")
                        step(v.scalar_tensor_tensor(c[:, SEQ:T], h, col(j), c[:, SEQ:T], ALU.mult, ALU.add))
                    step(v.tensor_copy(ulast[:, bass.ds(f, 1), :], ub[:, s, SEQ:2 + T].unsqueeze(1)), u_free)
                    dve.sem_inc(c_ready, 1)
                dve.wait_ge(gelu_done, i + 1)
                step(v.tensor_tensor(gl[:], gl[:], cc[:, 0], ALU.mult), act_ready)
                dve.wait_ge(g_hi, i + 1)
                step(v.tensor_tensor(gLo[:, bass.ds(i, 1), :], gl[:].unsqueeze(1), gHi[:, bass.ds(i, 1), :].bitcast(F32),
                                     ALU.subtract))
                while n[0] < UP_STEPS:
                    n[0] += 1
                    dve.sem_inc(up_step, 1)
                dve.sem_inc(g_lo, 1)

        def pe_last(pe):
            pe.wait_ge(g_lo, NFT)
            for i in range(2 * NFT // 4):
                bank = pe_bank(pe, i % 2)
                for f in range(4):
                    m = nc.tensor.transpose(bank[0:2 + B, f * P:(f + 1) * P], ulast[:, 4 * i + f, :], ident[:])
                m.then_inc(bank_full[i % 2], 1)

        def act_last(act):
            stage_done(act, "up", w_used)
            for i in range(2 * NFT // 4):
                S(nc.scalar.copy(conv_rows[:, i * SEQ:(i + 1) * SEQ], rd_bank(act, i % 2)[0:2 + B, :]), bank_read[i % 2])
            act.dma_start(O["p_conv"][0, 0], conv_rows[0:2]).then_inc(out_stores, 16)
            act.dma_start(O["s_conv"][0, :, 1], conv_rows[2:2 + B]).then_inc(out_stores, 16)

        THIRDS = ((0, 8), (8, 7), (15, 7))

        def sp_down(sp):
            w = A["w_down"][0].rearrange("(k p) c -> p k c", p=P)
            base = BASE["down"]
            with sp.Fori(0, KT // 2) as i:
                for j in range(6):
                    s, (k0, kn) = j % 2, THIRDS[j % 3]
                    sp.wait_ge(split_full[s], i * 3 + (base[s] + j // 2))
                    sp.dma_start(raw[:, s, 0:kn], w[:, k0:k0 + kn, bass.ds(i * (2 * P) + (j // 3) * P, P)]).then_inc(raw_full[s], 16)

        def act_down(act):
            base = BASE["down"]
            with act.Fori(0, 11) as i:
                for s in range(2):
                    act_split(act, s, i + (base[s] + 1))

        def pe_down(pe):
            base = BASE["down"]
            with pe.Fori(0, KT // 2) as i:
                for j in range(6):
                    s, (k0, kn), o = j % 2, THIRDS[j % 3], j // 3
                    pe.wait_ge(split_full[s], i * 3 + (base[s] + j // 2 + 1))
                    if j % 3 == 0:
                        pe.wait_ge(out_free[o], i + base[o])
                    pe_product(s, PJ[o], P, kn, gHi, gLo, first=(j % 3 == 0), last=(j % 3 == 2), k0=k0).then_inc(w_used[s], 1)

        def vec_down(dve):
            base = BASE["down"]
            with dve.Fori(0, KT // 2) as i:
                for o in range(2):
                    dve.wait_ge(w_used[o], i * 3 + (base[o] + 2 + o))
                    x = xT[:, bass.ds(i * 2 + o, 1), :].rearrange("p a (c b) -> p (a c) b", c=2)
                    nc.vector.tensor_tensor(x, x, PJ[o][:, :, 0:HALF], ALU.add).then_inc(out_free[o], 1)

        def pe_out(pe):
            for o in range(2):
                pe.wait_ge(out_free[o], BASE["down"][o] + KT // 2)
            for k in range(KT):
                bank = pe_bank(pe, k % 2)
                for tt in range(NTT):
                    m = nc.tensor.transpose(bank[:, tt * P:(tt + 1) * P], xT[:, k, tt * P:(tt + 1) * P], ident[:])
                m.then_inc(bank_full[k % 2], 1)
            for i in range(2):
                bank = pe_bank(pe, 2 + i)
                for k in range(4):
                    m = nc.tensor.transpose(bank[0:B, k * P:(k + 1) * P], xT[:, 4 * i + k, SEQ:T], ident[:])
                m.then_inc(bank_full[2 + i], 1)

        def act_out(act):
            act.wait_ge(g_lo, NFT)
            for k in range(KT):
                S(nc.scalar.copy(y_tok[:, :, k * P:(k + 1) * P], rd_bank(act, k % 2)[:].rearrange("p (t f) -> p t f", t=NTT)),
                  bank_read[k % 2])
                if k % 4 == 3:
                    act.dma_start(O["y_prompt"][0].rearrange("(t p) d -> p t d", p=P)[:, :, (k - 3) * P:(k + 1) * P],
                                  y_tok[:, :, (k - 3) * P:(k + 1) * P]).then_inc(out_stores, 16)
            act.wait_ge(y_ready, 1)
            act.dma_start(O["y_sample"][:, 0], ys_tok[:]).then_inc(out_stores, 16)

        def vec_out(dve):
            for i in range(2):
                V(nc.vector.tensor_copy(ys_tok[:, i * SEQ:(i + 1) * SEQ], rd_bank(dve, 2 + i)[0:B, :]), bank_read[2 + i])
            dve.sem_inc(y_ready, 1)

        def sync_tail(sp):
            w = A["w_out"][0].rearrange("(k p) c -> p k c", p=P)
            for s in range(2):
                sp.wait_ge(split_full[s], BASE["out"][s])
                sp.dma_start(raw[:, s], w[:, :, s * P:(s + 1) * P]).then_inc(raw_full[s], 16)
            sync_mls(sp)
            sp.wait_ge(mix_stored, 1)
            sp.wait_ge(y_lo, KT)
            sp.dma_start(mem_in[:], A["mem_prompt"][0].rearrange("(t p) d -> p t d", p=P)).then_inc(xm_in, 16)
            for t in range(NTT):
                sp.dma_start(x_in[:, t, :], A["x_prompt"][0, t * P:(t + 1) * P, :]).then_inc(xm_in, 16)
            sp.dma_start(xs_in[:], A["x_sample"][:, 0, :]).then_inc(xm_in, 16)
            sp_stream(sp, "out", 1)
            for stage in ("ck", "cv", "cq"):
                sp_stream(sp, stage)
            for s in range(2):
                sp.wait_ge(split_full[s], BASE["co"][s])
                sp.dma_start(raw[:, s], A["w_co"][0].rearrange("(k p) c -> p k c", p=P)[:, :, s * P:(s + 1) * P]).then_inc(
                    raw_full[s], 16)
            sp_cache(sp)
            sp.wait_ge(xs_used, B)
            sp.wait_ge(o_ready, 1)
            sp.wait_ge(mem_stored, 32)
            sp.dma_start(hist_rows[:], A["state_conv"][0].rearrange("b j c -> (b j) c")).then_inc(hist_in, 16)
            sp.dma_start(O["s_conv"][0, :, 0], A["state_conv"][0, :, 1]).then_inc(out_stores, 16)
            sp_stream(sp, "co", 1)
            sp_stream(sp, "up")
            sp_down(sp)

        def pool_tail(pool):
            pool_split(pool, 0)
            pool_satt(pool)
            with pool.Fori(1, N_PAIRS) as i:
                pool_split(pool, i)

        def act_tail(act):
            for s in range(2):
                act_split(act, s, BASE["out"][s])
            act_mixers(act)
            act.wait_ge(stores, 16 * 8)
            act.wait_ge(sv_stored, 16)
            for i in range(2):
                act.wait_ge(rt_stored[i], 32)
                act.wait_ge(c_stored[i], 16 * (H // 2))
                act.wait_ge(sc_stored[i], 16 * (B // 2))
            act.sem_inc(mix_stored, 1)
            for k in range(KT):
                act.wait_ge(memT_ready, k + 1)
                act.wait_ge(sq_used, KT + max(k - 1, 0))
                nc.scalar.activation(sq2[:, k % 2, 0:NMEM], memT[:, k], ACT.Square).then_inc(sq_ready, 1)
            act_rstd(act, 1, rstd2, NMEM, D)
            for k in range(KT):
                act.wait_ge(hs_ready, KT + k + 1)
                nc.scalar.copy(hmhi[:, k], hs2[:, k % 2, 0:NMEM]).then_inc(nhi_ready, 1)
            act_proj(act, "out")
            stage_done(act, "out", out_free)
            act_norm(act, 2, xT, T, ahi)
            act_proj(act, "ck", lambda i, s: nc.scalar.copy(
                mk_t[:, :, bass.ds(i * (2 * P) + s * P, P)], PJ[s][:, :, 0:P]).then_inc(out_free[s], 1))
            act_proj(act, "cv", lambda i, s: nc.scalar.copy(
                mv_t[:, :, bass.ds(i * (2 * P) + s * P, P)], PJ[s][:, :, 0:P]).then_inc(out_free[s], 1))
            act_mem_keys(act)
            act.wait_ge(mk_ready, 1)
            stage_done(act, "cv", out_free)
            for name, t in (("p_mem_k", mk_t), ("p_mem_v", mv_t)):
                act.dma_start(O[name][0, 0].rearrange("(t p) h d -> p t (h d)", p=P), t[:]).then_inc(mem_stored, 16)
            act_query(act)
            for i in range(N_ATT + 2):
                act_cross(act, i)
            act_sample_q(act)
            act_sample_soft(act)
            act_split_o(act)
            act_proj(act, "co")
            stage_done(act, "co", out_free)
            act_norm(act, 3, xT, T, ahi)
            act.wait_ge(h_zero, 1)
            act_up(act)
            act_last(act)
            act_down(act)
            act_out(act)
            act.wait_ge(mem_stored, 32)
            act.wait_ge(out_stores, 16 * 6)

        def vec_tail(dve):
            vec_mixers(dve)
            vec_turn_in(dve)
            vec_norm(dve, 1, memT, rstd2, G_MEM, hs2, NMEM, (hmhi, hmlo))
            vec_residual(dve, "out")
            vec_norm(dve, 2, xT, rstd2, G_CROSS, hs2, T)
            vec_mem_keys(dve)
            vec_query(dve)
            for i in range(N_ATT + 2):
                vec_cross(dve, i)
            vec_sample_q(dve)
            for b in range(B):
                vec_sample_k(dve, b)
            vec_sample_soft(dve)
            vec_sample_v(dve)
            vec_split_o(dve)
            vec_residual(dve, "co")
            vec_hist(dve)
            vec_norm(dve, 3, xT, rstd2, G_FFN, hs2, T)
            vec_up(dve)
            vec_down(dve)
            vec_out(dve)

        def pe_tail(pe):
            pe_mixers(pe)
            pe_turn_in(pe)
            pe.wait_ge(y_lo, KT)
            pe_proj(pe, "out")
            for k in range(KT):
                pe_sumsq(pe, 2, k, sq2, T)
            pe.wait_ge(nlo_ready, 2 * KT)
            pe_proj(pe, "ck")
            pe_proj(pe, "cv")
            pe_mem_keys(pe)
            pe.wait_ge(nlo_ready, 3 * KT)
            pe_query(pe)
            for i in range(N_ATT + 2):
                pe_cross(pe, i)
            pe_sample_q(pe)
            for b in range(B):
                pe_sample_k(pe, b)
            pe_sample_soft(pe)
            for b in range(B):
                pe_sample_v(pe, b)
            pe.wait_ge(y_lo, 2 * KT)
            pe_proj(pe, "co")
            pe_hist(pe)
            for k in range(KT):
                pe_sumsq(pe, 3, k, sq2, T)
            pe.wait_ge(nlo_ready, 4 * KT)
            pe_proj(pe, "up")
            pe_last(pe)
            pe_down(pe)
            pe_out(pe)
        block = ctx.enter_context(nc.Block())

        @block.sync
        def _(sp):
            for t in range(NTT):
                sp.dma_start(x_in[:, t, :], A["x_prompt"][0, t * P:(t + 1) * P, :]).then_inc(x_in_s, 16)
            sp.dma_start(xs_in[:], A["x_sample"][:, 0, :]).then_inc(x_in_s, 16)
            w_in = A["w_in"][0].rearrange("(k p) c -> p k c", p=P)
            for n, (name, col) in enumerate(IN_TILES):
                s, u = uses(n)
                if u:
                    sp.wait_ge(split_full[s], u)
                if name == "ikw":
                    w = C_IQ + H * D_IDX
                    sp.dma_start(raw[:, s, :, 0:D_IDX + H], w_in[:, :, w:w + D_IDX + H]).then_inc(gates_in, 16)
                    sp.dma_start(raw[:, s, :, D_IDX + H:D_IDX + 3 * H], w_in[:, :, C_G:C_G + 2 * H]).then_inc(gates_in, 16)
                    sp.wait_ge(gates_in, 32)
                    sp.sem_inc(raw_full[s], 16)
                else:
                    sp.dma_start(raw[:, s], w_in[:, :, col:col + P]).then_inc(raw_full[s], 16)
            sync_tail(sp)

        @block.gpsimd
        def _(pool):
            g = nc.gpsimd
            made = [0]

            def made_by(ins):
                made[0] += 1
                ins.then_inc(consts_made, 1)
                pool.wait_ge(consts_made, made[0])

            for t, v in ((ident, 0.0), (ones, 1.0), (tri, 1.0), (negm, 0.0), (posm, 0.0), (rowsel, 1.0), (own, 1.0),
                         (gt, 0.0), (epsc, EPS)):
                made_by(g.memset(t[:], v))
            made_by(g.affine_select(out=ident[:], in_=ident[:], compare_op=ALU.not_equal, fill=1.0, base=0,
                                    pattern=[[-1, P]], channel_multiplier=1))
            made_by(g.affine_select(out=tri[:], in_=tri[:], compare_op=ALU.is_ge, fill=0.0, base=0,
                                    pattern=[[1, P]], channel_multiplier=-1))
            made_by(g.affine_select(out=negm[:], in_=negm[:], compare_op=ALU.is_ge, fill=NEG, base=0,
                                    pattern=[[-1, P]], channel_multiplier=1))
            made_by(g.affine_select(out=posm[:], in_=posm[:], compare_op=ALU.is_ge, fill=-NEG, base=0,
                                    pattern=[[1, P]], channel_multiplier=-1))
            made_by(g.affine_select(out=rowsel[:], in_=rowsel[:], compare_op=ALU.is_equal, fill=0.0, base=0,
                                    pattern=[[-1, B], [0, P]], channel_multiplier=1))
            made_by(g.affine_select(out=own[:], in_=own[:], compare_op=ALU.is_equal, fill=0.0, base=0,
                                    pattern=[[0, H], [-1, B]], channel_multiplier=1))
            for n in range(N_IN):
                s, u = uses(n)
                w = D_IDX + 3 * H if n == 2 else P
                pool.wait_ge(hi_full[s], u + 1)
                g.tensor_tensor(wlo[:, s, :, 0:w], raw[:, s, :, 0:w], whi[:, s, :, 0:w].bitcast(F32),
                                ALU.subtract).then_inc(split_full[s], 1)
                pool_hooks(pool, n)
            pool_tail(pool)

        @block.scalar
        def _(act):
            a = nc.scalar
            a.preload_act_table_set("natural_log_exp_and_others")
            for dst, src in (
                    (rope_m[:], A["rope_main"][0:SEQ].rearrange("(t p) a b -> p t a b", p=P)),
                    (rope_ms[:], A["rope_main"][SEQ:T]),
                    (rope_i[:], A["rope_index"][0:SEQ].rearrange("(t p) a b -> p t a b", p=P)),
                    (rope_is[:], A["rope_index"][SEQ:T]),
                    (vecs[G_MIX:G_MIX + 8], A["norm_mix"].rearrange("o (a b) -> (o a) b", b=P)),
                    (vecs[G_CROSS:G_CROSS + 8], A["norm_cross"].rearrange("o (a b) -> (o a) b", b=P)),
                    (vecs[G_MEM:G_MEM + 8], A["norm_mem"].rearrange("o (a b) -> (o a) b", b=P)),
                    (vecs[G_FFN:G_FFN + 8], A["norm_ffn"].rearrange("o (a b) -> (o a) b", b=P)),
                    (vecs[G_CQ:G_CQ + 2], A["cq_norm"].rearrange("o (a b) -> (o a) b", b=P)),
                    (vecs[G_ML:G_ML + 4], A["mlstm_norm"].rearrange("o (a b) -> (o a) b", b=P)),
                    (vecs[G_CB:G_CB + 44], A["conv_b"].rearrange("o (a b) -> (o a) b", b=P)),
                    (cwrows[:], A["conv_w"][0].rearrange("j (a b) -> a j b", b=P)),
                    (qg[:], A["q_norm"].to_broadcast([P, DH])),
                    (kg[:], A["k_norm"].to_broadcast([P, DH])),
                    (ckg[:], A["ck_norm"].to_broadcast([P, 2 * DH])),
                    (ptw[:], A["page_table"].rearrange("b (g o) -> (b g) o", o=1)),
                    (ptr[:], A["page_table"]),
                    (bif[:], A["b_if"].to_broadcast([P, 2 * H]))):
                act.dma_start(dst, src).then_inc(consts_in, 16)

            def split_hi(n):
                s, u = uses(n)
                w = D_IDX + 3 * H if n == 2 else P
                act.wait_ge(raw_full[s], 16 * (u + 1))
                if u:
                    act.wait_ge(w_used[s], u)
                a.copy(whi[:, s, :, 0:w], raw[:, s, :, 0:w]).then_inc(hi_full[s], 1)

            bank = rd_bank(act, 0)
            S(a.copy(gains[:], bank[:, 0:82]), vec_ready)
            S(a.copy(cw[:], bank[:, 128:260].rearrange("p (j f) -> p j f", j=3)), bank_read[0])
            for k in range(KT):
                act.wait_ge(xT_turned, k + 1)
                a.copy(xT0[:, k, 0:SEQ], PJ[k % 2][:, 0, :])
                a.copy(xT0[:, k, SEQ:T], PJ[k % 2][:, 1, 0:B]).then_inc(xT_ready, 1)
                act.wait_ge(xT_ready, k + 1)
                if k >= 2:
                    act.wait_ge(sq_used, k - 1)
                a.activation(sq[:, k % 2], xT0[:, k], ACT.Square).then_inc(sq_ready, 1)
                if k == 6:
                    split_hi(0)
            split_hi(1)
            act_rstd(act, 0, rstd, T, D)
            for k in range(KT):
                act.wait_ge(hs_ready, k + 1)
                a.copy(ahi[:, k], hs[:, k % 2]).then_inc(nhi_ready, 1)
            for n, (name, _) in enumerate(IN_TILES):
                s, u = uses(n)
                act.wait_ge(w_used[s], u + 1)
                dst, rows = (z_i[:, n], P) if n < 3 else (z_a[:, n - 3], P) if n < 15 else (z_m[:, n - 15], P)
                if n == 2:
                    dst, rows = z_i[0:D_IDX + 3 * H, 2], D_IDX + 3 * H
                a.copy(dst.rearrange("p (a b) -> p a b", a=2), PJ[s][0:rows, :, 0:HALF]).then_inc(out_free[s], 1)
                if n + 2 < N_IN:
                    split_hi(n + 2)
                act_hooks(act, n)
            act_tail(act)

        @block.vector
        def _(dve):
            v = nc.vector
            dve.wait_ge(consts_in, 16 * 18)
            ptf = tiny[0:B * NPG, 104:109]
            V(v.tensor_copy(ptf[:, 4:5], ptw[:]))
            for c in range(4):
                V(v.tensor_scalar(ptf[:, c:c + 1], ptf[:, 4:5], 4.0, float(c), ALU.mult, ALU.add))
            V(v.tensor_copy(pidx[:], ptf[:, 0:4]), pidx_ready)
            dve.wait_ge(vec_ready, 1)
            vec_norm(dve, 0, xT0, rstd, G_MIX, hs, T)
            for n in range(N_IN):
                vec_hooks(dve, n)
            vec_tail(dve)

        @block.tensor
        def _(pe):
            t = nc.tensor
            pe.wait_ge(consts_made, 15)
            pe.wait_ge(consts_in, 16 * 18)
            t.transpose(pe_bank(pe, 0)[:, 0:82], vecs[:], ident[0:82, 0:82])
            bank = TA
            for j in range(3):
                m = t.transpose(bank[:, 128 + j * 44:128 + (j + 1) * 44], cwrows[:, j, :], ident[0:44, 0:44])
            m.then_inc(bank_full[0], 1)
            pe.wait_ge(x_in_s, 16 * (NTT + 1))
            for k in range(KT):
                if k >= 2:
                    pe.wait_ge(xT_ready, k - 1)
                for tt in range(NTT):
                    t.transpose(PJ[k % 2][:, 0, tt * P:(tt + 1) * P], x_in[:, tt, k * P:(k + 1) * P], ident[:])
                t.transpose(PJ[k % 2][:, 1, 0:B], xs_in[:, k * P:(k + 1) * P], ident[0:B, 0:B]).then_inc(xT_turned, 1)
                if k >= 1:
                    pe_sumsq(pe, 0, k - 1, sq, T)
            pe_sumsq(pe, 0, KT - 1, sq, T)
            pe.wait_ge(nlo_ready, KT)
            for n in range(N_IN):
                s, u = uses(n)
                m = P if n != 2 else D_IDX + 3 * H
                pe.wait_ge(split_full[s], u + 1)
                if u:
                    pe.wait_ge(out_free[s], u)
                pe_product(s, PJ[s], m, KT, ahi, alo).then_inc(w_used[s], 1)
                pe_hooks(pe, n)
            pe_tail(pe)


_OUT_SHAPES = [(1, SEQ, D), (B, 1, D), (1, 1, SEQ, H, DH), (1, 1, SEQ, H, DH), (1, 1, SEQ, D_IDX),
               (1, 1, H, DH, DH), (1, 1, H, DH), (1, 1, H), (1, 1, NMEM, H, 2 * DH), (1, 1, NMEM, H, 2 * DH),
               (1, 1, 2, 2 * DFF), (1, B, 1, H, DH), (1, B, 1, H, DH), (1, B, 1, D_IDX),
               (1, B, H, DH, DH), (1, B, H, DH), (1, B, H), (1, B, 2, 2 * DFF)]
_OUT_NAMES = ["y_prompt", "y_sample", "p_k", "p_v", "p_idx_k", "p_c", "p_n", "p_m", "p_mem_k", "p_mem_v", "p_conv",
              "s_k", "s_v", "s_idx_k", "s_c", "s_n", "s_m", "s_conv"]


def kernel(**inputs):
    import concourse.bacc as bacc
    from concourse.bass_utils import run_bass_kernel_spmd

    nc = bacc.Bacc("TRN2", target_bir_lowering=False, num_devices=1)
    arrays, A, O = {}, {}, {}
    rope_main, rope_index = rope_tables()
    for name, value in list(inputs.items()) + [("rope_main", rope_main), ("rope_index", rope_index)]:
        value = np.ascontiguousarray(value)
        arrays[f"in_{name}"] = value
        A[name] = nc.dram_tensor(f"in_{name}", value.shape, mybir.dt.from_np(value.dtype), kind="ExternalInput").ap()
    for name, shape in zip(_OUT_NAMES, _OUT_SHAPES):
        O[name] = nc.dram_tensor(f"out_{name}", shape, F32, kind="ExternalOutput").ap()
    build(nc, A, O)
    r = run_bass_kernel_spmd(nc, [arrays], core_ids=[0])
    return tuple(r.results[0][f"out_{name}"] for name in _OUT_NAMES)
```

```python
import numpy as np
from contextlib import ExitStack

import concourse.bass as bass
from concourse import mybir

F32 = mybir.dt.float32
F32R = mybir.dt.float32r
I32 = mybir.dt.int32
U32 = mybir.dt.uint32
ALU = mybir.AluOpType
ACT = mybir.ActivationFunctionType
AX = mybir.AxisListType.X

P = 128
D = 1024
KT = D // P
SEQ = 512
NTT = SEQ // P
B = 8
T = SEQ + B
HALF = T // 2
H = 4
DH = 128
MIX = H * DH
D_IDX = 64
N_MISC = H * D_IDX + D_IDX + H + 2 * H
DFF = 2816
NFT = DFF // P
PAGE = 128
NPG = 8
PAST = NPG * PAGE
TOPK_P = 128
TOPK_S = 256
NMEM = 256
EPS = 1e-6
NEG = -1e30
TAKEN = -3e38
SCALE = DH ** -0.5
SCALE_C = 256 ** -0.5
C_MQ, C_MK, C_MV, C_MO, C_G = 0, MIX, 2 * MIX, 3 * MIX, 4 * MIX
C_AQ = C_G + 2 * H
C_AK, C_AV = C_AQ + MIX, C_AQ + 2 * MIX
C_IQ = C_AQ + 3 * MIX
IN_TILES = ([("iq0", C_IQ), ("iq1", C_IQ + P), ("ikw", C_IQ + 2 * P)]
            + [(f"{g}{h}", c + h * DH) for g, c in (("aq", C_AQ), ("ak", C_AK), ("av", C_AV), ("mq", C_MQ),
                                                     ("mk", C_MK), ("mv", C_MV), ("mo", C_MO)) for h in range(H)])
TI = {name: n for n, (name, _) in enumerate(IN_TILES)}


def rope_tables():
    pos = np.concatenate([np.arange(SEQ), np.full(B, PAST)]).astype(np.float32)
    out = []
    for half in (DH // 2, D_IDX // 2):
        inv = (np.float32(10000.0) ** (-np.arange(half, dtype=np.float32) / np.float32(half))).astype(np.float32)
        ang = pos[:, None] * inv[None, :]
        out.append(np.stack([np.cos(ang), np.sin(ang)], axis=1).astype(np.float32))
    return out


def build(nc, A, O):
    with ExitStack() as ctx:
        sems = {}

        def sem(name):
            sems[name] = ctx.enter_context(nc.semaphore(name))
            return sems[name]

        cursor = [(nc.sbuf_base + 63) // 64 * 64]

        def sb(name, shape, dt=F32):
            n = int(np.prod(shape[1:])) * 4
            t = nc.alloc_sbuf_tensor_at(name, shape, dt, offset=cursor[0])
            cursor[0] += (n + 31) // 32 * 32
            return t

        raw = sb("raw", [P, 2, KT, P])
        whi = sb("whi", [P, 2, KT, P], F32R)
        wlo = sb("wlo", [P, 2, KT, P], F32R)
        ahi_at = cursor[0]
        ahi = sb("ahi", [P, KT, T], F32R)
        alo = sb("alo", [P, KT, T], F32R)
        ident = sb("ident", [P, P])
        ones = sb("ones", [P, P])
        tri = sb("tri", [P, P])
        negm = sb("negm", [P, P])
        posm = sb("posm", [P, P])
        rowsel = sb("rowsel", [B, B, P])
        own = sb("own", [B, H, B])
        rope_m = sb("rope_m", [P, NTT, 2, DH // 2])
        rope_ms = sb("rope_ms", [B, 2, DH // 2])
        rope_i = sb("rope_i", [P, NTT, 2, D_IDX // 2])
        rope_is = sb("rope_is", [B, 2, D_IDX // 2])
        vecs = sb("vecs", [82, P])
        gains = sb("gains", [P, 82])
        cwrows = sb("cwrows", [2 * NFT, 3, P])
        cw = sb("cw", [P, 3, 2 * NFT])
        qg = sb("qg", [P, DH])
        kg = sb("kg", [P, DH])
        ckg = sb("ckg", [P, 2 * DH])
        bif = sb("bif", [P, 2 * H])
        epsc = sb("epsc", [P, 1])
        gt = sb("gt", [P, NTT + 1, 2 * H])
        ptw = sb("ptw", [B * NPG, 1], I32)
        pidx = sb("pidx", [B * NPG, 4], U32)
        ptr = sb("ptr", [B, NPG], I32)
        G_MIX, G_CROSS, G_MEM, G_FFN, G_CQ, G_ML, G_CB = 0, 8, 16, 24, 32, 34, 38
        R0 = cursor[0]

        def reg(name, shape, at, dt=F32):
            return nc.alloc_sbuf_tensor_at(name, shape, dt, offset=R0 + 4 * at)

        z_m = reg("z_m", [P, 4 * H, T], 0)
        mk_tok = reg("mk_tok", [P, NTT, MIX], 8320)
        mv_tok = reg("mv_tok", [P, NTT, MIX], 10368)
        z_a = reg("z_a", [P, 3 * H, T], 12416)
        av_tok = reg("av_tok", [P, NTT, MIX], 18656)
        tk = reg("tk", [P, 4, SEQ], 20704)
        selb = reg("selb", [P, 9, P], 22752)
        aw = reg("aw", [P, 4, SEQ], 23904)
        rt = reg("rt", [P, 2, NTT, DH], 25952)
        rw = reg("rw", [P, 3, NTT, DH], 26976)
        s_tok = reg("s_tok", [B, 3, MIX], 28512)
        skv = reg("skv", [P, 2, 2, MIX], 30048)
        iw_tok = reg("iw_tok", [P, NTT, H], 32096)
        sw = reg("sw", [B, MIX], 32112)
        srow = reg("srow", [2 * B, SEQ + 8], 32624)
        svals = reg("svals", [2 * B, 2, TOPK_S], 33144)
        sidx = reg("sidx", [2 * B, TOPK_S], 33656, U32)
        rowf = reg("rowf", [B, TOPK_S], 33912)
        maskf = reg("maskf", [B, TOPK_S], 34168)
        sv = reg("sv", [B, MIX], 33912)
        rowT = reg("rowT", [P, 2, B], 34424, U32)
        maskT = reg("maskT", [P, 2, B], 34440)
        iqS = reg("iqS", [D_IDX, H, B], 34456)
        iwb = reg("iwb", [P, B, H], 34488)
        tiny = reg("tiny", [P, 200], 34520)
        s_scr = reg("s_scr", [P, 4, 2, B, H], 7400)
        s_sum = reg("s_sum", [P, 4, 2, B], 7656)
        sg = reg("sg", [B * NPG, 2048], 30048)
        ikc = reg("ikc", [D_IDX, B * NPG, 32], 23904)
        x_in = reg("x_in", [P, NTT, D], 4160)
        xs_in = reg("xs_in", [B, D], 8320)
        xT0 = reg("xT0", [P, KT, T], 0)
        sq = reg("sq", [P, 2, T], 12416)
        rstd = reg("rstd", [P, T], 13456)
        hs = reg("hs", [P, 2, T], 13976)
        z_i = reg("z_i", [P, 3, T], 4160)
        m_tok = reg("m_tok", [P, NTT, N_MISC], 5720)
        ms_tok = reg("ms_tok", [B, N_MISC], 7048)
        m_rot = reg("m_rot", [P, NTT, 3 * P], 8320)
        ms_rot = reg("ms_rot", [B, 3 * P], 9856)
        m_tmp = reg("m_tmp", [P, 2, 5 * D_IDX], 10240)
        iqT = reg("iqT", [P, 3, SEQ], 10880)

        PS = ctx.enter_context(nc.psum_tensor("PS", [P, 8, 512], F32))
        PJ = [PS[:, 0:2, :], PS[:, 2:4, :]]
        TA, TB, XA, XB = (PS[:, b, :] for b in (4, 5, 6, 7))

        consts_in, gates_in, x_in_s = sem("consts_in"), sem("gates_in"), sem("x_in_s")
        consts_made, vec_ready = sem("consts_made"), sem("vec_ready")
        raw_full = [sem("raw_full0"), sem("raw_full1")]
        hi_full = [sem("hi_full0"), sem("hi_full1")]
        split_full = [sem("split_full0"), sem("split_full1")]
        w_used = [sem("w_used0"), sem("w_used1")]
        out_free = [sem("out_free0"), sem("out_free1")]
        xT_turned, xT_ready, sq_ready, sq_used = sem("xT_turned"), sem("xT_ready"), sem("sq_ready"), sem("sq_used")
        rstd_ready, hs_ready, nhi_ready, nlo_ready = (
            sem("rstd_ready"), sem("hs_ready"), sem("nhi_ready"), sem("nlo_ready"))
        v_step, a_step = sem("v_step"), sem("a_step")

        bank_full = [sem(f"bank{b}_full") for b in range(4)]
        bank_read = [sem(f"bank{b}_read") for b in range(4)]
        BANKS = [TA, TB, XA, XB]
        filled, taken = [0] * 4, [0] * 4

        def pe_bank(pe, b):
            if filled[b]:
                pe.wait_ge(bank_read[b], filled[b])
            filled[b] += 1
            return BANKS[b]

        def rd_bank(eng, b):
            taken[b] += 1
            eng.wait_ge(bank_full[b], taken[b])
            return BANKS[b]

        count = {}

        def signal(eng, ins, s):
            count[s.name] = count.get(s.name, 0) + 1
            ins.then_inc(s, 1)
            eng.wait_ge(s, count[s.name])

        def S(ins, s=None):
            signal(nc.scalar, ins, a_step if s is None else s)

        def V(ins, s=None):
            signal(nc.vector, ins, v_step if s is None else s)

        def uses(n):
            return n % 2, n // 2

        N_IN = len(IN_TILES)
        BASE0 = (N_IN + 1) // 2


        def pe_product(s, out, m, kt, hi, lo, first=True, last=True, k0=0, ks=None):
            for k in ks or range(kt):
                for j, (w, x) in enumerate(((whi, hi), (whi, lo), (wlo, hi))):
                    for half in range(2):
                        ins = nc.tensor.matmul(out[0:m, half, 0:HALF], w[:, s, k, 0:m],
                                               x[:, k0 + k, half * HALF:(half + 1) * HALF],
                                               start=(first and k == 0 and j == 0),
                                               stop=(last and k == kt - 1 and j == 2))
            return ins

        def pe_sumsq(pe, stage, k, squares, width):
            pe.wait_ge(sq_ready, KT * stage + k + 1)
            w = width // 2
            for half in range(2):
                bank = pe_bank(pe, half) if k == 0 else BANKS[half]
                ins = nc.tensor.matmul(bank[:, 0:w], ones[:], squares[:, k % 2, half * w:(half + 1) * w],
                                       start=(k == 0), stop=(k == KT - 1))
            ins.then_inc(sq_used, 1)

        def act_rstd(act, stage, out, width, n):
            act.wait_ge(sq_used, KT * (stage + 1))
            w = width // 2
            for half in range(2):
                S(nc.scalar.activation(out[:, half * w:(half + 1) * w], BANKS[half][:, 0:w], ACT.Ln, bias=epsc[:],
                                       scale=1.0 / n), bank_read[half])
            S(nc.scalar.activation(out[:, 0:width], out[:, 0:width], ACT.Exp, scale=-0.5), rstd_ready)

        def vec_norm(dve, stage, src, r, g0, h, width, lo=None):
            hi, lo = (ahi, alo) if lo is None else lo
            dve.wait_ge(rstd_ready, stage + 1)
            for k in range(KT + 1):
                if k < KT:
                    if KT * stage + k >= 2:
                        dve.wait_ge(nlo_ready, KT * stage + k - 1)
                    nc.vector.scalar_tensor_tensor(h[:, k % 2, 0:width], src[:, k, 0:width], gains[:, g0 + k:g0 + k + 1],
                                                   r[:, 0:width], ALU.mult, ALU.mult).then_inc(hs_ready, 1)
                if k:
                    dve.wait_ge(nhi_ready, KT * stage + k)
                    nc.vector.tensor_tensor(lo[:, k - 1, 0:width], h[:, (k - 1) % 2, 0:width],
                                            hi[:, k - 1, 0:width].bitcast(F32), ALU.subtract).then_inc(nlo_ready, 1)

        HOOKS = {(3, 1): ["misc"], (5, 2): ["idx_back"], (6, 0): ["gather:0"], (6, 3): ["idx_score:1"], (9, 1): ["gather:1"],
                 (9, 2): ["idx_sel:1", "idx_score:2"], (11, 3): ["gather:2"], (12, 2): ["idx_sel:2", "idx_score:3"],
                 (13, 3): ["gather:3"], (14, 3): ["sidx"], (18, 2): ["idx_sel:3"], (26, 0): ["ml_prep"],
                 (19, 1): ["turn:mq0"], (20, 2): ["turn:mq1"], (21, 1): ["turn:mq2"], (21, 2): ["turn:mq3"]}

        def at(n, q, step):
            HOOKS.setdefault((n, q), []).append(step)

        for g, first in (("aq", 12), ("ak", 16)):
            for h in range(H):
                at(first + h, 0, f"turn:{g}{h}")
                at(first + h, 2, f"norm:{g}{h}")
                at(first + h + 1, 1, f"back:{g}{h}")
            at(first + H - 1, 3, f"head_s:{g}")
            at(first + H + (g == "ak"), 1, f"back_s:{g}")
        for g, first in (("av", 17), ("mk", 21), ("mv", 25)):
            for h in range(H):
                at(first + h, 3, f"turn:{g}{h}")
        for n, k in ((7, 6), (8, 6), (10, 5), (11, 5), (13, 3), (14, 3), (15, 3), (16, 2), (17, 3)):
            at(n, 2, f"idx_rounds:{k}")
        ATT_FIRST = 9
        for i in range(ATT_FIRST):
            at((90 + 4 * i) // 4, (90 + 4 * i) % 4, f"att:{i}")
        for n in range(18, 31):
            at(n, 1, f"rounds:{1 if n == 18 else 2}")
        ROUNDS = [1, 1, 1, 1, 1, 1, 1]
        ROT = 5 * D_IDX

        def halves(x, h):
            return x.rearrange("p (h a d) -> p h a d", h=h, a=2)

        def rope(x, t1, t2, out, cos, sin):
            shape = list(x.shape)
            for a in range(2):
                V(nc.vector.tensor_tensor(t1[:, :, a], x[:, :, a], cos, ALU.mult))
                V(nc.vector.tensor_tensor(t2[:, :, a], x[:, :, 1 - a], sin, ALU.mult))
            V(nc.vector.tensor_tensor(out[:, :, 0], t1[:, :, 0], t2[:, :, 0], ALU.subtract))
            return nc.vector.tensor_tensor(out[:, :, 1], t1[:, :, 1], t2[:, :, 1], ALU.add)

        def tile_ready(eng, name):
            s, u = uses(TI[name])
            eng.wait_ge(out_free[s], u + 1)

        (misc_tok, gate_abs, gate_ln, iqT_ready, m_rot_ready, iwm_ready, rl_used, rl_ready, sg_full, ikc_full, s_scr_ready,
         s_sum_ready, srow_ready, halves_ready, rows_found, rt_ready, rs_ready, head_sq, head_ss, head_rstd,
         back_ready, sv_stored, stores, pidx_ready) = (sem(x) for x in (
             "misc_tok gate_abs gate_ln iqT_ready m_rot_ready iwm_ready rl_used rl_ready sg_full ikc_full s_scr_ready "
             "s_sum_ready srow_ready halves_ready rows_found rt_ready rs_ready head_sq head_ss head_rstd "
             "back_ready sv_stored stores pidx_ready").split())
        rt_stored = [sem("rt_stored0"), sem("rt_stored1")]
        turn_ready = {g: sem(f"turn_{g}") for g in ("aq", "ak", "av", "mq", "mk", "mv")}

        def pe_misc(pe):
            tile_ready(pe, "iq1")
            tile_ready(pe, "ikw")
            r = D_IDX + 3 * H
            for tt in range(NTT + 1):
                w = P if tt < NTT else B
                bank = pe_bank(pe, tt % 2)
                for f, rows in ((0, P), (1, P), (2, r)):
                    m = nc.tensor.transpose(bank[0:w, f * P:f * P + rows], z_i[0:rows, f, tt * P:tt * P + w],
                                            ident[0:rows, 0:rows])
                m.then_inc(bank_full[tt % 2], 1)

        def pe_idx_back(pe):
            pe.wait_ge(m_rot_ready, NTT + 1)
            for f in range(3):
                bank = pe_bank(pe, f % 2)
                for tt in range(NTT):
                    m = nc.tensor.transpose(bank[:, tt * P:(tt + 1) * P], m_rot[:, tt, f * P:(f + 1) * P], ident[:])
                m.then_inc(bank_full[f % 2], 1)
            bank = pe_bank(pe, 1)
            for h in range(H):
                m = nc.tensor.transpose(bank[0:D_IDX, h * B:(h + 1) * B], ms_rot[:, h * D_IDX:(h + 1) * D_IDX],
                                        ident[0:B, 0:B])
            m.then_inc(bank_full[1], 1)
            pe.wait_ge(iwm_ready, 1)
            m = nc.tensor.matmul(pe_bank(pe, 0)[:, 0:B * H], ones[0:B, :], tiny[0:B, 64:96], start=True, stop=True)
            m.then_inc(bank_full[0], 1)

        def pe_idx_score(pe, qt):
            pe.wait_ge(iqT_ready, 3)
            n = (qt + 1) * P
            for h in range(H):
                r = D_IDX * (h % 2)
                nc.tensor.matmul(pe_bank(pe, h % 2)[:, 0:n], iqT[r:r + D_IDX, h // 2, qt * P:(qt + 1) * P],
                                 iqT[r:r + D_IDX, 2, 0:n], start=True, stop=True).then_inc(bank_full[h % 2], 1)

        def pe_gather(pe, c):
            pe.wait_ge(sg_full, 16 * (c + 1))
            for g in range(4):
                bank = pe_bank(pe, g % 2)
                for r in range(8):
                    m = nc.tensor.transpose(bank[0:D_IDX, r * D_IDX:(r + 1) * D_IDX],
                                            sg[:, (g * 8 + r) * D_IDX:(g * 8 + r + 1) * D_IDX], ident[0:B * NPG, 0:B * NPG])
                m.then_inc(bank_full[g % 2], 1)
            pe.wait_ge(ikc_full, 4 * (c + 1))
            bank = pe_bank(pe, 0)
            for b in range(B):
                for pg in range(2):
                    j = (pg * B + b) * H
                    p0 = b * NPG + 4 * pg
                    m = nc.tensor.matmul(bank[:, j:j + H], ikc[:, p0:p0 + 4, :].rearrange("d a r -> d (a r)"),
                                         iqS[:, :, b], start=True, stop=True)
            m.then_inc(bank_full[0], 1)

        def pe_sidx(pe):
            pe.wait_ge(s_sum_ready, 1)
            bank = pe_bank(pe, 0)
            for c in range(4):
                m = nc.tensor.transpose(bank[0:2 * B, c * P:(c + 1) * P], s_sum[:, c].rearrange("p g b -> p (g b)"), ident[:])
            m.then_inc(bank_full[0], 1)
            nc.tensor.matmul(pe_bank(pe, 1)[0:2 * B, 0:1], own[:, 0:2, :].rearrange("r h b -> r (h b)"), tiny[0:B, 41:42],
                             start=True, stop=True).then_inc(bank_full[1], 1)

        def pe_turn(pe, name):
            tile_ready(pe, name)
            n = TI[name]
            z = z_a[:, n - 3] if n < 15 else z_m[:, n - 15]
            if name[:2] != "mq":
                bank = pe_bank(pe, 0)
                for tt in range(NTT):
                    m = nc.tensor.transpose(bank[:, tt * P:(tt + 1) * P], z[:, tt * P:(tt + 1) * P], ident[:])
                m.then_inc(bank_full[0], 1)
            if name[:2] != "mv":
                i = 0 if name[:2] == "mk" else 1
                nc.tensor.transpose(pe_bank(pe, i)[0:B, 0:P], z[:, SEQ:T], ident[:]).then_inc(bank_full[i], 1)

        def pe_back(pe, g, h):
            j = H * g + h
            pe.wait_ge(rt_ready, j + 1)
            bank = pe_bank(pe, 0)
            for tt in range(NTT):
                m = nc.tensor.transpose(bank[:, tt * P:(tt + 1) * P], rt[:, j % 2, tt, :], ident[:])
            m.then_inc(bank_full[0], 1)

        def pe_back_s(pe, g):
            pe.wait_ge(rs_ready, g + 1)
            bank = pe_bank(pe, 1)
            src = sw if g == 0 else s_tok[:, 0, :]
            for h in range(H):
                m = nc.tensor.transpose(bank[:, h * B:(h + 1) * B], src[:, h * DH:(h + 1) * DH], ident[0:B, 0:B])
            m.then_inc(bank_full[1], 1)

        def act_misc(act):
            for tt in range(NTT + 1):
                bank = rd_bank(act, tt % 2)
                dst, w = (m_tok[:, tt, :], P) if tt < NTT else (ms_tok[:], B)
                S(nc.scalar.copy(dst, bank[0:w, 0:N_MISC]), bank_read[tt % 2])
            act.sem_inc(misc_tok, 1)

        def act_gates(act):
            act.wait_ge(gate_abs, 1)
            S(nc.scalar.activation(tiny[:, 0:20], tiny[:, 0:20], ACT.Exp))
            S(nc.scalar.activation(tiny[:, 0:20], tiny[:, 0:20], ACT.Ln, bias=ones[:, 0:1]), gate_ln)

        def act_idx_back(act):
            for f in range(3):
                bank = rd_bank(act, f % 2)
                S(nc.scalar.copy(iqT[:, f, :], bank[:]), bank_read[f % 2])
                act.sem_inc(iqT_ready, 1)
            S(nc.scalar.copy(iqS[:].rearrange("d h b -> d (h b)"), rd_bank(act, 1)[0:D_IDX, 0:H * B]), bank_read[1])
            S(nc.scalar.copy(iwb[:].rearrange("p b h -> p (b h)"), rd_bank(act, 0)[:, 0:H * B]), bank_read[0])
            act.dma_start(O["p_idx_k"][0, 0].rearrange("(t p) d -> p t d", p=P),
                          m_rot[:, :, H * D_IDX:ROT]).then_inc(stores, 16)
            act.dma_start(O["s_idx_k"][0, :, 0, :], ms_rot[:, H * D_IDX:ROT]).then_inc(stores, 16)

        def act_idx_score(act, qt):
            n = (qt + 1) * P
            for h in range(H):
                j = 4 * (qt - 1) + h
                bank = rd_bank(act, h % 2)
                if j >= 2:
                    act.wait_ge(rl_used, j - 1)
                S(nc.scalar.activation(tk[:, 2 + h % 2, 0:n], bank[:, 0:n], ACT.Relu), bank_read[h % 2])
                act.sem_inc(rl_ready, 1)

        def act_gather(act, c):
            for g in range(4):
                bank = rd_bank(act, g % 2)
                S(nc.scalar.copy(ikc[:, :, g * 8:(g + 1) * 8].rearrange("d q r -> d r q"),
                                 bank[0:D_IDX, :].rearrange("d (r q) -> d r q", r=8)), bank_read[g % 2])
                act.sem_inc(ikc_full, 1)
            S(nc.scalar.activation(s_scr[:, c].rearrange("p g b h -> p (g b h)"), rd_bank(act, 0)[:, 0:2 * B * H],
                                   ACT.Relu), bank_read[0])
            act.sem_inc(s_scr_ready, 1)

        def act_sidx(act):
            bank = rd_bank(act, 0)
            for c in range(4):
                S(nc.scalar.copy(srow[:, 0:SEQ].rearrange("b (g c r) -> b g c r", g=4, c=4)[:, :, c],
                                 bank[0:2 * B, c * P:(c + 1) * P].rearrange("b (g r) -> b g r", g=4)),
                  bank_read[0] if c == 3 else None)
            S(nc.scalar.copy(srow[:, SEQ:SEQ + 1], rd_bank(act, 1)[0:2 * B, 0:1]), bank_read[1])
            act.sem_inc(srow_ready, 1)

        def act_rms_small(act, x, n, sem_in, k, sem_out):
            act.wait_ge(sem_in, k)
            S(nc.scalar.activation(x, x, ACT.Ln, bias=epsc[0:x.shape[0]], scale=1.0 / n))
            S(nc.scalar.activation(x, x, ACT.Exp, scale=-0.5), sem_out)

        def act_turn(act, name):
            g, h = name[:2], int(name[2])
            if g in ("aq", "ak"):
                j = h + (H if g == "ak" else 0)
                if j:
                    act.wait_ge(rt_ready, j)
                if j == H:
                    act.wait_ge(rs_ready, 1)
            dst = {"aq": rw[:, 0], "ak": rw[:, 0], "av": av_tok[:, :, h * DH:(h + 1) * DH],
                   "mk": mk_tok[:, :, h * DH:(h + 1) * DH], "mv": mv_tok[:, :, h * DH:(h + 1) * DH]}.get(g)
            if dst is not None:
                bank = rd_bank(act, 0)
                if g in ("aq", "ak"):
                    S(nc.scalar.activation(rw[:, 1], bank[:].rearrange("p (t d) -> p t d", t=NTT), ACT.Square), head_sq)
                S(nc.scalar.copy(dst, bank[:].rearrange("p (t d) -> p t d", t=NTT)), bank_read[0])
            sdst = {"aq": sw[:, h * DH:(h + 1) * DH], "ak": s_tok[:, 0, h * DH:(h + 1) * DH], "av": sv[:, h * DH:(h + 1) * DH],
                    "mq": s_tok[:, 1, h * DH:(h + 1) * DH], "mk": s_tok[:, 2, h * DH:(h + 1) * DH]}.get(g)
            if sdst is not None:
                i = 0 if g == "mk" else 1
                S(nc.scalar.copy(sdst, rd_bank(act, i)[0:B, 0:DH]), bank_read[i])
            act.sem_inc(turn_ready[g], 1)
            if g == "av" and h == H - 1:
                act.dma_start(O["p_v"][0, 0].rearrange("(t p) h d -> p t (h d)", p=P), av_tok[:]).then_inc(stores, 16)
                act.dma_start(O["s_v"][0, :, 0].rearrange("b h d -> b (h d)"), sv[:]).then_inc(sv_stored, 16)

        def act_norm_head(act, j):
            k = jn(j // H, j % H) + 1
            act_rms_small(act, tiny[:, 20:24], DH, head_ss, k, head_rstd)

        def act_back(act, g, h):
            j = H * g + h
            bank = rd_bank(act, 0)
            S(nc.scalar.copy(z_a[:, j, 0:SEQ], bank[:]), bank_read[0])
            act.sem_inc(back_ready, 1)
            if g == 1:
                act.dma_start(O["p_k"][0, 0].rearrange("(t p) h d -> p t h d", p=P)[:, :, h, :],
                              rt[:, j % 2]).then_inc(rt_stored[j % 2], 16)

        def act_back_s(act, g):
            S(nc.scalar.copy(z_a[:, H * g:H * (g + 1), SEQ:T],
                             rd_bank(act, 1)[:, 0:H * B].rearrange("p (h b) -> p h b", h=H)), bank_read[1])
            if g == 1:
                act.dma_start(O["s_k"][0, :, 0].rearrange("b h d -> b (h d)"), s_tok[:, 0, :]).then_inc(stores, 16)

        def vec_misc(dve):
            v = nc.vector
            dve.wait_ge(misc_tok, 1)
            dve.wait_ge(consts_in, 16 * 18)
            for tt in range(NTT + 1):
                prompt = tt < NTT
                x, rot, w = (m_tok[:, tt], m_rot[:, tt], P) if prompt else (ms_tok[:], ms_rot[:], B)
                tab = rope_i[:, tt] if prompt else rope_is[:]
                cos, sin = (tab[:, a].unsqueeze(1).to_broadcast([w, 5, D_IDX // 2]) for a in range(2))
                V(rope(halves(x[:, 0:ROT], 5), halves(m_tmp[0:w, 0], 5), halves(m_tmp[0:w, 1], 5),
                       halves(rot[:, 0:ROT], 5), cos, sin))
                V(v.tensor_copy(rot[:, ROT:ROT + D_IDX], rot[:, H * D_IDX:ROT]), m_rot_ready)
                if prompt:
                    V(v.tensor_copy(iw_tok[:, tt], x[:, ROT:ROT + H]))
                V(v.tensor_tensor(gt[0:w, tt], x[:, ROT + H:N_MISC], bif[0:w], ALU.add))
            f = gt[:, :, H:2 * H]
            ab = tiny[:, 0:20].rearrange("p (t h) -> p t h", h=H)
            V(v.scalar_tensor_tensor(ab, f, -1.0, f, ALU.mult, ALU.min), gate_abs)
            V(v.tensor_tensor(tiny[0:B, 64:96].rearrange("r (b h) -> r b h", b=B), own[:].rearrange("r h b -> r b h"),
                              ms_tok[:, ROT:ROT + H].unsqueeze(1).to_broadcast([B, B, H]), ALU.mult), iwm_ready)

        def vec_gates(dve):
            f = gt[:, :, H:2 * H]
            dve.wait_ge(gate_ln, 1)
            V(nc.vector.scalar_tensor_tensor(f, f, 0.0, tiny[:, 0:20].rearrange("p (t h) -> p t h", h=H), ALU.min,
                                             ALU.subtract))

        def vec_new_score(dve):
            v = nc.vector
            t = rw[0:B, 2].rearrange("b t d -> b (t d)")[:, 0:256]
            V(v.tensor_tensor(t.rearrange("b (h d) -> b h d", h=H), ms_rot[:, 0:256].rearrange("b (h d) -> b h d", h=H),
                              ms_rot[:, 256:320].unsqueeze(1).to_broadcast([B, H, D_IDX]), ALU.mult))
            V(v.tensor_reduce(tiny[0:B, 96:100], t.rearrange("b (h d) -> b h d", h=H), AX, ALU.add))
            V(v.scalar_tensor_tensor(tiny[0:B, 100:104], tiny[0:B, 96:100], 0.0, ms_tok[:, ROT:ROT + H], ALU.max, ALU.mult))
            V(v.tensor_reduce(tiny[0:B, 41:42], tiny[0:B, 100:104], AX, ALU.add))

        def take_rounds(row, m8, rounds):
            for _ in range(rounds):
                V(nc.vector.max(m8, row))
                V(nc.vector.match_replace(row, m8, row, TAKEN))

        def vec_idx_score(dve, qt):
            v = nc.vector
            n = (qt + 1) * P
            acc = tk[:, qt % 2, 0:n]
            for h in range(H):
                dve.wait_ge(rl_ready, 4 * (qt - 1) + h + 1)
                w = iw_tok[:, qt, h:h + 1]
                if h == 0:
                    V(v.tensor_scalar(acc, tk[:, 2 + h % 2, 0:n], w, None, ALU.mult), rl_used)
                else:
                    V(v.scalar_tensor_tensor(acc, tk[:, 2 + h % 2, 0:n], w, acc, ALU.mult, ALU.add), rl_used)
            V(v.tensor_tensor(acc[:, qt * P:n], acc[:, qt * P:n], negm[:], ALU.add))
            idx_now[:] = [qt, 0]

        idx_now = [0, 0]

        def vec_idx_rounds(dve, n):
            qt, done = idx_now
            take_rounds(tk[:, qt % 2, 0:(qt + 1) * P], tiny[:, 24:32], n)
            idx_now[1] = done + n

        def vec_idx_sel(dve, qt):
            v = nc.vector
            vec_idx_rounds(dve, TOPK_P // 8 - idx_now[1])
            n = (qt + 1) * P
            acc = tk[:, qt % 2, 0:n]
            o = (0, 2, 5)[qt - 1]
            V(v.tensor_scalar(selb[:, o:o + qt + 1, :].rearrange("p a b -> p (a b)"), acc, 0.1 * TAKEN, NEG,
                              ALU.is_gt, ALU.mult))

        def vec_gather(dve, c):
            if c < 3:
                return
            v = nc.vector
            dve.wait_ge(s_scr_ready, 4)
            x = s_scr[:].rearrange("p c g b h -> p (c g) (b h)")
            V(v.tensor_tensor(x, x, iwb[:].rearrange("p b h -> p (b h)").unsqueeze(1).to_broadcast([P, 8, B * H]), ALU.mult))
            V(v.tensor_reduce(s_sum[:].rearrange("p c g b -> p (c g b)"),
                              s_scr[:].rearrange("p c g b h -> p (c g b) h"), AX, ALU.add), s_sum_ready)

        rounds_done = [0]

        def vec_rounds(dve, n):
            v = nc.vector
            row = srow[:, 0:SEQ + 1]
            if rounds_done[0] == 0:
                dve.wait_ge(srow_ready, 1)
                V(v.memset(srow[0:B, SEQ:SEQ + 1], TAKEN))
            for r in range(rounds_done[0], rounds_done[0] + n):
                m8 = svals[:, 0, r * 8:(r + 1) * 8]
                V(v.max(m8, row))
                V(v.max_index(sidx[:, r * 8:(r + 1) * 8], m8, row))
                V(v.match_replace(row, m8, row, TAKEN))
            rounds_done[0] += n

        def pe_sidx_merge(pe):
            pe.wait_ge(halves_ready, 1)
            nc.tensor.matmul(pe_bank(pe, 2)[0:B, 0:2 * TOPK_S], ident[0:2 * B, B:2 * B],
                             svals[:].rearrange("b a k -> b (a k)"), start=True, stop=True).then_inc(bank_full[2], 1)

        def vec_sidx(dve):
            v = nc.vector
            vec_rounds(dve, TOPK_S // 8 - rounds_done[0])
            V(v.tensor_copy(svals[:, 1], sidx[:]), halves_ready)
            b = srow[0:B, 0:2 * TOPK_S]
            V(v.tensor_copy(b, rd_bank(dve, 2)[0:B, 0:2 * TOPK_S]), bank_read[2])
            dve.wait_ge(sv_stored, 16)
            V(v.tensor_tensor(maskf[:], svals[0:B, 0], srow[0:B, 0:TOPK_S][:, ::-1], ALU.is_ge))
            V(v.tensor_scalar(b[:, TOPK_S:], b[:, TOPK_S:], float(SEQ), None, ALU.add))
            V(v.tensor_tensor(rowf[:], svals[0:B, 1], srow[0:B, TOPK_S:2 * TOPK_S][:, ::-1], ALU.subtract))
            V(v.tensor_tensor(rowf[:], rowf[:], maskf[:], ALU.mult))
            V(v.tensor_tensor(rowf[:], rowf[:], srow[0:B, TOPK_S:2 * TOPK_S][:, ::-1], ALU.add))
            V(v.tensor_reduce(tiny[0:B, 40:41], rowf[:], AX, ALU.max))
            V(v.tensor_scalar(tiny[0:B, 40:41], tiny[0:B, 40:41], float(PAST), NEG, ALU.is_lt, ALU.mult))
            V(v.tensor_scalar(maskf[:], rowf[:], float(PAST), NEG, ALU.is_ge, ALU.mult))
            V(v.tensor_scalar(rowf[:], rowf[:], float(PAST - 1), None, ALU.min))
            d = tiny[0:B, 48:56]
            V(v.tensor_copy(d, ptr[:]))
            V(v.tensor_scalar(d, d, float(PAGE), None, ALU.mult))
            e = tiny[0:B, 56:64]
            acc, passed = srow[0:B, 0:TOPK_S], srow[0:B, TOPK_S:2 * TOPK_S]
            V(v.tensor_tensor(e[:, 1:8], d[:, 1:8], d[:, 0:7], ALU.subtract))
            V(v.tensor_scalar(e[:, 1:8], e[:, 1:8], -float(PAGE), None, ALU.add))
            V(v.tensor_scalar(acc, rowf[:], d[:, 0:1], None, ALU.add))
            for p in range(1, NPG):
                V(v.tensor_scalar(passed, rowf[:], float(PAGE * p), e[:, p:p + 1], ALU.is_ge, ALU.mult))
                V(v.tensor_tensor(acc, acc, passed, ALU.add))
            V(v.tensor_copy(rowf[:], acc), rows_found)

        def vec_norm_rope(dve, x, t1, t2, out, gain, tab, rstd_col, ready_s, j, w):
            v = nc.vector
            dve.wait_ge(head_rstd, j + 1)
            V(v.tensor_tensor(x, x, rstd_col.unsqueeze(2).to_broadcast([w, 4, DH]), ALU.mult))
            V(v.tensor_tensor(x, x, gain[0:w].unsqueeze(1).to_broadcast([w, 4, DH]), ALU.mult))
            spl = lambda y: y.rearrange("p t (a d) -> p t a d", a=2)
            V(rope(spl(x), spl(t1), spl(t2), spl(out), tab[0], tab[1]), ready_s)

        def vec_head_sum(dve, g, h):
            dve.wait_ge(turn_ready[("aq", "ak")[g]], h + 1)
            V(nc.vector.tensor_reduce(tiny[:, 20:24], rw[:, 1], AX, ALU.add), head_ss)

        def vec_head(dve, g, h):
            j = H * g + h
            if j >= 2:
                dve.wait_ge(back_ready, j - 1)
                if j >= 6:
                    dve.wait_ge(rt_stored[j % 2], 16 * ((j - 4) // 2))
            tab = [rope_m[:, :, a] for a in range(2)]
            vec_norm_rope(dve, rw[:, 0], rw[:, 1], rw[:, 2], rt[:, j % 2], (qg, kg)[g], tab, tiny[:, 20:24], rt_ready,
                          jn(g, h), P)

        def vec_head_s(dve, g):
            x = (sw[:] if g == 0 else s_tok[:, 0, :]).rearrange("b (h d) -> b h d", h=H)
            V(nc.vector.tensor_tensor(rw[0:B, 1], x, x, ALU.mult))
            V(nc.vector.tensor_reduce(tiny[0:B, 20:24], rw[0:B, 1], AX, ALU.add), head_ss)
            tab = [rope_ms[:, a].unsqueeze(1).to_broadcast([B, 4, DH // 2]) for a in range(2)]
            vec_norm_rope(dve, x, rw[0:B, 1], rw[0:B, 2], x, (qg, kg)[g], tab, tiny[0:B, 20:24], rs_ready, jn(g, H), B)

        def jn(g, h):
            return (H + 1) * g + h

        def pe_hooks(pe, n, q):
            for step in HOOKS.get((n, q), ()):
                what, _, arg = step.partition(":")
                if what == "misc":
                    pe_misc(pe)
                elif what == "idx_back":
                    pe_idx_back(pe)
                elif what == "idx_score":
                    pe_idx_score(pe, int(arg))
                elif what == "gather":
                    pe_gather(pe, int(arg))
                elif what == "sidx":
                    pe_sidx(pe)
                elif what == "att":
                    pe_att(pe, int(arg))
                elif what == "ml_prep":
                    pe_ml_prep(pe)
                elif what == "turn":
                    pe_turn(pe, arg)
                elif what == "back":
                    pe_back(pe, ("aq", "ak").index(arg[:2]), int(arg[2]))
                elif what == "back_s":
                    pe_back_s(pe, ("aq", "ak").index(arg))

        def act_hooks(act, n, q):
            for step in HOOKS.get((n, q), ()):
                what, _, arg = step.partition(":")
                if what == "misc":
                    act_misc(act)
                    act_gates(act)
                elif what == "idx_back":
                    act_idx_back(act)
                elif what == "idx_score":
                    act_idx_score(act, int(arg))
                elif what == "gather":
                    act_gather(act, int(arg))
                elif what == "sidx":
                    act_sidx(act)
                elif what == "att":
                    act_att(act, int(arg))
                elif what == "ml_prep":
                    act_ml_prep(act)
                elif what == "turn":
                    act_turn(act, arg)
                elif what == "norm":
                    act_norm_head(act, H * ("aq", "ak").index(arg[:2]) + int(arg[2]))
                elif what == "back":
                    act_back(act, ("aq", "ak").index(arg[:2]), int(arg[2]))
                elif what == "head_s":
                    act_rms_small(act, tiny[0:B, 20:24], DH, head_ss, jn(("aq", "ak").index(arg), H) + 1, head_rstd)
                elif what == "back_s":
                    act_back_s(act, ("aq", "ak").index(arg))

        def vec_hooks(dve, n, q):
            for step in HOOKS.get((n, q), ()):
                what, _, arg = step.partition(":")
                if what == "misc":
                    vec_misc(dve)
                    vec_gates(dve)
                    vec_new_score(dve)
                elif what == "idx_score":
                    vec_idx_score(dve, int(arg))
                elif what == "gather":
                    vec_gather(dve, int(arg))
                elif what == "rounds":
                    vec_rounds(dve, int(arg))
                elif what == "att":
                    vec_att(dve, int(arg))
                elif what == "ml_prep":
                    vec_ml_prep(dve)
                elif what == "idx_rounds":
                    vec_idx_rounds(dve, int(arg))
                elif what == "idx_sel":
                    vec_idx_sel(dve, int(arg))
                elif what == "turn" and arg[:2] in ("aq", "ak"):
                    vec_head_sum(dve, ("aq", "ak").index(arg[:2]), int(arg[2]))
                elif what == "norm":
                    vec_head(dve, ("aq", "ak").index(arg[:2]), int(arg[2]))
                elif what == "head_s":
                    vec_head_s(dve, ("aq", "ak").index(arg))

        def pool_hooks(pool, n):
            c = {2: 0, 8: 1, 10: 2, 13: 3}.get(n)
            if c is not None:
                if c == 0:
                    pool.wait_ge(pidx_ready, 1)
                else:
                    pool.wait_ge(ikc_full, 4 * c)
                nc.gpsimd.indirect_dma_start(sg[:], None, A["cache_idx_k"][0].rearrange("n (c r) d -> (n c) (r d)", c=4),
                                             bass.IndirectOffsetOnAxis(ap=pidx[:, c:c + 1], axis=0)).then_inc(sg_full, 16)

        (att_max, att_exp, att_p, p_turned, pv_done, k_used, rowT_ready, sp_max, sp_exp, sp_ready, spT_ready, v_used,
         ya_ready, dn_ready, rden_ready, qkn_ready, ab_ready, arow_ready, mrow_ready, mb_ready, em_ready, md_ready, dd_ready, wd_ready, nd_done,
         wv_ready, h_ready, hsq_ready, hrs_ready, sig_exp, ym_ready, n_ready, qm_ready, cs_in, sc_in,
         y_hi, y_lo, sst_ready, sx_a, sx_b, shs_ready) = (sem(x) for x in (
             "att_max att_exp att_p p_turned pv_done k_used rowT_ready sp_max sp_exp sp_ready spT_ready v_used "
             "ya_ready dn_ready rden_ready qkn_ready ab_ready arow_ready mrow_ready mb_ready em_ready md_ready dd_ready wd_ready nd_done "
             "wv_ready h_ready hsq_ready hrs_ready sig_exp ym_ready n_ready qm_ready cs_in sc_in "
             "y_hi y_lo sst_ready sx_a sx_b shs_ready").split())
        yv_ready = sem("yv_ready")
        skv_full = [sem("skv_full0"), sem("skv_full1")]
        SEL = [None, (0, 2), (2, 5), (5, 9)]
        N_ATT = H * NTT

        def acol(j, c):
            return tiny[:, 8 + 4 * (j % 2) + c:9 + 4 * (j % 2) + c]

        def pe_att(pe, i):
            if 0 <= i - 1 < N_ATT:
                j = i - 1
                pe.wait_ge(att_p, j + 1)
                bank = pe_bank(pe, 0)
                for kt in range(j % NTT + 1):
                    m = nc.tensor.transpose(bank[:, kt * P:(kt + 1) * P], aw[:, j % 2, kt * P:(kt + 1) * P], ident[:])
                m.then_inc(bank_full[0], 1)
            if i < N_ATT:
                h, qt = divmod(i, NTT)
                if i == 0:
                    pe.wait_ge(back_ready, 2 * H)
                nc.tensor.matmul(pe_bank(pe, 2 + i % 2)[:, 0:(qt + 1) * P], z_a[:, h, qt * P:(qt + 1) * P],
                                 z_a[:, H + h, 0:(qt + 1) * P], start=True, stop=True).then_inc(bank_full[2 + i % 2], 1)
            if i >= 2:
                j = i - 2
                h, qt = divmod(j, NTT)
                pe.wait_ge(p_turned, j + 1)
                bank = pe_bank(pe, 1) if qt == 0 else BANKS[1]
                for kt in range(qt + 1):
                    m = nc.tensor.matmul(bank[:, qt * P:(qt + 1) * P], av_tok[:, kt, h * DH:(h + 1) * DH],
                                         aw[:, 2 + j % 2, kt * P:(kt + 1) * P], start=(kt == 0), stop=(kt == qt))
                m.then_inc(pv_done, 1)

        def act_att(act, i):
            if 0 <= i - 1 < N_ATT:
                j = i - 1
                n = (j % NTT + 1) * P
                bank = rd_bank(act, 0)
                if j >= 2:
                    act.wait_ge(pv_done, j - 1)
                S(nc.scalar.copy(aw[:, 2 + j % 2, 0:n], bank[:, 0:n]), bank_read[0])
                act.sem_inc(p_turned, 1)
            if i < N_ATT:
                n = (i % NTT + 1) * P
                act.wait_ge(att_max, i + 1)
                S(nc.scalar.activation(aw[:, i % 2, 0:n], aw[:, i % 2, 0:n], ACT.Exp, bias=acol(i, 1), scale=SCALE,
                                       accum_out=acol(i, 2)), att_exp)
            if i >= 2 and (i - 2) % NTT == NTT - 1:
                h = (i - 2) // NTT
                act.wait_ge(pv_done, i - 1)
                S(nc.scalar.copy(z_a[:, 2 * H + h, 0:SEQ], BANKS[1][:]), bank_read[1])

        def vec_att(dve, i):
            v = nc.vector
            if 0 <= i - 1 < N_ATT:
                j = i - 1
                n = (j % NTT + 1) * P
                dve.wait_ge(att_exp, j + 1)
                V(v.reciprocal(acol(j, 3), acol(j, 2)))
                V(v.tensor_scalar(aw[:, j % 2, 0:n], aw[:, j % 2, 0:n], acol(j, 3), None, ALU.mult), att_p)
            if i < N_ATT:
                qt = i % NTT
                n = (qt + 1) * P
                bank = rd_bank(dve, 2 + i % 2)
                if i >= 2:
                    dve.wait_ge(p_turned, i - 1)
                bias = negm[:] if qt == 0 else selb[:, SEL[qt][0]:SEL[qt][1], :].rearrange("p a b -> p (a b)")
                V(v.tensor_tensor_reduce(aw[:, i % 2, 0:n], bank[:, 0:n], bias, 1.0, TAKEN, ALU.add, ALU.max, acol(i, 0)),
                  bank_read[2 + i % 2])
                V(v.tensor_scalar(acol(i, 1), acol(i, 0), -SCALE, None, ALU.mult), att_max)

        HB = H * B
        S64 = tiny[:, 104:168]
        spT = tiny[:, 104:200]
        qkn = iwb[:].rearrange("p b h -> p (b h)")
        sp = aw[0:HB, 0, 0:2 * P + 1]

        def pe_satt_rows(pe):
            pe.wait_ge(rows_found, 1)
            bank = pe_bank(pe, 2)
            for t in range(2):
                nc.tensor.transpose(bank[:, t * B:(t + 1) * B], rowf[:, t * P:(t + 1) * P], ident[0:B, 0:B])
            for t in range(2):
                m = nc.tensor.transpose(bank[:, (2 + t) * B:(3 + t) * B], maskf[:, t * P:(t + 1) * P], ident[0:B, 0:B])
            m.then_inc(bank_full[2], 1)

        def vec_satt_rows(dve):
            bank = rd_bank(dve, 2)
            V(nc.vector.tensor_copy(rowT[:].rearrange("p t b -> p (t b)"), bank[:, 0:2 * B]), rowT_ready)
            V(nc.vector.tensor_copy(maskT[:].rearrange("p t b -> p (t b)"), bank[:, 2 * B:4 * B]), bank_read[2])
            V(nc.vector.tensor_tensor(qkn.rearrange("p (h b) -> p h b", h=H), z_a[:, 0:H, SEQ:T], z_a[:, H:2 * H, SEQ:T],
                                      ALU.mult), qkn_ready)

        def pool_satt(pool):
            pool.wait_ge(rowT_ready, 1)
            for i, cache in enumerate((A["cache_k"], A["cache_v"])):
                table = cache[0].rearrange("n r h d -> (n r) (h d)")
                for b in range(B):
                    if i == 0 and b >= 2:
                        pool.wait_ge(k_used, 2 * (b - 1))
                    if i == 1:
                        if b < 2:
                            pool.wait_ge(k_used, 2 * (B - 1 + b))
                        else:
                            pool.wait_ge(v_used, b - 1)
                    for t in range(2):
                        nc.gpsimd.indirect_dma_start(skv[:, b % 2, t, :], None, table, bass.IndirectOffsetOnAxis(
                            ap=rowT[:, t, b:b + 1], axis=0)).then_inc(skv_full[b % 2], 16)

        kprod = reg("kprod", [P, 2, MIX], 24928)

        def pe_satt_k(pe, b):
            nc.tensor.matmul(pe_bank(pe, 2)[:], rowsel[:, b, :], sw[:], start=True, stop=True).then_inc(bank_full[2], 1)

        def vec_satt_k(dve, b):
            v = nc.vector
            dve.wait_ge(skv_full[b % 2], 32 * (b // 2 + 1))
            V(v.tensor_tensor(kprod[:], skv[:, b % 2], rd_bank(dve, 2).unsqueeze(1).to_broadcast([P, 2, MIX]), ALU.mult),
              bank_read[2])
            dve.sem_inc(k_used, 2)
            s = S64.rearrange("p (t h b) -> p t h b", t=2, h=H)[:, :, :, b]
            V(v.tensor_reduce(s, kprod[:].rearrange("p t (h d) -> p t h d", h=H), AX, ALU.add))
            V(v.tensor_tensor(s, s, maskT[:, :, b:b + 1].to_broadcast([P, 2, H]), ALU.add))
            dve.sem_inc(sx_a, 1)

        def pe_satt_soft(pe):
            pe.wait_ge(sx_a, B)
            bank = pe_bank(pe, 2)
            for t in range(2):
                nc.tensor.transpose(bank[0:HB, t * P:(t + 1) * P], S64[:, t * HB:(t + 1) * HB], ident[:])
            nc.tensor.matmul(bank[0:HB, 2 * P:2 * P + 1], qkn, ones[:, 0:1], start=True, stop=False)
            nc.tensor.matmul(bank[0:HB, 2 * P:2 * P + 1], own[:].rearrange("r h b -> r (h b)"), tiny[0:B, 40:41],
                             start=False, stop=True).then_inc(bank_full[2], 1)
            pe.wait_ge(sp_ready, 1)
            bank = pe_bank(pe, 3)
            for t in range(2):
                nc.tensor.transpose(bank[:, t * HB:(t + 1) * HB], sp[:, t * P:(t + 1) * P], ident[0:HB, 0:HB])
            nc.tensor.matmul(bank[:, 2 * HB:3 * HB], aw[0:HB, 1, 0:P], ident[0:HB, 0:HB], start=True,
                             stop=True).then_inc(bank_full[3], 1)

        def act_satt_soft(act):
            act.wait_ge(sp_max, 1)
            S(nc.scalar.activation(sp, sp, ACT.Exp, bias=tiny[0:HB, 9:10], scale=SCALE, accum_out=tiny[0:HB, 10:11]), sp_exp)

        def vec_satt_soft(dve):
            v = nc.vector
            V(v.tensor_copy(sp, rd_bank(dve, 2)[0:HB, 0:2 * P + 1]), bank_read[2])
            V(v.tensor_reduce(tiny[0:HB, 8:9], sp, AX, ALU.max))
            V(v.tensor_scalar(tiny[0:HB, 9:10], tiny[0:HB, 8:9], -SCALE, None, ALU.mult), sp_max)
            dve.wait_ge(sp_exp, 1)
            V(v.reciprocal(tiny[0:HB, 11:12], tiny[0:HB, 10:11]))
            V(v.tensor_scalar(sp, sp, tiny[0:HB, 11:12], None, ALU.mult))
            V(v.tensor_copy(aw[0:HB, 1, 0:P], sp[:, 2 * P:2 * P + 1].to_broadcast([HB, P])), sp_ready)
            V(v.tensor_copy(spT, rd_bank(dve, 3)[:, 0:3 * HB]), bank_read[3])
            dve.sem_inc(spT_ready, 1)

        def pe_satt_v(pe, b):
            if b == 0:
                pe.wait_ge(spT_ready, 1)
            bank = pe_bank(pe, 1) if b == 0 else BANKS[1]
            pe.wait_ge(skv_full[b % 2], 32 * (B // 2 + b // 2 + 1))
            for h in range(H):
                for t in range(2):
                    j = h * B + b
                    m = nc.tensor.matmul(bank[:, j:j + 1], skv[:, b % 2, t, h * DH:(h + 1) * DH],
                                         spT[:, t * HB + j:t * HB + j + 1], start=(t == 0), stop=(t == 1))
            m.then_inc(v_used, 1)

        def vec_satt_v(dve):
            ys = z_a[:, 2 * H:3 * H, SEQ:T]
            V(nc.vector.tensor_tensor(ys, ys, spT[:, 2 * HB:3 * HB].rearrange("p (h b) -> p h b", h=H), ALU.mult))
            dve.wait_ge(yv_ready, 1)
            V(nc.vector.tensor_tensor(ys, ys, S64[:, 0:HB].rearrange("p (h b) -> p h b", h=H), ALU.add))

        def act_satt_v(act):
            act.wait_ge(v_used, B)
            S(nc.scalar.copy(S64[:, 0:HB], BANKS[1][:, 0:HB]), bank_read[1])
            act.sem_inc(yv_ready, 1)

        ab = reg("ab", [P, 2, NTT, H], 25952)
        wcol = reg("wcol", [P, 2, NTT], 25984)
        nml = reg("nml", [P, 1], 25992)
        sg_s = reg("sg_s", [P, H, B], 26000)
        Qb = reg("Qb", [P, 4, H, B], 26032)
        cq = reg("cq", [P, H, B], 26160)
        sx = reg("sx", [P, 4, HB], 26192)
        s8 = reg("s8", [B, 16, H], 26320)
        qm = reg("qm", [B, 4, H, B], 26384)
        rows = reg("rows", [H, 3, SEQ], 26976)
        mb, em, md = (reg(x, [P, SEQ], 12416 + 512 * i) for i, x in enumerate(("mb", "em", "md")))
        dd = reg("dd", [P, 2, SEQ], 13952)
        wv = reg("wv", [P, NTT, DH], 14976)
        dn = reg("dn", [P, SEQ], 15488)
        hb = reg("hb", [P, SEQ], 16000)
        hsq = reg("hsq", [P, SEQ], 20704)
        hrs = reg("hrs", [P, SEQ], 21216)
        sg_e = reg("sg_e", [P, T], 21728)
        cst = reg("cst", [P, 2, DH], 22752)
        nst = reg("nst", [1, H, DH], 23008)

        def pe_ml_prep(pe):
            bank = pe_bank(pe, 2)
            for c in range(NTT):
                for e in range(c + 1):
                    m = nc.tensor.matmul(bank[:, c * H:(c + 1) * H], ones[:] if e < c else tri[:], gt[:, e, H:2 * H],
                                         start=(e == 0), stop=(e == c))
            m.then_inc(bank_full[2], 1)
            pe.wait_ge(ab_ready, 1)
            for i in range(2):
                bank = pe_bank(pe, 0)
                for c in range(NTT):
                    m = nc.tensor.transpose(bank[0:H, c * P:(c + 1) * P], ab[:, i, c, :], ident[:])
                m.then_inc(bank_full[0], 1)

        def act_ml_prep(act):
            for i in range(2):
                S(nc.scalar.copy(rows[:, i], rd_bank(act, 0)[0:H, :]), bank_read[0])
            act.sem_inc(arow_ready, 1)

        def vec_ml_prep(dve):
            v = nc.vector
            for i in range(2):
                dve.wait_ge(rt_stored[i], 32)
            V(v.tensor_copy(ab[:, 1].rearrange("p c h -> p (c h)"), rd_bank(dve, 2)[:, 0:NTT * H]), bank_read[2])
            V(v.tensor_tensor(ab[:, 0], gt[:, 0:NTT, 0:H], ab[:, 1], ALU.subtract), ab_ready)
            dve.wait_ge(arow_ready, 1)
            V(v.tensor_tensor_scan(rows[:, 2], rows[:, 0], rows[:, 0], 0.0, ALU.max, ALU.max))
            V(v.tensor_tensor(rows[:, 1], rows[:, 1], rows[:, 2], ALU.add), mrow_ready)

        def pe_ml_rows(pe, h):
            pe.wait_ge(mrow_ready, 1)
            for i, r in enumerate((2, 1)):
                nc.tensor.matmul(pe_bank(pe, i)[:], rowsel[0:H, h, :], rows[:, r], start=True,
                                 stop=True).then_inc(bank_full[i], 1)

        def pe_ml(pe, h):
            if h == 0:
                pe_ml_rows(pe, 0)
            nd = PJ[h % 2]
            for st in range(NTT + 1):
                if st < NTT:
                    n = SEQ - st * P
                    nc.tensor.matmul(pe_bank(pe, 2 + st % 2)[:, 0:n], z_m[:, H + h, st * P:(st + 1) * P],
                                     z_m[:, h, st * P:SEQ], start=True, stop=True).then_inc(bank_full[2 + st % 2], 1)
                if st >= 1:
                    s = st - 1
                    n = SEQ - s * P
                    if s == 0 and h >= 2:
                        pe.wait_ge(h_ready, h - 1)
                    pe.wait_ge(wd_ready, NTT * h + s + 1)
                    nc.tensor.matmul(nd[:, 0, s * P:SEQ], mv_tok[:, s, h * DH:(h + 1) * DH], dd[:, s % 2, 0:n],
                                     start=(s == 0), stop=(s == NTT - 1))
                    nc.tensor.matmul(nd[:, 1, s * P:SEQ], ones[:], dd[:, s % 2, 0:n],
                                     start=(s == 0), stop=(s == NTT - 1)).then_inc(nd_done, 1)
            pe.wait_ge(wv_ready, h + 1)
            bank = pe_bank(pe, 0)
            for c in range(NTT):
                m = nc.tensor.matmul(bank[:, 0:DH], wv[:, c, :], mk_tok[:, c, h * DH:(h + 1) * DH],
                                     start=(c == 0), stop=(c == NTT - 1))
            m.then_inc(bank_full[0], 1)
            bank = pe_bank(pe, 1)
            for c in range(NTT):
                m = nc.tensor.matmul(bank[0:1, 0:DH], wcol[:, 1, c:c + 1], mk_tok[:, c, h * DH:(h + 1) * DH],
                                     start=(c == 0), stop=(c == NTT - 1))
            m.then_inc(bank_full[1], 1)
            if h < H - 1:
                pe_ml_rows(pe, h + 1)
            pe.wait_ge(hsq_ready, h + 1)
            nc.tensor.matmul(pe_bank(pe, 0)[:], ones[:], hsq[:], start=True, stop=True).then_inc(bank_full[0], 1)

        def act_ml_m(act):
            S(nc.scalar.copy(mb[:], rd_bank(act, 0)[:]), bank_read[0])
            act.sem_inc(mb_ready, 1)

        def act_ml_em(act):
            S(nc.scalar.activation(em[:], rd_bank(act, 1)[:], ACT.Exp, scale=-1.0), bank_read[1])
            act.sem_inc(em_ready, 1)

        def act_ml(act, h):
            a = nc.scalar
            if h == 0:
                act.wait_ge(qkn_ready, 1)
                act_ml_m(act)
                act_ml_em(act)
            act.wait_ge(md_ready, h + 1)
            S(a.activation(wcol[:, 0, :], ab[:, 0, :, h], ACT.Exp, bias=nml[:]))
            for st in range(NTT):
                j = NTT * h + st
                if j >= 2:
                    act.wait_ge(nd_done, j - 1)
                bias = ab[:, 0, st, h:h + 1]
                S(a.activation(dd[:, st % 2, 0:P], md[:, st * P:(st + 1) * P], ACT.Exp, bias=bias, scale=-1.0))
                if st < NTT - 1:
                    S(a.activation(dd[:, st % 2, P:SEQ - st * P], mb[:, (st + 1) * P:SEQ], ACT.Exp, bias=bias, scale=-1.0))
                act.sem_inc(dd_ready, 1)
            if h >= 1:
                act.wait_ge(ym_ready, h)
            S(a.activation(sg_e[:], z_m[:, 3 * H + h, :], ACT.Exp, scale=-1.0))
            S(a.activation(sg_e[:], sg_e[:], ACT.Ln, bias=ones[:, 0:1]))
            S(a.activation(sg_e[:], sg_e[:], ACT.Exp, scale=-1.0), sig_exp)
            if h >= 2:
                act.wait_ge(c_stored[h % 2], 16 * (h // 2))
            S(a.copy(cst[:, h % 2], rd_bank(act, 0)[:, 0:DH]), bank_read[0])
            act.dma_start(O["p_c"][0, 0, h], cst[:, h % 2]).then_inc(c_stored[h % 2], 16)
            S(a.copy(nst[:, h], rd_bank(act, 1)[0:1, 0:DH]), bank_read[1])
            act.wait_ge(dn_ready, h + 1)
            S(a.activation(dn[:], dn[:], ACT.Ln))
            S(a.activation(dn[:], dn[:], ACT.Exp, scale=-1.0), rden_ready)
            if h < H - 1:
                act_ml_m(act)
            act.wait_ge(h_ready, h + 1)
            S(a.activation(hsq[:], hb[:], ACT.Square), hsq_ready)
            if h < H - 1:
                act_ml_em(act)
            S(a.activation(hrs[:], rd_bank(act, 0)[:], ACT.Ln, bias=epsc[:], scale=1.0 / DH), bank_read[0])
            S(a.activation(hrs[:], hrs[:], ACT.Exp, scale=-0.5), hrs_ready)

        def vec_ml_m(dve, h):
            v = nc.vector
            dve.wait_ge(mb_ready, h + 1)
            V(v.tensor_tensor(md[:].rearrange("p (c t) -> p c t", c=NTT), mb[:].rearrange("p (c t) -> p c t", c=NTT),
                              posm[:].unsqueeze(1).to_broadcast([P, NTT, P]), ALU.add))
            V(v.tensor_scalar(nml[:], mb[:, SEQ - 1:SEQ], -1.0, None, ALU.mult), md_ready)

        def vec_ml(dve, h):
            v = nc.vector
            if h == 0:
                vec_ml_m(dve, 0)
            for st in range(NTT):
                n = SEQ - st * P
                dve.wait_ge(dd_ready, NTT * h + st + 1)
                V(v.scalar_tensor_tensor(dd[:, st % 2, 0:n], rd_bank(dve, 2 + st % 2)[:, 0:n], SCALE, dd[:, st % 2, 0:n],
                                         ALU.mult, ALU.mult), bank_read[2 + st % 2])
                dve.sem_inc(wd_ready, 1)
                if st == 1:
                    V(v.tensor_scalar(wcol[:, 1], wcol[:, 0], SCALE, None, ALU.mult))
                    V(v.tensor_tensor(wv[:], mv_tok[:, :, h * DH:(h + 1) * DH],
                                      wcol[:, 1].unsqueeze(2).to_broadcast([P, NTT, DH]), ALU.mult), wv_ready)
            dve.wait_ge(sig_exp, h + 1)
            V(v.tensor_copy(sg_s[:, h], sg_e[:, SEQ:T]))
            dve.wait_ge(em_ready, h + 1)
            dve.wait_ge(nd_done, NTT * (h + 1))
            V(v.tensor_tensor(dn[:], PJ[h % 2][:, 1, :], em[:], ALU.max))
            V(v.scalar_tensor_tensor(dn[:], PJ[h % 2][:, 1, :], -1.0, dn[:], ALU.mult, ALU.max), dn_ready)
            dve.wait_ge(rden_ready, h + 1)
            V(v.tensor_tensor(hb[:], PJ[h % 2][:, 0, :], dn[:], ALU.mult), h_ready)
            if h < H - 1:
                vec_ml_m(dve, h + 1)
            dve.wait_ge(hrs_ready, h + 1)
            y = z_m[:, 3 * H + h, 0:SEQ]
            V(v.scalar_tensor_tensor(y, hb[:], gains[:, G_ML + h:G_ML + h + 1], hrs[:], ALU.mult, ALU.mult))
            V(v.tensor_tensor(y, y, sg_e[:, 0:SEQ], ALU.mult), ym_ready)

        cb = reg("cb", [P, 2, H, DH], 20704)
        ct = reg("ct", [P, 2, H, DH], 21728)
        sn = reg("sn", [B, 2, H, DH], 12416)
        sm = reg("sm", [B, H], 23776)

        def sync_mls(sp):
            for b in range(B):
                if b == 2:
                    sync_reload(sp)
                if b >= 2:
                    sp.wait_ge(sc_stored[b % 2], 16 * (b // 2))
                else:
                    sp.wait_ge(ym_ready, H)
                sp.dma_start(cb[:, b % 2], A["state_mlstm_c"][0, b].rearrange("h e d -> e h d")).then_inc(cs_slot[b % 2], 16)

        c_stored, sc_stored = ([sem(f"{n}{i}") for i in range(2)] for n in ("c_stored", "sc_stored"))
        cs_slot = [sem("cs_slot0"), sem("cs_slot1")]

        def act_mls_load(act):
            act.wait_ge(ym_ready, H)
            act.dma_start(sn[:, 0], A["state_mlstm_n"][0]).then_inc(cs_in, 16)
            act.dma_start(sm[:], A["state_mlstm_m"][0]).then_inc(cs_in, 16)

        def pe_mls(pe):
            pe.wait_ge(qm_ready, 1)
            nc.tensor.matmul(pe_bank(pe, 2)[:, 0:4 * HB], ones[0:B, :], qm[:].rearrange("r q h b -> r (q h b)"),
                             start=True, stop=True).then_inc(bank_full[2], 1)
            for b in range(B):
                for i in range(2):
                    nc.tensor.matmul(pe_bank(pe, 2 + i)[:], rowsel[:, b, :], s_tok[:, 1 + i, :], start=True,
                                     stop=True).then_inc(bank_full[2 + i], 1)
                pe_satt_v(pe, b)
            pe.wait_ge(sst_ready, 1)
            nc.tensor.matmul(pe_bank(pe, 0)[:, 0:HB], ones[:], sx[:, 1], start=True, stop=True).then_inc(bank_full[0], 1)

        def vec_mls(dve):
            v = nc.vector
            dve.wait_ge(cs_in, 32)
            li, lf = gt[0:B, NTT, 0:H], gt[0:B, NTT, H:2 * H]
            bc = lambda x: x.unsqueeze(2).to_broadcast([B, H, DH])
            heads = lambda x: x.rearrange("b (h d) -> b h d", h=H)
            q, k = heads(s_tok[:, 1]), heads(s_tok[:, 2])
            V(v.tensor_tensor(s8[:, 0], lf, sm[:], ALU.add))
            V(v.tensor_tensor(s8[:, 1], s8[:, 0], li, ALU.max), n_ready)
            V(v.tensor_tensor(s8[:, 4], s8[:, 0], s8[:, 1], ALU.subtract))
            V(v.tensor_tensor(s8[:, 5], li, s8[:, 1], ALU.subtract))
            V(v.tensor_scalar(s8[:, 6], s8[:, 1], -1.0, None, ALU.mult), sx_b)
            V(v.tensor_tensor(sn[:, 1], q, k, ALU.mult))
            V(v.tensor_reduce(s8[:, 7], sn[:, 1], AX, ALU.add))
            V(v.tensor_tensor(sn[:, 1], q, sn[:, 0], ALU.mult))
            V(v.tensor_reduce(s8[:, 8], sn[:, 1], AX, ALU.add))
            dve.wait_ge(shs_ready, 1)
            V(v.tensor_scalar(s8[:, 5], s8[:, 5], SCALE, None, ALU.mult))
            V(v.tensor_tensor(s8[:, 9], s8[:, 7], s8[:, 5], ALU.mult))
            V(v.tensor_tensor(s8[:, 10], s8[:, 8], s8[:, 4], ALU.mult))
            V(v.tensor_tensor(s8[:, 10], s8[:, 10], s8[:, 9], ALU.add))
            V(v.scalar_tensor_tensor(s8[:, 10], s8[:, 10], -1.0, s8[:, 10], ALU.mult, ALU.max))
            V(v.tensor_tensor(s8[:, 10], s8[:, 10], s8[:, 6], ALU.max))
            V(v.reciprocal(s8[:, 10], s8[:, 10]))
            V(v.tensor_tensor(s8[:, 11], s8[:, 9], s8[:, 10], ALU.mult))
            V(v.tensor_tensor(s8[:, 12], s8[:, 4], s8[:, 10], ALU.mult))
            for i, c in enumerate((4, 5, 11, 12)):
                V(v.tensor_tensor(qm[:, i], own[:], s8[:, c].unsqueeze(2).to_broadcast([B, H, B]), ALU.mult),
                  qm_ready if i == 3 else None)
            V(v.tensor_tensor(sn[:, 0], sn[:, 0], bc(s8[:, 4]), ALU.mult))
            V(v.tensor_tensor(sn[:, 1], k, bc(s8[:, 5]), ALU.mult))
            V(v.tensor_tensor(sn[:, 0], sn[:, 0], sn[:, 1], ALU.add), n_ready)
            V(v.tensor_copy(Qb[:].rearrange("p q h b -> p (q h b)"), rd_bank(dve, 2)[:, 0:4 * HB]), bank_read[2])
            vT = z_m[:, 2 * H:3 * H, SEQ:T]
            vw = sx[:, 3].rearrange("p (h b) -> p h b", h=H)
            V(v.tensor_tensor(vw, vT, Qb[:, 1], ALU.mult))
            cbc = lambda x: x.unsqueeze(2).to_broadcast([P, H, DH])
            for b in range(B):
                c = cb[:, b % 2]
                dve.wait_ge(cs_slot[b % 2], 16 * (b // 2 + 1))
                V(v.tensor_tensor(ct[:, 0], c, rd_bank(dve, 2)[:].rearrange("p (h d) -> p h d", h=H), ALU.mult), bank_read[2])
                V(v.tensor_reduce(cq[:, :, b], ct[:, 0], AX, ALU.add))
                V(v.tensor_tensor(c, c, cbc(Qb[:, 0, :, b]), ALU.mult))
                V(v.tensor_tensor(ct[:, 1], rd_bank(dve, 3)[:].rearrange("p (h d) -> p h d", h=H), cbc(vw[:, :, b]),
                                  ALU.mult), bank_read[3])
                V(v.tensor_tensor(c, c, ct[:, 1], ALU.add), sc_in)
            sh = sx[:, 0].rearrange("p (h b) -> p h b", h=H)
            V(v.tensor_tensor(cq[:], cq[:], Qb[:, 3], ALU.mult))
            V(v.tensor_tensor(sh, vT, Qb[:, 2], ALU.mult))
            V(v.tensor_tensor(sh, sh, cq[:], ALU.add))
            V(v.tensor_tensor(sx[:, 1], sx[:, 0], sx[:, 0], ALU.mult), sst_ready)
            dve.wait_ge(shs_ready, 2)
            V(v.tensor_tensor(sx[:, 0], sx[:, 0], sx[:, 2], ALU.mult))
            V(v.tensor_tensor(sh, sh, gains[:, G_ML:G_ML + H].unsqueeze(2).to_broadcast([P, H, B]), ALU.mult))
            V(v.tensor_tensor(z_m[:, 3 * H:4 * H, SEQ:T], sh, sg_s[:], ALU.mult))

        def act_mls_store(act):
            act.dma_start(O["p_n"][0, 0].rearrange("(o h) d -> o h d", o=1), nst[:]).then_inc(stores, 16)
            act.dma_start(O["p_m"][0, 0].rearrange("(h o) -> h o", o=1), rows[:, 1, SEQ - 1:SEQ]).then_inc(stores, 16)
            act.wait_ge(n_ready, 2)
            act.dma_start(O["s_m"][0], s8[:, 1]).then_inc(stores, 16)
            act.dma_start(O["s_n"][0], sn[:, 0]).then_inc(stores, 16)
            for b in range(B):
                act.wait_ge(sc_in, b + 1)
                act.dma_start(O["s_c"][0, b].rearrange("h e d -> e h d"), cb[:, b % 2]).then_inc(sc_stored[b % 2], 16)

        def y_tile(k):
            return z_m[:, 3 * H + k, :] if k < H else z_a[:, 2 * H + k - H, :]

        def act_split_y(act):
            act.wait_ge(ya_ready, 1)
            act.wait_ge(w_used[0], BASE0)
            for k in range(KT):
                S(nc.scalar.copy(ahi[:, k], y_tile(k)), y_hi)

        def vec_split_y(dve):
            for k in range(KT):
                dve.wait_ge(y_hi, k + 1)
                V(nc.vector.tensor_tensor(alo[:, k], y_tile(k), ahi[:, k].bitcast(F32), ALU.subtract), y_lo)

        def pe_mixers(pe):
            for i in range(ATT_FIRST, N_ATT + 2):
                pe_att(pe, i)
            pe_sidx_merge(pe)
            pe_satt_rows(pe)
            for h in range(H):
                pe_ml(pe, h)
                for b in range(2 * h, 2 * h + 2):
                    pe_satt_k(pe, b)
            pe_satt_soft(pe)
            pe_mls(pe)

        def act_mixers(act):
            for i in range(ATT_FIRST, N_ATT + 2):
                act_att(act, i)
            for h in range(H):
                act_ml(act, h)
            act_mls_load(act)
            act_satt_soft(act)
            act_mls_first(act)
            act_mls_store(act)
            act_satt_v(act)
            act_mls_last(act)
            act_split_y(act)

        def act_mls_first(act):
            act.wait_ge(sx_b, 1)
            S(nc.scalar.activation(s8[:, 4:7].rearrange("b q h -> b (q h)"), s8[:, 4:7].rearrange("b q h -> b (q h)"),
                                   ACT.Exp), shs_ready)

        def act_mls_last(act):
            S(nc.scalar.activation(sx[:, 2], rd_bank(act, 0)[:, 0:HB], ACT.Ln, bias=epsc[:], scale=1.0 / DH), bank_read[0])
            S(nc.scalar.activation(sx[:, 2], sx[:, 2], ACT.Exp, scale=-0.5), shs_ready)

        def vec_mixers(dve):
            for i in range(ATT_FIRST, N_ATT + 2):
                vec_att(dve, i)
                if i - ATT_FIRST < len(ROUNDS):
                    vec_rounds(dve, ROUNDS[i - ATT_FIRST])
            vec_sidx(dve)
            vec_satt_rows(dve)
            for h in range(H):
                vec_ml(dve, h)
                for b in range(2 * h, 2 * h + 2):
                    vec_satt_k(dve, b)
            vec_satt_soft(dve)
            vec_mls(dve)
            vec_satt_v(dve)
            dve.sem_inc(ya_ready, 1)
            vec_split_y(dve)


        FREE = 15600
        gHi = reg("gHi", [P, NFT, T], 0, F32R)
        gLo = reg("gLo", [P, NFT, T], FREE, F32R)
        xT = reg("xT", [P, KT, T], 11440)
        qT = reg("qT", [P, KT, T], 0)
        oT = reg("oT", [P, KT, T], 4160)
        px = reg("px", [P, 2, NMEM], 9344)
        pT = reg("pT", [P, 2, SEQ], 9856)
        x_re = [reg(f"x_re{i}", [P, D], o) for i, o in enumerate((8320, 9344, 10368, 24928))]
        xs_re = reg("xs_re", [B, D], 32624)
        mem_in = reg("mem_in", [P, 2, D], 13440)
        mem_sq = reg("mem_sq", [P, 2, D], FREE)
        memT = reg("memT", [P, KT, NMEM], FREE + 2048)
        hmhi = reg("hmhi", [P, KT, NMEM], FREE + 4096, F32R)
        hmlo = reg("hmlo", [P, KT, NMEM], FREE + 6144, F32R)
        ckv = [reg(f"ckv{i}", [P, 2, D], o) for i, o in enumerate((FREE, FREE + 2048, FREE + 4096, 32576))]
        prod = reg("prod", [P, 2, D], 23792)
        qs_tok = reg("qs_tok", [B, D], FREE + 6144)
        xS = reg("xS", [P, 2, H, B], FREE + 7168)
        xSm = reg("xSm", [P, B, 2, HB], 8320)
        xO = reg("xO", [HB, 2, SEQ], FREE + 6144)
        xp = reg("xp", [HB, NMEM], FREE + 7232)
        qs = reg("qs", [P, KT, B], FREE + 7488)
        mk_t = reg("mk_t", [P, 2, D], 23792)
        mv_t = reg("mv_t", [P, 2, D], 25840)
        mkT = reg("mkT", [P, KT, NMEM], 27888)
        hs2 = reg("hs2", [P, 2, T], 29936)
        rstd2 = reg("rstd2", [P, T], 30976)
        sq2 = reg("sq2", [P, 2, T], 31496)
        kvT = reg("kvT", [P, 2, NMEM], 10880)
        rq = reg("rq", [P, 5, H], 32536)
        xc = reg("xc", [P, 16], 32560)
        hist_rows = reg("hist_rows", [2 * B, 2 * DFF], FREE)
        ub = reg("ub", [P, 2, 2 + T], 27040)
        cc = reg("cc", [P, 2, T], 28088)
        gl = reg("gl", [P, T], 29128)
        hist = reg("hist", [P, 2 * NFT, B, 2], 32704)
        ulast = reg("ulast", [P, 2 * NFT, 2 + B], 33408)
        y_tok = reg("y_tok", [P, NTT, D], 27040)
        ys_tok = reg("ys_tok", [B, D], 31136)
        conv_rows = nc.alloc_sbuf_tensor_at("conv_rows", [2 + B, 2 * DFF], F32, offset=ahi_at)

        (mix_stored, xm_in, memT_ready, ck_ss, ck_rstd, mk_ready, kn_ready, qsq_used, rq_ready,
         xa_max, xa_exp, xa_p, xa_turned, xa_done, xa_read, qs_ready, qst_ready, qsn_ready, xs_max, xs_exp, xs_p, xsT_ready,
         xs_scored, xs_used, xo_ready, o_ready, hist_in, u_free, c_ready, gelu_done, g_lo,
         kvT_ready, kv_turned, up_step, y_ready, out_stores, mem_stored, h_zero) = (sem(x) for x in (
             "mix_stored xm_in memT_ready ck_ss ck_rstd mk_ready kn_ready qsq_used rq_ready "
             "xa_max xa_exp xa_p xa_turned xa_done xa_read qs_ready qst_ready qsn_ready xs_max xs_exp xs_p xsT_ready "
             "xs_scored xs_used xo_ready o_ready hist_in u_free c_ready gelu_done g_lo "
             "kvT_ready kv_turned up_step y_ready out_stores mem_stored h_zero").split())
        ckv_full = [sem(f"ckv_full{i}") for i in range(4)]

        PAIRS = [("out", 4), ("ck", 4), ("cv", 4), ("cq", 4), ("co", 4), ("up", NFT), ("down", 12)]
        BASE, at = {}, (BASE0, N_IN - BASE0)
        for stage, n in PAIRS:
            BASE[stage] = at
            at = (at[0] + n, at[1] + n)
        N_PAIRS = sum(n for _, n in PAIRS)

        def sp_stream(sp, stage, start=0):
            w = A["w_" + stage][0].rearrange("(k p) c -> p k c", p=P)
            base = BASE[stage]
            with sp.Fori(start + 1, dict(PAIRS)[stage] + 1) as i:
                for s in range(2):
                    sp.wait_ge(split_full[s], i + (base[s] - 1))
                    col = i * P + ((1 - s) * DFF - P) if stage == "up" else i * (2 * P) + (s * P - 2 * P)
                    sp.dma_start(raw[:, s], w[:, :, bass.ds(col, P)]).then_inc(raw_full[s], 16)

        def act_split(act, s, u):
            act.wait_ge(raw_full[s], (u + 1) * 16)
            act.wait_ge(w_used[s], u)
            nc.scalar.copy(whi[:, s], raw[:, s]).then_inc(hi_full[s], 1)

        def act_proj(act, stage, evac=None):
            base = BASE[stage]
            with act.Fori(0, dict(PAIRS)[stage]) as i:
                for s in range(2):
                    if evac is not None:
                        act_split(act, s, i + (base[s] + 1))
                        evac(i, s)
                    else:
                        act_split(act, s, i + (base[s] + 1))

        def pool_split(pool, i):
            for s in range(2):
                pool.wait_ge(hi_full[s], i + (BASE["out"][s] + 1))
                nc.gpsimd.tensor_tensor(wlo[:, s], raw[:, s], whi[:, s].bitcast(F32), ALU.subtract).then_inc(split_full[s], 1)

        def pe_mem_proj(pe, stage):
            base, v = BASE[stage], (0, 4)[stage == "cv"]
            with pe.Fori(0, dict(PAIRS)[stage]) as i:
                for s in range(2):
                    pe.wait_ge(split_full[s], i + (base[s] + 1))
                    pe.wait_ge(out_free[s], i + base[s])
                    for k in range(KT):
                        for j, (w, x) in enumerate(((whi, hmhi), (whi, hmlo), (wlo, hmhi))):
                            m = nc.tensor.matmul(PJ[s][:, 0, 0:NMEM], w[:, s, k, :], x[:, k, :],
                                                 start=(k == 0 and j == 0), stop=(k == KT - 1 and j == 2))
                    m.then_inc(w_used[s], 1)
                for s in range(2):
                    pe.wait_ge(kvT_ready, i * 2 + (2 * v + s + 1))
                    for mt in range(2):
                        m = nc.tensor.transpose(PJ[s][:, 1, mt * P:(mt + 1) * P], kvT[:, s, mt * P:(mt + 1) * P], ident[:])
                    m.then_inc(kv_turned, 1)

        def act_mem_proj(act, stage, dst):
            base, v = BASE[stage], (0, 4)[stage == "cv"]
            with act.Fori(0, dict(PAIRS)[stage]) as i:
                for s in range(2):
                    act.wait_ge(w_used[s], i + (base[s] + 1))
                    act.wait_ge(kv_turned, i * 2 + 2 * v)
                    nc.scalar.copy(kvT[:, s], PJ[s][:, 0, 0:NMEM]).then_inc(kvT_ready, 1)
                    act_split(act, s, i + (base[s] + 1))
                for s in range(2):
                    act.wait_ge(kv_turned, i * 2 + (2 * v + s + 1))
                    nc.scalar.copy(dst[:, :, bass.ds(i * (2 * P) + s * P, P)],
                                   PJ[s][:, 1, 0:NMEM].rearrange("p (t f) -> p t f", t=2)).then_inc(out_free[s], 1)

        def pe_pair(pe, stage, i, between=None):
            base = BASE[stage]
            for s in range(2):
                pe.wait_ge(split_full[s], i + (base[s] + 1))
                pe.wait_ge(out_free[s], i + base[s])
                pe_product(s, PJ[s], P, KT, ahi, alo).then_inc(w_used[s], 1)
                if s == 0 and between is not None:
                    between(i)

        def pe_proj(pe, stage, start=0, between=None):
            with pe.Fori(start, dict(PAIRS)[stage]) as i:
                pe_pair(pe, stage, i, between)

        def vec_residual(dve, stage):
            base = BASE[stage]
            with dve.Fori(0, dict(PAIRS)[stage]) as i:
                for s in range(2):
                    dve.wait_ge(w_used[s], i + (base[s] + 1))
                    x = xT[:, bass.ds(i * 2 + s, 1), :].rearrange("p o (a b) -> p (o a) b", a=2)
                    nc.vector.tensor_tensor(x, x, PJ[s][:, :, 0:HALF], ALU.add).then_inc(out_free[s], 1)

        def stage_done(eng, stage, sems_):
            for s in range(2):
                eng.wait_ge(sems_[s], BASE[stage][s] + dict(PAIRS)[stage])

        def act_norm(act, stage, src, width, hi):
            for k in range(KT):
                act.wait_ge(sq_used, KT * stage + k - 1 if k >= 2 else KT * stage)
                nc.scalar.activation(sq2[:, k % 2, 0:width], src[:, k, 0:width], ACT.Square).then_inc(sq_ready, 1)
            act_rstd(act, stage, rstd2, width, D)
            for k in range(KT):
                act.wait_ge(hs_ready, KT * stage + k + 1)
                nc.scalar.copy(hi[:, k, 0:width], hs2[:, k % 2, 0:width]).then_inc(nhi_ready, 1)

        def pe_turn_in(pe):
            pe.wait_ge(xm_in, 16 * 6)
            for k in range(KT):
                bank = pe_bank(pe, 2 + k % 2)
                for mt in range(2):
                    m = nc.tensor.transpose(bank[:, mt * P:(mt + 1) * P], mem_in[:, mt, k * P:(k + 1) * P], ident[:])
                m.then_inc(bank_full[2 + k % 2], 1)
            for k in range(KT):
                bank = pe_bank(pe, 2 + k % 2)
                for tt in range(NTT):
                    m = nc.tensor.transpose(bank[:, tt * P:(tt + 1) * P], x_re[tt][:, k * P:(k + 1) * P], ident[:])
                m.then_inc(bank_full[2 + k % 2], 1)
            bank = pe_bank(pe, 2)
            for k in range(KT):
                m = nc.tensor.transpose(bank[:, k * B:(k + 1) * B], xs_re[:, k * P:(k + 1) * P], ident[0:B, 0:B])
            m.then_inc(bank_full[2], 1)
            for k in range(KT):
                pe_sumsq(pe, 1, k, sq2, NMEM)

        def vec_turn_in(dve):
            v = nc.vector
            dve.wait_ge(mix_stored, 1)
            for k in range(KT):
                V(v.tensor_copy(memT[:, k], rd_bank(dve, 2 + k % 2)[:, 0:NMEM]), bank_read[2 + k % 2])
                dve.sem_inc(memT_ready, 1)
            for k in range(KT):
                V(v.tensor_copy(xT[:, k, 0:SEQ], rd_bank(dve, 2 + k % 2)), bank_read[2 + k % 2])
            V(v.tensor_copy(xT[:, :, SEQ:T], rd_bank(dve, 2)[:, 0:KT * B].rearrange("p (k b) -> p k b", k=KT)), bank_read[2])

        def vec_mem_keys(dve):
            v = nc.vector
            stage_done(dve, "ck", out_free)
            k4 = mk_t[:].rearrange("p t (h d) -> p (t h) d", h=H)
            q4 = mem_sq[:].rearrange("p t (h d) -> p (t h) d", h=H)
            V(v.tensor_tensor(q4, k4, k4, ALU.mult))
            V(v.tensor_reduce(xc[:, 0:8], q4, AX, ALU.add), ck_ss)
            dve.wait_ge(ck_rstd, 1)
            V(v.tensor_tensor(k4, k4, xc[:, 0:8].unsqueeze(2).to_broadcast([P, 8, 2 * DH]), ALU.mult))
            V(v.tensor_tensor(k4, k4, ckg[:].unsqueeze(1).to_broadcast([P, 8, 2 * DH]), ALU.mult), mk_ready)
            for f in range(KT):
                V(v.tensor_scalar(mkT[:, f], rd_bank(dve, 2 + f % 2)[:, 0:NMEM], gains[:, G_CQ + f % 2:G_CQ + f % 2 + 1], None,
                                  ALU.mult), bank_read[2 + f % 2])
                dve.sem_inc(kn_ready, 1)

        def act_mem_keys(act):
            act.wait_ge(ck_ss, 1)
            S(nc.scalar.activation(xc[:, 0:8], xc[:, 0:8], ACT.Ln, bias=epsc[:], scale=1.0 / (2 * DH)))
            S(nc.scalar.activation(xc[:, 0:8], xc[:, 0:8], ACT.Exp, scale=-0.5), ck_rstd)

        def pe_mem_keys(pe):
            pe.wait_ge(mk_ready, 1)
            for f in range(KT):
                bank = pe_bank(pe, 2 + f % 2)
                for mt in range(2):
                    m = nc.tensor.transpose(bank[:, mt * P:(mt + 1) * P], mk_t[:, mt, f * P:(f + 1) * P], ident[:])
                m.then_inc(bank_full[2 + f % 2], 1)

        def act_query(act):
            def evac(i, s):
                nc.scalar.copy(qT[:, bass.ds(i * 2 + s, 1), :].rearrange("p o (a b) -> p (o a) b", a=2), PJ[s][:, :, 0:HALF])
                act.wait_ge(qsq_used, i)
                nc.scalar.activation(sq2[:, s].rearrange("p (a b) -> p a b", a=2), PJ[s][:, :, 0:HALF],
                                     ACT.Square).then_inc(out_free[s], 1)
            act_proj(act, "cq", evac)
            bank = rd_bank(act, 0)
            r = rq[:].rearrange("p t h -> p (t h)")
            for w, a, b in ((P, 0, NTT * H), (B, NTT * H, (NTT + 1) * H)):
                S(nc.scalar.activation(r[0:w, a:b], bank[0:w, a:b], ACT.Ln, bias=epsc[0:w], scale=1.0 / (2 * DH)),
                  bank_read[0] if w == B else None)
                S(nc.scalar.activation(r[0:w, a:b], r[0:w, a:b], ACT.Exp, scale=-0.5))
            act.sem_inc(rq_ready, 1)

        def pe_query(pe):
            bank = pe_bank(pe, 0)

            def sums(i):
                for s in range(2):
                    pe.wait_ge(out_free[s], i + BASE["cq"][s])
                for tt in range(NTT + 1):
                    w = P if tt < NTT else B
                    for dh in range(2):
                        m = nc.tensor.matmul(bank[0:w, bass.ds(i + (tt * H - 1), 1)], sq2[:, dh, tt * P:tt * P + w], ones[:, 0:1],
                                             start=(dh == 0), stop=(dh == 1))
                m.then_inc(qsq_used, 1)
            pe_pair(pe, "cq", 0)
            pe_proj(pe, "cq", 1, sums)
            sums(H)
            pe.wait_ge(qsq_used, H)
            pe.sem_inc(bank_full[0], 1)

        def vec_query(dve):
            dve.wait_ge(rq_ready, 1)
            V(nc.vector.tensor_scalar(rq[:, 0:NTT], rq[:, 0:NTT], SCALE_C, None, ALU.mult))
            V(nc.vector.tensor_scalar(rq[0:B, NTT], rq[0:B, NTT], SCALE_C, None, ALU.mult))

        def xcol(j, c):
            return xc[:, 4 * (j % 2) + c:4 * (j % 2) + c + 1]

        def score_bank(i):
            return 2 + i % 2 if i < B + 2 else 2

        def pe_cross_score(pe, i):
            h, qt = divmod(i, NTT)
            if i == 0:
                pe.wait_ge(kn_ready, KT)
            bank = pe_bank(pe, score_bank(i))
            for dh in range(2):
                m = nc.tensor.matmul(bank[:, 0:NMEM], qT[:, 2 * h + dh, qt * P:(qt + 1) * P], mkT[:, 2 * h + dh, :],
                                     start=(dh == 0), stop=(dh == 1))
            m.then_inc(bank_full[score_bank(i)], 1)

        def pe_cross(pe, i):
            if 0 <= i - 1 < N_ATT:
                j = i - 1
                pe.wait_ge(xa_p, j + 1)
                bank = pe_bank(pe, 0)
                for mt in range(2):
                    m = nc.tensor.transpose(bank[:, mt * P:(mt + 1) * P], px[:, j % 2, mt * P:(mt + 1) * P], ident[:])
                m.then_inc(bank_full[0], 1)
            if i >= 2 and (i - 2) % NTT == NTT - 1:
                h = (i - 2) // NTT
                pe.wait_ge(xa_turned, i - 1)
                if h >= 2:
                    pe.wait_ge(xa_read, h - 1)
                for dh in range(2):
                    for mt in range(2):
                        c = (2 * h + dh) * P
                        m = nc.tensor.matmul(PJ[h % 2][:, dh, :], mv_t[:, mt, c:c + P], pT[:, mt, :], start=(mt == 0),
                                             stop=(mt == 1))
                m.then_inc(xa_done, 1)

        def act_cross(act, i):
            if i >= 2 and (i - 2) % NTT == NTT - 1:
                h = (i - 2) // NTT
                act.wait_ge(xa_done, h + 1)
                S(nc.scalar.copy(oT[:, 2 * h:2 * h + 2, 0:SEQ], PJ[h % 2]), xa_read)
            if 0 <= i - 1 < N_ATT:
                j = i - 1
                qt = j % NTT
                bank = rd_bank(act, 0)
                S(nc.scalar.copy(pT[:, :, qt * P:(qt + 1) * P], bank[:, 0:NMEM].rearrange("p (t q) -> p t q", t=2)), bank_read[0])
                act.sem_inc(xa_turned, 1)
            if i < N_ATT:
                act.wait_ge(xa_max, i + 1)
                S(nc.scalar.activation(px[:, i % 2], px[:, i % 2], ACT.Exp, bias=xcol(i, 1), accum_out=xcol(i, 2)), xa_exp)

        def vec_cross(dve, i):
            v = nc.vector
            if 0 <= i - 1 < N_ATT:
                j = i - 1
                dve.wait_ge(xa_exp, j + 1)
                V(v.reciprocal(xcol(j, 3), xcol(j, 2)))
                V(v.tensor_scalar(px[:, j % 2], px[:, j % 2], xcol(j, 3), None, ALU.mult), xa_p)
            if i < N_ATT:
                h, qt = divmod(i, NTT)
                bank = rd_bank(dve, score_bank(i))
                if i >= 2:
                    dve.wait_ge(xa_turned, i - 1)
                V(v.tensor_scalar(px[:, i % 2], bank[:, 0:NMEM], rq[:, qt, h:h + 1], None, ALU.mult), bank_read[score_bank(i)])
                V(v.tensor_reduce(xcol(i, 0), px[:, i % 2], AX, ALU.max))
                V(v.tensor_scalar(xcol(i, 1), xcol(i, 0), -1.0, None, ALU.mult), xa_max)

        def sp_cache(sp):
            stage_done(sp, "cv", w_used)
            sp.wait_ge(mk_ready, 1)
            for n in range(2 * B):
                if n >= 4:
                    sp.wait_ge(*((xs_scored, n - 3) if n - 4 < B else (xs_used, n - 4 - B + 1)))
                name = "cache_mem_k" if n < B else "cache_mem_v"
                sp.dma_start(ckv[n % 4][:], A[name][0, n % B].rearrange("(t p) h d -> p t (h d)", p=P)).then_inc(
                    ckv_full[n % 4], 16)

        def vec_sample_q(dve):
            v = nc.vector
            V(v.tensor_tensor(qs[:].rearrange("p (h a) b -> p h a b", a=2), qT[:, :, SEQ:T].rearrange("p (h a) b -> p h a b", a=2),
                              gains[:, G_CQ:G_CQ + 2].unsqueeze(1).unsqueeze(3).to_broadcast([P, H, 2, B]), ALU.mult), qs_ready)
            dve.wait_ge(qst_ready, 1)
            q = qs_tok[:].rearrange("b (h d) -> b h d", h=H)
            V(v.tensor_tensor(q, q, rq[0:B, NTT].unsqueeze(2).to_broadcast([B, H, 2 * DH]), ALU.mult), qsn_ready)

        def pe_sample_q(pe):
            pe.wait_ge(qs_ready, 1)
            for i in range(2):
                bank = pe_bank(pe, i)
                for k in range(4):
                    m = nc.tensor.transpose(bank[0:B, k * P:(k + 1) * P], qs[:, 4 * i + k, :], ident[:])
                m.then_inc(bank_full[i], 1)
            pe.wait_ge(qsn_ready, 1)

        def act_sample_q(act):
            for i in range(2):
                S(nc.scalar.copy(qs_tok[:, i * SEQ:(i + 1) * SEQ], rd_bank(act, i)[0:B, :]), bank_read[i])
            act.sem_inc(qst_ready, 1)

        def pe_sample_k(pe, b):
            for i in (1 - b % 2, b % 2):
                nc.tensor.matmul(pe_bank(pe, 2 + i)[:], rowsel[:, b, :], qs_tok[:, i * SEQ:(i + 1) * SEQ], start=True,
                                 stop=True).then_inc(bank_full[2 + i], 1)

        def vec_sample_k(dve, b):
            v = nc.vector
            if b == 0:
                dve.wait_ge(mem_stored, 32)
            dve.wait_ge(ckv_full[b % 4], 16 * (b // 4 + 1))
            for i in (1 - b % 2, b % 2):
                V(v.tensor_tensor(prod[:, :, i * SEQ:(i + 1) * SEQ], ckv[b % 4][:, :, i * SEQ:(i + 1) * SEQ],
                                  rd_bank(dve, 2 + i).unsqueeze(1).to_broadcast([P, 2, SEQ]), ALU.mult), bank_read[2 + i])
            dve.sem_inc(xs_scored, 1)
            V(v.tensor_reduce(xS[:, :, :, b], prod[:].rearrange("p t (h d) -> p t h d", h=H), AX, ALU.add),
              qs_ready if b == B - 1 else None)

        def pe_sample_soft(pe):
            pe.wait_ge(qs_ready, 2)
            bank = pe_bank(pe, 2)
            for t in range(2):
                m = nc.tensor.transpose(bank[0:HB, t * P:(t + 1) * P], xS[:, t].rearrange("p h b -> p (h b)"), ident[:])
            m.then_inc(bank_full[2], 1)

        def pe_sample_turn(pe):
            pe.wait_ge(xs_p, 1)
            bank = pe_bank(pe, 3)
            for t in range(2):
                m = nc.tensor.transpose(bank[:, t * HB:(t + 1) * HB], xp[:, t * P:(t + 1) * P], ident[0:HB, 0:HB])
            m.then_inc(bank_full[3], 1)

        def vec_sample_soft(dve):
            v = nc.vector
            V(v.tensor_copy(xp[:], rd_bank(dve, 2)[0:HB, 0:NMEM]), bank_read[2])
            V(v.tensor_reduce(xc[0:HB, 8:9], xp[:], AX, ALU.max))
            V(v.tensor_scalar(xc[0:HB, 9:10], xc[0:HB, 8:9], -1.0, None, ALU.mult), xs_max)
            dve.wait_ge(xs_exp, 1)
            V(v.reciprocal(xc[0:HB, 11:12], xc[0:HB, 10:11]))
            V(v.tensor_scalar(xp[:], xp[:], xc[0:HB, 11:12], None, ALU.mult), xs_p)

        def vec_sample_turn(dve):
            v = nc.vector
            V(v.memset(xSm[:], 0.0))
            w = rd_bank(dve, 3)[:, 0:2 * HB].rearrange("p (t h b) -> p t h b", t=2, h=H)
            for b in range(B):
                V(v.tensor_copy(xSm[:, b].rearrange("p t (h b) -> p t h b", h=H)[:, :, :, b], w[:, :, :, b]),
                  bank_read[3] if b == B - 1 else None)
            dve.sem_inc(xsT_ready, 1)

        def act_sample_soft(act):
            act.wait_ge(xs_max, 1)
            S(nc.scalar.activation(xp[:], xp[:], ACT.Exp, bias=xc[0:HB, 9:10], accum_out=xc[0:HB, 10:11]), xs_exp)

        def pe_sample_v(pe, b):
            if b == 0:
                pe.wait_ge(xsT_ready, 1)
                pe_bank(pe, 1)
                pe_bank(pe, 3)
            pe.wait_ge(ckv_full[b % 4], 16 * (B // 4 + b // 4 + 1))
            for half, bank in enumerate((TB, XB)):
                for t in range(2):
                    m = nc.tensor.matmul(bank[0:HB, :], xSm[:, b, t, :], ckv[b % 4][:, t, half * SEQ:(half + 1) * SEQ],
                                         start=(b == 0 and t == 0), stop=(b == B - 1 and t == 1))
            m.then_inc(xs_used, 1)

        def act_sample_v(act):
            act.wait_ge(xs_used, B)
            S(nc.scalar.copy(xO[:, 0], TB[0:HB, :]), bank_read[1])
            act.sem_inc(xo_ready, 1)

        def pe_sample_out(pe):
            pe.wait_ge(xo_ready, 2)
            bank = pe_bank(pe, 2)
            for f in range(KT):
                m = nc.tensor.transpose(bank[:, f * HB:(f + 1) * HB], xO[:, f // 4, (f % 4) * P:(f % 4 + 1) * P],
                                        ident[0:HB, 0:HB])
            m.then_inc(bank_full[2], 1)

        def vec_sample_out(dve):
            dve.wait_ge(xs_used, B)
            V(nc.vector.tensor_copy(xO[:, 1], XB[0:HB, :]), bank_read[3])
            dve.sem_inc(xo_ready, 1)
            o = rd_bank(dve, 2)[:, 0:KT * HB].rearrange("p (f r) -> p f r", f=KT)
            for h in range(H):
                V(nc.vector.tensor_copy(oT[:, 2 * h:2 * h + 2, SEQ:T], o[:, 2 * h:2 * h + 2, h * B:(h + 1) * B]),
                  bank_read[2] if h == H - 1 else None)
            dve.sem_inc(o_ready, 1)

        def act_split_o(act):
            act.wait_ge(o_ready, 1)
            for k in range(KT):
                S(nc.scalar.copy(ahi[:, k], oT[:, k]), y_hi)

        def vec_split_o(dve):
            for k in range(KT):
                dve.wait_ge(y_hi, KT + k + 1)
                V(nc.vector.tensor_tensor(alo[:, k], oT[:, k], ahi[:, k].bitcast(F32), ALU.subtract), y_lo)

        def pe_hist(pe):
            pe.wait_ge(hist_in, 16)
            for i in range(2):
                bank = pe_bank(pe, 2 + i)
                for f in range(NFT):
                    m = nc.tensor.transpose(bank[:, f * 2 * B:(f + 1) * 2 * B],
                                            hist_rows[:, (i * NFT + f) * P:(i * NFT + f + 1) * P], ident[0:2 * B, 0:2 * B])
                m.then_inc(bank_full[2 + i], 1)

        def vec_hist(dve):
            for i in range(2):
                V(nc.vector.tensor_copy(hist[:, i * NFT:(i + 1) * NFT].rearrange("p f b j -> p (f b j)"),
                                        rd_bank(dve, 2 + i)[:, 0:NFT * 2 * B]), bank_read[2 + i])
            stage_done(dve, "co", w_used)
            V(nc.vector.memset(ub[:, :, 0:2], 0.0), h_zero)

        UP_STEPS = 13

        def act_up(act):
            base = BASE["up"]
            nc.scalar.preload_act_table_set("gelu_apprx_tanh_and_others")
            with act.Fori(0, NFT) as i:
                for s in range(2):
                    act_split(act, s, i + (base[s] + 1))
                    act.wait_ge(u_free, i * 2 + s)
                    nc.scalar.copy(ub[:, s, 2:2 + T].rearrange("p (a b) -> p a b", a=2), PJ[s][:, :, 0:HALF])
                    act.wait_ge(*((gelu_done, i) if s == 0 else (g_lo, i)))
                    f = i + (1 - s) * NFT
                    nc.scalar.activation(cc[:, s].rearrange("p (a b) -> p a b", a=2), PJ[s][:, :, 0:HALF], ACT.Identity,
                                         bias=gains[:, bass.ds(f + G_CB, 1)], scale=cw[:, 2, bass.ds(f, 1)]).then_inc(
                        out_free[s], 1)
                    if s == 0:
                        act.wait_ge(c_ready, i * 2 + 1)
                        act.wait_ge(g_lo, i)
                        nc.scalar.activation(gl[:], cc[:, 0], ACT.Gelu_apprx_tanh).then_inc(gelu_done, 1)

        def vec_up(dve):
            v = nc.vector
            base = BASE["up"]
            with dve.Fori(0, NFT) as i:
                n = [0]

                def step(*instructions):
                    for ins in instructions:
                        ins.then_inc(up_step, 1)
                    n[0] += len(instructions)
                    dve.wait_ge(up_step, i * UP_STEPS + n[0])

                for s in range(2):
                    f = i + (1 - s) * NFT
                    c = cc[:, s]
                    hj = [hist[:, bass.ds(f, 1), :, j].rearrange("p o b -> p (o b)") for j in range(2)]
                    col = [cw[:, j, bass.ds(f, 1)] for j in range(2)]
                    dve.wait_ge(out_free[s], i + (base[s] + 1))
                    step(*(v.scalar_tensor_tensor(y, x, col[1], y, ALU.mult, ALU.add)
                           for y, x in ((c[:, 0:SEQ], ub[:, s, 1:1 + SEQ]), (c[:, SEQ:T], hj[1]))))
                    step(*[v.scalar_tensor_tensor(y, x, col[0], y, ALU.mult, ALU.add)
                           for y, x in ((c[:, 0:SEQ], ub[:, s, 0:SEQ]), (c[:, SEQ:T], hj[0]))],
                         v.tensor_copy(ulast[:, bass.ds(f, 1), :], ub[:, s, SEQ:2 + T].unsqueeze(1)))
                    dve.sem_inc(u_free, 1)
                    dve.sem_inc(c_ready, 1)
                dve.wait_ge(gelu_done, i + 1)
                step(v.tensor_tensor(gl[:], gl[:], cc[:, 1], ALU.mult))
                step(v.tensor_copy(gHi[:, bass.ds(i, 1), :], gl[:].unsqueeze(1)))
                step(v.tensor_tensor(gLo[:, bass.ds(i, 1), :], gl[:].unsqueeze(1), gHi[:, bass.ds(i, 1), :].bitcast(F32),
                                     ALU.subtract))
                dve.sem_inc(g_lo, 1)

        def pe_last(pe):
            for i in range(2 * NFT // 4):
                bank = pe_bank(pe, i % 2)
                for f in range(4):
                    m = nc.tensor.transpose(bank[0:2 + B, f * P:(f + 1) * P], ulast[:, 4 * i + f, :], ident[:])
                m.then_inc(bank_full[i % 2], 1)

        def act_last(act):
            stage_done(act, "up", w_used)
            for i in range(2 * NFT // 4):
                S(nc.scalar.copy(conv_rows[:, i * SEQ:(i + 1) * SEQ], rd_bank(act, i % 2)[0:2 + B, :]), bank_read[i % 2])
            act.dma_start(O["p_conv"][0, 0], conv_rows[0:2]).then_inc(out_stores, 16)
            act.dma_start(O["s_conv"][0, :, 1], conv_rows[2:2 + B]).then_inc(out_stores, 16)

        THIRDS = ((0, 8), (8, 7), (15, 7))

        def sp_down(sp):
            w = A["w_down"][0].rearrange("(k p) c -> p k c", p=P)
            base = BASE["down"]
            with sp.Fori(0, KT // 2) as i:
                for j in range(6):
                    s, (k0, kn) = j % 2, THIRDS[j % 3]
                    sp.wait_ge(split_full[s], i * 3 + (base[s] + j // 2))
                    sp.dma_start(raw[:, s, 0:kn], w[:, k0:k0 + kn, bass.ds(i * (2 * P) + (j // 3) * P, P)]).then_inc(raw_full[s], 16)

        def act_down(act, start, end):
            base = BASE["down"]
            with act.Fori(start, end) as i:
                for s in range(2):
                    act_split(act, s, i + (base[s] + 1))

        def pe_down_pair(pe, i):
            base = BASE["down"]
            for j in range(6):
                s, (k0, kn), o = j % 2, THIRDS[j % 3], j // 3
                pe.wait_ge(split_full[s], i * 3 + (base[s] + j // 2 + 1))
                pe.wait_ge(g_lo, k0 + kn)
                if j % 3 == 0:
                    pe.wait_ge(out_free[o], i + base[o])
                pe_product(s, PJ[o], P, kn, gHi, gLo, first=(j % 3 == 0), last=(j % 3 == 2), k0=k0).then_inc(w_used[s], 1)

        def vec_down(dve):
            base = BASE["down"]
            with dve.Fori(0, KT // 2) as i:
                for o in range(2):
                    dve.wait_ge(w_used[o], i * 3 + (base[o] + 2 + o))
                    x = xT[:, bass.ds(i * 2 + o, 1), :].rearrange("p a (c b) -> p (a c) b", c=2)
                    nc.vector.tensor_tensor(x, x, PJ[o][:, :, 0:HALF], ALU.add).then_inc(out_free[o], 1)

        def pe_out(pe):
            for o in range(2):
                pe.wait_ge(out_free[o], BASE["down"][o] + KT // 2)
            for k in range(KT):
                bank = pe_bank(pe, k % 2)
                for tt in range(NTT):
                    m = nc.tensor.transpose(bank[:, tt * P:(tt + 1) * P], xT[:, k, tt * P:(tt + 1) * P], ident[:])
                m.then_inc(bank_full[k % 2], 1)
            for i in range(2):
                bank = pe_bank(pe, 2 + i)
                for k in range(4):
                    m = nc.tensor.transpose(bank[0:B, k * P:(k + 1) * P], xT[:, 4 * i + k, SEQ:T], ident[:])
                m.then_inc(bank_full[2 + i], 1)

        def act_out(act):
            act.wait_ge(g_lo, NFT)
            for k in range(KT):
                S(nc.scalar.copy(y_tok[:, :, k * P:(k + 1) * P], rd_bank(act, k % 2)[:].rearrange("p (t f) -> p t f", t=NTT)),
                  bank_read[k % 2])
                if k % 4 == 3:
                    act.dma_start(O["y_prompt"][0].rearrange("(t p) d -> p t d", p=P)[:, :, (k - 3) * P:(k + 1) * P],
                                  y_tok[:, :, (k - 3) * P:(k + 1) * P]).then_inc(out_stores, 16)
            act.wait_ge(y_ready, 1)
            act.dma_start(O["y_sample"][:, 0], ys_tok[:]).then_inc(out_stores, 16)

        def vec_out(dve):
            for i in range(2):
                V(nc.vector.tensor_copy(ys_tok[:, i * SEQ:(i + 1) * SEQ], rd_bank(dve, 2 + i)[0:B, :]), bank_read[2 + i])
            dve.sem_inc(y_ready, 1)

        def sync_reload(sp):
            sp.wait_ge(ym_ready, H)
            sp.wait_ge(spT_ready, 1)
            sp.dma_start(mem_in[:], A["mem_prompt"][0].rearrange("(t p) d -> p t d", p=P)).then_inc(xm_in, 16)
            for t in range(NTT):
                sp.dma_start(x_re[t][:], A["x_prompt"][0, t * P:(t + 1) * P, :]).then_inc(xm_in, 16)
            sp.dma_start(xs_re[:], A["x_sample"][:, 0, :]).then_inc(xm_in, 16)

        def sync_tail(sp):
            w = A["w_out"][0].rearrange("(k p) c -> p k c", p=P)
            for s in range(2):
                sp.wait_ge(split_full[s], BASE["out"][s])
                sp.dma_start(raw[:, s], w[:, :, s * P:(s + 1) * P]).then_inc(raw_full[s], 16)
            sync_mls(sp)
            sp_stream(sp, "out", 1)
            for stage in ("ck", "cv", "cq"):
                sp_stream(sp, stage)
            for s in range(2):
                sp.wait_ge(split_full[s], BASE["co"][s])
                sp.dma_start(raw[:, s], A["w_co"][0].rearrange("(k p) c -> p k c", p=P)[:, :, s * P:(s + 1) * P]).then_inc(
                    raw_full[s], 16)
            sp_cache(sp)
            sp.wait_ge(xs_used, B)
            sp.wait_ge(mem_stored, 32)
            sp.dma_start(hist_rows[:], A["state_conv"][0].rearrange("b j c -> (b j) c")).then_inc(hist_in, 16)
            sp.dma_start(O["s_conv"][0, :, 0], A["state_conv"][0, :, 1]).then_inc(out_stores, 16)
            sp_stream(sp, "co", 1)
            sp_stream(sp, "up")
            sp_down(sp)

        def pool_tail(pool):
            pool_split(pool, 0)
            pool_satt(pool)
            with pool.Fori(1, N_PAIRS) as i:
                pool_split(pool, i)

        def act_tail(act):
            for s in range(2):
                act_split(act, s, BASE["out"][s])
            act_mixers(act)
            act.wait_ge(stores, 16 * 8)
            act.wait_ge(sv_stored, 16)
            for i in range(2):
                act.wait_ge(rt_stored[i], 32)
                act.wait_ge(c_stored[i], 16 * (H // 2))
                act.wait_ge(sc_stored[i], 16 * (B // 2))
            act.sem_inc(mix_stored, 1)
            for k in range(KT):
                act.wait_ge(memT_ready, k + 1)
                act.wait_ge(sq_used, KT + max(k - 1, 0))
                nc.scalar.activation(sq2[:, k % 2, 0:NMEM], memT[:, k], ACT.Square).then_inc(sq_ready, 1)
            act_rstd(act, 1, rstd2, NMEM, D)
            for k in range(KT):
                act.wait_ge(hs_ready, KT + k + 1)
                nc.scalar.copy(hmhi[:, k], hs2[:, k % 2, 0:NMEM]).then_inc(nhi_ready, 1)
            act_proj(act, "out")
            stage_done(act, "out", out_free)
            act_norm(act, 2, xT, T, ahi)
            act_mem_proj(act, "ck", mk_t)
            act_mem_proj(act, "cv", mv_t)
            act_mem_keys(act)
            act.wait_ge(mk_ready, 1)
            stage_done(act, "cv", out_free)
            for name, t in (("p_mem_k", mk_t), ("p_mem_v", mv_t)):
                act.dma_start(O[name][0, 0].rearrange("(t p) h d -> p t (h d)", p=P), t[:]).then_inc(mem_stored, 16)
            act_query(act)
            act_sample_q(act)
            for i in range(N_ATT + 2):
                act_cross(act, i)
                if i == B:
                    act_sample_soft(act)
            act_sample_v(act)
            act_split_o(act)
            act_proj(act, "co")
            stage_done(act, "co", out_free)
            act_norm(act, 3, xT, T, ahi)
            act.wait_ge(h_zero, 1)
            act_up(act)
            act_down(act, 0, 3)
            act_last(act)
            act_down(act, 3, 11)
            act_out(act)
            act.wait_ge(mem_stored, 32)
            act.wait_ge(out_stores, 16 * 6)

        def vec_tail(dve):
            vec_mixers(dve)
            vec_turn_in(dve)
            vec_norm(dve, 1, memT, rstd2, G_MEM, hs2, NMEM, (hmhi, hmlo))
            vec_residual(dve, "out")
            vec_norm(dve, 2, xT, rstd2, G_CROSS, hs2, T)
            vec_mem_keys(dve)
            vec_query(dve)
            vec_sample_q(dve)
            for i in range(N_ATT + 2):
                vec_cross(dve, i)
                if i < B:
                    vec_sample_k(dve, i)
                elif i == B:
                    vec_sample_soft(dve)
                elif i == B + 1:
                    vec_sample_turn(dve)
            vec_sample_out(dve)
            vec_split_o(dve)
            vec_residual(dve, "co")
            vec_hist(dve)
            vec_norm(dve, 3, xT, rstd2, G_FFN, hs2, T)
            vec_up(dve)
            vec_down(dve)
            vec_out(dve)

        def pe_tail(pe):
            pe_mixers(pe)
            pe_turn_in(pe)
            pe.wait_ge(y_lo, KT)
            pe_proj(pe, "out")
            for k in range(KT):
                pe_sumsq(pe, 2, k, sq2, T)
            pe.wait_ge(nlo_ready, 2 * KT)
            pe_mem_proj(pe, "ck")
            pe_mem_proj(pe, "cv")
            pe_mem_keys(pe)
            pe.wait_ge(nlo_ready, 3 * KT)
            pe_query(pe)
            pe_sample_q(pe)
            for i in range(N_ATT + 2):
                if i < N_ATT:
                    pe_cross_score(pe, i)
                if i < B:
                    pe_sample_k(pe, i)
                elif i == B:
                    pe_sample_soft(pe)
                elif i == B + 1:
                    pe_sample_turn(pe)
                else:
                    pe_sample_v(pe, i - B - 2)
                pe_cross(pe, i)
            pe_sample_out(pe)
            pe.wait_ge(y_lo, 2 * KT)
            pe_proj(pe, "co")
            pe_hist(pe)
            for k in range(KT):
                pe_sumsq(pe, 3, k, sq2, T)
            pe.wait_ge(nlo_ready, 4 * KT)
            pe_proj(pe, "up")
            pe_down_pair(pe, 0)
            pe_last(pe)
            with pe.Fori(1, KT // 2) as i:
                pe_down_pair(pe, i)
            pe_out(pe)
        block = ctx.enter_context(nc.Block())

        @block.sync
        def _(sp):
            for t in range(NTT):
                sp.dma_start(x_in[:, t, :], A["x_prompt"][0, t * P:(t + 1) * P, :]).then_inc(x_in_s, 16)
            sp.dma_start(xs_in[:], A["x_sample"][:, 0, :]).then_inc(x_in_s, 16)
            w_in = A["w_in"][0].rearrange("(k p) c -> p k c", p=P)
            for n, (name, col) in enumerate(IN_TILES):
                s, u = uses(n)
                if u:
                    sp.wait_ge(split_full[s], u)
                if name == "ikw":
                    w = C_IQ + H * D_IDX
                    sp.dma_start(raw[:, s, :, 0:D_IDX + H], w_in[:, :, w:w + D_IDX + H]).then_inc(gates_in, 16)
                    sp.dma_start(raw[:, s, :, D_IDX + H:D_IDX + 3 * H], w_in[:, :, C_G:C_G + 2 * H]).then_inc(gates_in, 16)
                    sp.wait_ge(gates_in, 32)
                    sp.sem_inc(raw_full[s], 16)
                else:
                    sp.dma_start(raw[:, s], w_in[:, :, col:col + P]).then_inc(raw_full[s], 16)
            sync_tail(sp)

        @block.gpsimd
        def _(pool):
            g = nc.gpsimd
            made = [0]

            def made_by(ins):
                made[0] += 1
                ins.then_inc(consts_made, 1)
                pool.wait_ge(consts_made, made[0])

            for t, v in ((ident, 0.0), (ones, 1.0), (tri, 1.0), (negm, 0.0), (posm, 0.0), (rowsel, 1.0), (own, 1.0),
                         (gt, 0.0), (epsc, EPS)):
                made_by(g.memset(t[:], v))
            made_by(g.affine_select(out=ident[:], in_=ident[:], compare_op=ALU.not_equal, fill=1.0, base=0,
                                    pattern=[[-1, P]], channel_multiplier=1))
            made_by(g.affine_select(out=tri[:], in_=tri[:], compare_op=ALU.is_ge, fill=0.0, base=0,
                                    pattern=[[1, P]], channel_multiplier=-1))
            made_by(g.affine_select(out=negm[:], in_=negm[:], compare_op=ALU.is_ge, fill=NEG, base=0,
                                    pattern=[[-1, P]], channel_multiplier=1))
            made_by(g.affine_select(out=posm[:], in_=posm[:], compare_op=ALU.is_ge, fill=-NEG, base=0,
                                    pattern=[[1, P]], channel_multiplier=-1))
            made_by(g.affine_select(out=rowsel[:], in_=rowsel[:], compare_op=ALU.is_equal, fill=0.0, base=0,
                                    pattern=[[-1, B], [0, P]], channel_multiplier=1))
            made_by(g.affine_select(out=own[:], in_=own[:], compare_op=ALU.is_equal, fill=0.0, base=0,
                                    pattern=[[0, H], [-1, B]], channel_multiplier=1))
            for n in range(N_IN):
                s, u = uses(n)
                w = D_IDX + 3 * H if n == 2 else P
                pool.wait_ge(hi_full[s], u + 1)
                g.tensor_tensor(wlo[:, s, :, 0:w], raw[:, s, :, 0:w], whi[:, s, :, 0:w].bitcast(F32),
                                ALU.subtract).then_inc(split_full[s], 1)
                pool_hooks(pool, n)
            pool_tail(pool)

        @block.scalar
        def _(act):
            a = nc.scalar
            a.preload_act_table_set("natural_log_exp_and_others")
            for dst, src in (
                    (rope_m[:], A["rope_main"][0:SEQ].rearrange("(t p) a b -> p t a b", p=P)),
                    (rope_ms[:], A["rope_main"][SEQ:T]),
                    (rope_i[:], A["rope_index"][0:SEQ].rearrange("(t p) a b -> p t a b", p=P)),
                    (rope_is[:], A["rope_index"][SEQ:T]),
                    (vecs[G_MIX:G_MIX + 8], A["norm_mix"].rearrange("o (a b) -> (o a) b", b=P)),
                    (vecs[G_CROSS:G_CROSS + 8], A["norm_cross"].rearrange("o (a b) -> (o a) b", b=P)),
                    (vecs[G_MEM:G_MEM + 8], A["norm_mem"].rearrange("o (a b) -> (o a) b", b=P)),
                    (vecs[G_FFN:G_FFN + 8], A["norm_ffn"].rearrange("o (a b) -> (o a) b", b=P)),
                    (vecs[G_CQ:G_CQ + 2], A["cq_norm"].rearrange("o (a b) -> (o a) b", b=P)),
                    (vecs[G_ML:G_ML + 4], A["mlstm_norm"].rearrange("o (a b) -> (o a) b", b=P)),
                    (vecs[G_CB:G_CB + 44], A["conv_b"].rearrange("o (a b) -> (o a) b", b=P)),
                    (cwrows[:], A["conv_w"][0].rearrange("j (a b) -> a j b", b=P)),
                    (qg[:], A["q_norm"].to_broadcast([P, DH])),
                    (kg[:], A["k_norm"].to_broadcast([P, DH])),
                    (ckg[:], A["ck_norm"].to_broadcast([P, 2 * DH])),
                    (ptw[:], A["page_table"].rearrange("b (g o) -> (b g) o", o=1)),
                    (ptr[:], A["page_table"]),
                    (bif[:], A["b_if"].to_broadcast([P, 2 * H]))):
                act.dma_start(dst, src).then_inc(consts_in, 16)

            def split_hi(n):
                s, u = uses(n)
                w = D_IDX + 3 * H if n == 2 else P
                act.wait_ge(raw_full[s], 16 * (u + 1))
                if u:
                    act.wait_ge(w_used[s], u)
                a.copy(whi[:, s, :, 0:w], raw[:, s, :, 0:w]).then_inc(hi_full[s], 1)

            bank = rd_bank(act, 0)
            S(a.copy(gains[:], bank[:, 0:82]), vec_ready)
            S(a.copy(cw[:], bank[:, 128:260].rearrange("p (j f) -> p j f", j=3)), bank_read[0])
            for k in range(KT):
                act.wait_ge(xT_turned, k + 1)
                a.copy(xT0[:, k, 0:SEQ], PJ[k % 2][:, 0, :])
                a.copy(xT0[:, k, SEQ:T], PJ[k % 2][:, 1, 0:B]).then_inc(xT_ready, 1)
                act.wait_ge(xT_ready, k + 1)
                if k >= 2:
                    act.wait_ge(sq_used, k - 1)
                a.activation(sq[:, k % 2], xT0[:, k], ACT.Square).then_inc(sq_ready, 1)
                if k == 6:
                    split_hi(0)
            split_hi(1)
            act_rstd(act, 0, rstd, T, D)
            for k in range(KT):
                act.wait_ge(hs_ready, k + 1)
                a.copy(ahi[:, k], hs[:, k % 2]).then_inc(nhi_ready, 1)
            for n, (name, _) in enumerate(IN_TILES):
                s, u = uses(n)
                for q in range(3):
                    act_hooks(act, n, q)
                act.wait_ge(w_used[s], u + 1)
                dst, rows = (z_i[:, n], P) if n < 3 else (z_a[:, n - 3], P) if n < 15 else (z_m[:, n - 15], P)
                if n == 2:
                    dst, rows = z_i[0:D_IDX + 3 * H, 2], D_IDX + 3 * H
                if n + 2 < N_IN:
                    split_hi(n + 2)
                a.copy(dst.rearrange("p (a b) -> p a b", a=2), PJ[s][0:rows, :, 0:HALF]).then_inc(out_free[s], 1)
                act_hooks(act, n, 3)
            act_tail(act)

        @block.vector
        def _(dve):
            v = nc.vector
            dve.wait_ge(consts_in, 16 * 18)
            ptf = tiny[0:B * NPG, 104:109]
            V(v.tensor_copy(ptf[:, 4:5], ptw[:]))
            for c in range(4):
                V(v.tensor_scalar(ptf[:, c:c + 1], ptf[:, 4:5], 4.0, float(c), ALU.mult, ALU.add))
            V(v.tensor_copy(pidx[:], ptf[:, 0:4]), pidx_ready)
            dve.wait_ge(vec_ready, 1)
            vec_norm(dve, 0, xT0, rstd, G_MIX, hs, T)
            for n in range(N_IN):
                for q in range(4):
                    vec_hooks(dve, n, q)
            vec_tail(dve)

        @block.tensor
        def _(pe):
            t = nc.tensor
            pe.wait_ge(consts_made, 15)
            pe.wait_ge(consts_in, 16 * 18)
            t.transpose(pe_bank(pe, 0)[:, 0:82], vecs[:], ident[0:82, 0:82])
            bank = TA
            for j in range(3):
                m = t.transpose(bank[:, 128 + j * 44:128 + (j + 1) * 44], cwrows[:, j, :], ident[0:44, 0:44])
            m.then_inc(bank_full[0], 1)
            pe.wait_ge(x_in_s, 16 * (NTT + 1))
            for k in range(KT):
                if k >= 2:
                    pe.wait_ge(xT_ready, k - 1)
                for tt in range(NTT):
                    t.transpose(PJ[k % 2][:, 0, tt * P:(tt + 1) * P], x_in[:, tt, k * P:(k + 1) * P], ident[:])
                t.transpose(PJ[k % 2][:, 1, 0:B], xs_in[:, k * P:(k + 1) * P], ident[0:B, 0:B]).then_inc(xT_turned, 1)
                if k >= 1:
                    pe_sumsq(pe, 0, k - 1, sq, T)
            pe_sumsq(pe, 0, KT - 1, sq, T)
            pe.wait_ge(nlo_ready, KT)
            for n in range(N_IN):
                s, u = uses(n)
                m = P if n != 2 else D_IDX + 3 * H
                pe.wait_ge(split_full[s], u + 1)
                if u:
                    pe.wait_ge(out_free[s], u)
                for q in range(4):
                    ins = pe_product(s, PJ[s], m, KT, ahi, alo, ks=range(2 * q, 2 * q + 2))
                    if q == 3:
                        ins.then_inc(w_used[s], 1)
                    pe_hooks(pe, n, q)
            pe_tail(pe)


_OUT_SHAPES = [(1, SEQ, D), (B, 1, D), (1, 1, SEQ, H, DH), (1, 1, SEQ, H, DH), (1, 1, SEQ, D_IDX),
               (1, 1, H, DH, DH), (1, 1, H, DH), (1, 1, H), (1, 1, NMEM, H, 2 * DH), (1, 1, NMEM, H, 2 * DH),
               (1, 1, 2, 2 * DFF), (1, B, 1, H, DH), (1, B, 1, H, DH), (1, B, 1, D_IDX),
               (1, B, H, DH, DH), (1, B, H, DH), (1, B, H), (1, B, 2, 2 * DFF)]
_OUT_NAMES = ["y_prompt", "y_sample", "p_k", "p_v", "p_idx_k", "p_c", "p_n", "p_m", "p_mem_k", "p_mem_v", "p_conv",
              "s_k", "s_v", "s_idx_k", "s_c", "s_n", "s_m", "s_conv"]


def kernel(**inputs):
    import concourse.bacc as bacc
    from concourse.bass_utils import run_bass_kernel_spmd

    nc = bacc.Bacc("TRN2", target_bir_lowering=False, num_devices=1)
    arrays, A, O = {}, {}, {}
    rope_main, rope_index = rope_tables()
    for name, value in list(inputs.items()) + [("rope_main", rope_main), ("rope_index", rope_index)]:
        value = np.ascontiguousarray(value)
        arrays[f"in_{name}"] = value
        A[name] = nc.dram_tensor(f"in_{name}", value.shape, mybir.dt.from_np(value.dtype), kind="ExternalInput").ap()
    for name, shape in zip(_OUT_NAMES, _OUT_SHAPES):
        O[name] = nc.dram_tensor(f"out_{name}", shape, F32, kind="ExternalOutput").ap()
    build(nc, A, O)
    r = run_bass_kernel_spmd(nc, [arrays], core_ids=[0])
    return tuple(r.results[0][f"out_{name}"] for name in _OUT_NAMES)
```
